# Optimizing a Trainium2 kernel written in Bass

```python
import jax, jax.numpy as jnp
from jax import lax
import numpy as np

D_MODEL = 1024
BATCH = 1
SEQ = 512
DEPTH = 2
DEC_BATCH = 1
DEC_SEQ = 32
PAST_LEN = 128

CHUNK = 64
N_EVEN = (DEPTH + 1) // 2
N_ODD = DEPTH // 2
ALPHA = (2 * DEPTH) ** 0.25
BETA = (8 * DEPTH) ** -0.25
LN_EPS = 1e-5
D_MIX = D_MODEL

GLA_HEADS = 4
GLA_DV = D_MIX // 2 // GLA_HEADS
GLA_DK = GLA_DV // 2
GLA_GATE_RANK = 16
GLA_GATE_TAU = 16.0
POOL_GROUPS = 4
POOL_WIDTH = D_MIX // 2
POOL_CH = POOL_WIDTH // POOL_GROUPS
POOL_WINDOWS = (2, 4, 8, 16)
POOL_HIST = 15
D_IN_EVEN = 2 * GLA_HEADS * GLA_DK + 2 * GLA_HEADS * GLA_DV + GLA_GATE_RANK + POOL_WIDTH

MLA_HEADS = 8
MLA_NOPE = 64
MLA_ROPE = 32
MLA_V = 64
MLA_Q_RANK = 256
MLA_KV_RANK = 128
ROPE_THETA = 10000.0
ATTN_Q_BLOCK = 128
MLA_SCALE = (MLA_NOPE + MLA_ROPE) ** -0.5
GMLP_GROUPS = 4
GMLP_WIDTH = D_MIX - MLA_HEADS * MLA_V
GMLP_CH = GMLP_WIDTH // GMLP_GROUPS
GMLP_CHUNK = 128
D_IN_ODD = MLA_Q_RANK + MLA_KV_RANK + MLA_ROPE + 2 * GMLP_WIDTH

N_GROUPS = 4
EXPERTS_PER_GROUP = 8
N_EXPERTS = N_GROUPS * EXPERTS_PER_GROUP
TOP_K = 2
D_EXPERT = 256
MOE_BLOCK = 256

kernel_name = 'hybrid_gla_pool_mla_gmlp_hmoe_stream_step'

def layernorm(x, g, b):
    xf = x.astype(jnp.float32)
    mu = jnp.mean(xf, -1, keepdims=True)
    var = jnp.mean(jnp.square(xf - mu), -1, keepdims=True)
    return ((xf - mu) * lax.rsqrt(var + LN_EPS) * g + b).astype(x.dtype)

def rmsnorm(x, g):
    xf = x.astype(jnp.float32)
    return (xf * lax.rsqrt(jnp.mean(xf * xf, -1, keepdims=True) + LN_EPS) * g).astype(x.dtype)

def split_cols(x, widths):
    out, start = [], 0
    for w in widths:
        out.append(x[..., start:start + w])
        start += w
    return out

def rope(x, pos):
    half = MLA_ROPE // 2
    inv = ROPE_THETA ** (-jnp.arange(half, dtype=jnp.float32) * 2.0 / MLA_ROPE)
    ang = pos.astype(jnp.float32)[:, None] * inv[None, :]
    shape = (1, pos.shape[0]) + (1,) * (x.ndim - 3) + (half,)
    cos, sin = jnp.cos(ang).reshape(shape), jnp.sin(ang).reshape(shape)
    xf = x.astype(jnp.float32)
    x1, x2 = xf[..., :half], xf[..., half:]
    return jnp.concatenate([x1 * cos - x2 * sin, x1 * sin + x2 * cos], -1).astype(x.dtype)

def gla_recurrence(q, k, v, log_a, s0):
    B, L, H, _ = q.shape
    DV = v.shape[-1]
    cl = min(L, CHUNK)
    n = L // cl

    def to_blocks(a):
        return a.astype(jnp.float32).reshape(B, n, cl, H, a.shape[-1]).transpose(1, 0, 3, 2, 4)

    incl = jnp.tril(jnp.ones((cl, cl), bool))[None, None, :, :, None]

    def step(S, inp):
        qc, kc, vc, ac = inp
        b = jnp.cumsum(ac, axis=2)
        diff = b[:, :, :, None, :] - b[:, :, None, :, :]
        decay = jnp.exp(jnp.where(incl, diff, -jnp.inf))
        scores = jnp.einsum('bhijd,bhjd->bhij', qc[:, :, :, None, :] * decay, kc)
        o = jnp.einsum('bhij,bhje->bhie', scores, vc) + jnp.einsum('bhid,bhde->bhie', qc * jnp.exp(b), S)
        b_end = b[:, :, -1:, :]
        S = jnp.exp(b_end[:, :, 0, :])[..., None] * S + jnp.einsum('bhjd,bhje->bhde', kc * jnp.exp(b_end - b), vc)
        return S, o

    S, o = lax.scan(step, s0.astype(jnp.float32), (to_blocks(q), to_blocks(k), to_blocks(v), to_blocks(log_a)))
    return o.transpose(1, 0, 3, 2, 4).reshape(B, L, H, DV), S

def pool_mix(xp, hist, pos0, pool_w, pool_scale):
    B, L, C = xp.shape
    ext = jnp.concatenate([hist.astype(xp.dtype), xp], axis=1)
    cs = jnp.concatenate([jnp.zeros((B, 1, C), jnp.float32), jnp.cumsum(ext.astype(jnp.float32), axis=1)], axis=1)
    pos = pos0 + jnp.arange(L)
    means = []
    for g, w in enumerate(POOL_WINDOWS):
        sl = slice(g * POOL_CH, (g + 1) * POOL_CH)
        hi = cs[:, POOL_HIST + 1:POOL_HIST + 1 + L, sl]
        lo = cs[:, POOL_HIST + 1 - w:POOL_HIST + 1 - w + L, sl]
        cnt = jnp.minimum(pos + 1, w).astype(jnp.float32)[None, :, None]
        means.append((hi - lo) / cnt)
    mix = (jnp.concatenate(means, -1) - xp.astype(jnp.float32)).reshape(B, L, POOL_GROUPS, POOL_CH)
    out = jnp.einsum('blgc,gcd->blgd', mix, pool_w.astype(jnp.float32)).reshape(B, L, C) * pool_scale
    return out.astype(xp.dtype), ext[:, -POOL_HIST:]

def even_mixer(h, s_gla, pool_hist, pos0, w_in, w_gate_up, b_gate, gla_norm_g, pool_w, pool_scale, w_out):
    B, L, _ = h.shape
    q, k, v, r, g_lr, xp = split_cols(h @ w_in, (GLA_HEADS * GLA_DK, GLA_HEADS * GLA_DK, GLA_HEADS * GLA_DV,
                                                 GLA_HEADS * GLA_DV, GLA_GATE_RANK, POOL_WIDTH))
    q = q.reshape(B, L, GLA_HEADS, GLA_DK) * GLA_DK ** -0.5
    k = k.reshape(B, L, GLA_HEADS, GLA_DK)
    v = v.reshape(B, L, GLA_HEADS, GLA_DV)
    log_a = jax.nn.log_sigmoid((g_lr @ w_gate_up + b_gate).astype(jnp.float32)) / GLA_GATE_TAU
    log_a = log_a.reshape(B, L, GLA_HEADS, GLA_DK)
    o, s_new = gla_recurrence(q, k, v, log_a, s_gla)
    o = rmsnorm(o, gla_norm_g) * jax.nn.silu(r.reshape(B, L, GLA_HEADS, GLA_DV).astype(jnp.float32))
    o = o.astype(h.dtype).reshape(B, L, GLA_HEADS * GLA_DV)
    pooled, hist_new = pool_mix(xp, pool_hist, pos0, pool_w, pool_scale)
    y = jnp.concatenate([o, pooled], axis=-1) @ w_out
    return y, s_new.astype(h.dtype), hist_new

def mla_attention(q_nope, q_pe, q_pos, k_nope, k_pe, val, k_pos):
    B, L, H, _ = q_nope.shape
    qb = min(L, ATTN_Q_BLOCK)
    n = L // qb
    k_chunk = k_pos // CHUNK

    def block(args):
        qn, qp, qpos = args
        s = (jnp.einsum('bqhd,bkhd->bhqk', qn, k_nope) + jnp.einsum('bqhd,bkd->bhqk', qp, k_pe)).astype(jnp.float32) * MLA_SCALE
        mask = k_chunk[None, :] <= (qpos // CHUNK)[:, None]
        p = jax.nn.softmax(jnp.where(mask[None, None], s, -jnp.inf), axis=-1).astype(val.dtype)
        return jnp.einsum('bhqk,bkhd->bqhd', p, val)

    def to_blocks(a):
        return a.reshape((B, n, qb) + a.shape[2:]).transpose((1, 0, 2) + tuple(range(3, a.ndim + 1)))

    out = lax.map(block, (to_blocks(q_nope), to_blocks(q_pe), q_pos.reshape(n, qb)))
    return out.transpose(1, 0, 2, 3, 4).reshape(B, L, H, val.shape[-1])

def spatial_gate(vn, gmlp_ws, gmlp_bs):
    B, L, C = vn.shape
    cl = min(L, GMLP_CHUNK)
    n = L // cl
    w = jnp.tril(gmlp_ws[:, :cl, :cl])
    vg = vn.reshape(B, n, cl, GMLP_GROUPS, GMLP_CH)
    s = jnp.einsum('gts,bnsgc->bntgc', w, vg) + gmlp_bs[:, :cl].T[None, None, :, :, None]
    return s.reshape(B, L, C)

def odd_mixer(h, ckv_past, kpe_past, w_in, q_norm_g, w_uq, kv_norm_g, w_uk, w_uv,
              gmlp_norm_g, gmlp_norm_b, gmlp_ws, gmlp_bs, w_out):
    B, L, _ = h.shape
    n_past = ckv_past.shape[1]
    cq, ckv, kpe, u, v = split_cols(h @ w_in, (MLA_Q_RANK, MLA_KV_RANK, MLA_ROPE, GMLP_WIDTH, GMLP_WIDTH))
    q_pos = n_past + jnp.arange(L)
    k_pos = jnp.arange(n_past + L)
    q = (rmsnorm(cq, q_norm_g) @ w_uq).reshape(B, L, MLA_HEADS, MLA_NOPE + MLA_ROPE)
    q_nope = q[..., :MLA_NOPE]
    q_pe = rope(q[..., MLA_NOPE:], q_pos)
    ckv = rmsnorm(ckv, kv_norm_g)
    kpe = rope(kpe, q_pos)
    ckv_all = jnp.concatenate([ckv_past.astype(ckv.dtype), ckv], axis=1)
    kpe_all = jnp.concatenate([kpe_past.astype(kpe.dtype), kpe], axis=1)
    k_nope = jnp.einsum('bkr,rhd->bkhd', ckv_all, w_uk.reshape(MLA_KV_RANK, MLA_HEADS, MLA_NOPE))
    val = jnp.einsum('bkr,rhd->bkhd', ckv_all, w_uv.reshape(MLA_KV_RANK, MLA_HEADS, MLA_V))
    attn = mla_attention(q_nope, q_pe, q_pos, k_nope, kpe_all, val, k_pos).reshape(B, L, MLA_HEADS * MLA_V)
    u = jax.nn.gelu(u)
    vn = layernorm(jax.nn.gelu(v), gmlp_norm_g, gmlp_norm_b)
    gated = (u * spatial_gate(vn, gmlp_ws, gmlp_bs)).astype(attn.dtype)
    y = jnp.concatenate([attn, gated], axis=-1) @ w_out
    return y, ckv, kpe, vn

def grouped_experts(x, eid, gate, w1, w3, w2):
    T, D = x.shape
    A = T * TOP_K
    flat_e = eid.reshape(A)
    order = jnp.argsort(flat_e)
    sorted_e = flat_e[order]
    counts = jnp.zeros((N_EXPERTS,), jnp.int32).at[flat_e].add(1)
    padded = (counts + MOE_BLOCK - 1) // MOE_BLOCK * MOE_BLOCK
    pad_end = jnp.cumsum(padded)
    pad_start = pad_end - padded
    grp_start = jnp.cumsum(counts) - counts
    dest = pad_start[sorted_e] + jnp.arange(A) - grp_start[sorted_e]
    n_blocks = A // MOE_BLOCK + N_EXPERTS
    rows = n_blocks * MOE_BLOCK
    row_tok = jnp.full((rows,), T, jnp.int32).at[dest].set((order // TOP_K).astype(jnp.int32))
    row_w = jnp.zeros((rows,), jnp.float32).at[dest].set(gate.reshape(A)[order])
    block_e = jnp.minimum(jnp.searchsorted(pad_end, jnp.arange(n_blocks) * MOE_BLOCK, side='right'), N_EXPERTS - 1)
    xpad = jnp.concatenate([x, jnp.zeros((1, D), x.dtype)], axis=0)

    def step(acc, blk):
        tok, wrow, e = blk
        xb = xpad[tok]
        hid = jax.nn.silu(xb @ w1[e]) * (xb @ w3[e])
        y = (hid @ w2[e]).astype(jnp.float32)
        return acc.at[tok].add(y * wrow[:, None]), None

    acc, _ = lax.scan(step, jnp.zeros((T + 1, D), jnp.float32),
                      (row_tok.reshape(n_blocks, MOE_BLOCK), row_w.reshape(n_blocks, MOE_BLOCK), block_e))
    return acc[:T]

def hier_moe(h, wg, bg, we, be, w1, w3, w2):
    B, L, D = h.shape
    x = h.reshape(B * L, D)
    T = x.shape[0]
    xf = x.astype(jnp.float32)
    tok = jnp.arange(T)
    g_logits = xf @ wg.astype(jnp.float32) + bg.astype(jnp.float32)
    g_sel = jnp.argmax(g_logits, axis=-1).astype(jnp.int32)
    g_prob = jax.nn.softmax(g_logits, axis=-1)[tok, g_sel]
    e_logits = (xf @ we.astype(jnp.float32) + be.astype(jnp.float32)).reshape(T, N_GROUPS, EXPERTS_PER_GROUP)
    e_logits = e_logits[tok, g_sel]
    top_v, top_i = lax.top_k(e_logits, TOP_K)
    gate = jax.nn.softmax(top_v, axis=-1) * g_prob[:, None]
    eid = g_sel[:, None] * EXPERTS_PER_GROUP + top_i.astype(jnp.int32)
    y = grouped_experts(x, eid, gate, w1, w3, w2)
    return y.astype(h.dtype).reshape(B, L, D)

def setup_inputs(seed: int = 0) -> dict:
    key = jax.random.key(seed)
    ks = iter(jax.random.split(key, 40))

    def nrm(shape, scale=1.0):
        return jax.random.normal(next(ks), shape, jnp.float32) * scale

    def gain(shape):
        return 1.0 + nrm(shape, 0.1)

    return {
        'x_prompt': nrm((BATCH, SEQ, D_MODEL)),
        'x_sample': nrm((DEC_BATCH, DEC_SEQ, D_MODEL)),
        'state_gla': nrm((N_EVEN, DEC_BATCH, GLA_HEADS, GLA_DK, GLA_DV)),
        'state_pool': nrm((N_EVEN, DEC_BATCH, POOL_HIST, POOL_WIDTH)),
        'cache_mla_ckv': nrm((N_ODD, DEC_BATCH, PAST_LEN, MLA_KV_RANK)),
        'cache_mla_kpe': nrm((N_ODD, DEC_BATCH, PAST_LEN, MLA_ROPE)),
        'w_in_even': nrm((N_EVEN, D_MODEL, D_IN_EVEN), D_MODEL ** -0.5),
        'w_gate_up': nrm((N_EVEN, GLA_GATE_RANK, GLA_HEADS * GLA_DK), GLA_GATE_RANK ** -0.5),
        'b_gate': nrm((N_EVEN, GLA_HEADS * GLA_DK), 0.1),
        'gla_norm_g': gain((N_EVEN, GLA_DV)),
        'pool_w': nrm((N_EVEN, POOL_GROUPS, POOL_CH, POOL_CH), POOL_CH ** -0.5),
        'pool_scale': gain((N_EVEN, POOL_WIDTH)),
        'w_out_even': nrm((N_EVEN, D_MIX, D_MODEL), BETA * D_MIX ** -0.5),
        'w_in_odd': nrm((N_ODD, D_MODEL, D_IN_ODD), D_MODEL ** -0.5),
        'mla_q_norm_g': gain((N_ODD, MLA_Q_RANK)),
        'mla_w_uq': nrm((N_ODD, MLA_Q_RANK, MLA_HEADS * (MLA_NOPE + MLA_ROPE)), MLA_Q_RANK ** -0.5),
        'mla_kv_norm_g': gain((N_ODD, MLA_KV_RANK)),
        'mla_w_uk': nrm((N_ODD, MLA_KV_RANK, MLA_HEADS * MLA_NOPE), MLA_KV_RANK ** -0.5),
        'mla_w_uv': nrm((N_ODD, MLA_KV_RANK, MLA_HEADS * MLA_V), MLA_KV_RANK ** -0.5),
        'gmlp_norm_g': gain((N_ODD, GMLP_WIDTH)),
        'gmlp_norm_b': nrm((N_ODD, GMLP_WIDTH), 0.02),
        'gmlp_ws': nrm((N_ODD, GMLP_GROUPS, GMLP_CHUNK, GMLP_CHUNK), 0.05),
        'gmlp_bs': gain((N_ODD, GMLP_GROUPS, GMLP_CHUNK)),
        'w_out_odd': nrm((N_ODD, D_MIX, D_MODEL), BETA * D_MIX ** -0.5),
        'ln_mix_g': gain((DEPTH, D_MODEL)),
        'ln_mix_b': nrm((DEPTH, D_MODEL), 0.02),
        'router_group_w': nrm((DEPTH, D_MODEL, N_GROUPS), D_MODEL ** -0.5),
        'router_group_b': nrm((DEPTH, N_GROUPS), 0.01),
        'router_expert_w': nrm((DEPTH, D_MODEL, N_EXPERTS), D_MODEL ** -0.5),
        'router_expert_b': nrm((DEPTH, N_EXPERTS), 0.01),
        'expert_w1': nrm((DEPTH, N_EXPERTS, D_MODEL, D_EXPERT), D_MODEL ** -0.5),
        'expert_w3': nrm((DEPTH, N_EXPERTS, D_MODEL, D_EXPERT), D_MODEL ** -0.5),
        'expert_w2': nrm((DEPTH, N_EXPERTS, D_EXPERT, D_MODEL), BETA * D_EXPERT ** -0.5),
        'ln_ffn_g': gain((DEPTH, D_MODEL)),
        'ln_ffn_b': nrm((DEPTH, D_MODEL), 0.02),
    }

def reference(x_prompt, x_sample, state_gla, state_pool, cache_mla_ckv, cache_mla_kpe,
              w_in_even, w_gate_up, b_gate, gla_norm_g, pool_w, pool_scale, w_out_even,
              w_in_odd, mla_q_norm_g, mla_w_uq, mla_kv_norm_g, mla_w_uk, mla_w_uv,
              gmlp_norm_g, gmlp_norm_b, gmlp_ws, gmlp_bs, w_out_odd,
              ln_mix_g, ln_mix_b, router_group_w, router_group_b, router_expert_w, router_expert_b,
              expert_w1, expert_w3, expert_w2, ln_ffn_g, ln_ffn_b):
    hp, hs = x_prompt, x_sample
    bp = hp.shape[0]
    gla_p, gla_s, pool_p, pool_s = [], [], [], []
    ckv_p, ckv_s, kpe_p, kpe_s, gv_s = [], [], [], [], []
    for layer in range(DEPTH):
        i = layer // 2
        if layer % 2 == 0:
            ew = (w_in_even[i], w_gate_up[i], b_gate[i], gla_norm_g[i], pool_w[i], pool_scale[i], w_out_even[i])
            s0 = jnp.zeros((bp, GLA_HEADS, GLA_DK, GLA_DV), jnp.float32)
            hist0 = jnp.zeros((bp, POOL_HIST, POOL_WIDTH), hp.dtype)
            mp, sp, pp = even_mixer(hp, s0, hist0, 0, *ew)
            ms, ss, ps = even_mixer(hs, state_gla[i], state_pool[i], PAST_LEN, *ew)
            gla_p.append(sp); gla_s.append(ss); pool_p.append(pp); pool_s.append(ps)
        else:
            ow = (w_in_odd[i], mla_q_norm_g[i], mla_w_uq[i], mla_kv_norm_g[i], mla_w_uk[i], mla_w_uv[i],
                  gmlp_norm_g[i], gmlp_norm_b[i], gmlp_ws[i], gmlp_bs[i], w_out_odd[i])
            no_ckv = jnp.zeros((bp, 0, MLA_KV_RANK), hp.dtype)
            no_kpe = jnp.zeros((bp, 0, MLA_ROPE), hp.dtype)
            mp, cp, kp, _ = odd_mixer(hp, no_ckv, no_kpe, *ow)
            ms, cs, ksmp, vs = odd_mixer(hs, cache_mla_ckv[i], cache_mla_kpe[i], *ow)
            ckv_p.append(cp); ckv_s.append(cs); kpe_p.append(kp); kpe_s.append(ksmp); gv_s.append(vs)
        hp = layernorm(ALPHA * hp + mp, ln_mix_g[layer], ln_mix_b[layer])
        hs = layernorm(ALPHA * hs + ms, ln_mix_g[layer], ln_mix_b[layer])
        mw = (router_group_w[layer], router_group_b[layer], router_expert_w[layer], router_expert_b[layer],
              expert_w1[layer], expert_w3[layer], expert_w2[layer])
        hp = layernorm(ALPHA * hp + hier_moe(hp, *mw), ln_ffn_g[layer], ln_ffn_b[layer])
        hs = layernorm(ALPHA * hs + hier_moe(hs, *mw), ln_ffn_g[layer], ln_ffn_b[layer])
    return (hp, hs, jnp.stack(gla_p), jnp.stack(gla_s), jnp.stack(pool_p), jnp.stack(pool_s),
            jnp.stack(ckv_p), jnp.stack(ckv_s), jnp.stack(kpe_p), jnp.stack(kpe_s), jnp.stack(gv_s))


_drawn_inputs = setup_inputs


def setup_inputs(seed=0):
    import zlib

    import numpy as np

    out = dict(_drawn_inputs(seed))
    spreads = {}
    factors = {'cache_mla_kpe': 3.18,
     'mla_q_norm_g': 8.0,
     'gmlp_norm_b': 2.944,
     'router_group_b': 7.706,
     'router_expert_b': 13.364,
     'gmlp_bs': 3.062}
    for name, (base, spread) in spreads.items():
        noise = np.random.default_rng([zlib.crc32(name.encode()), seed]).standard_normal(out[name].shape)
        drawn = base * np.exp(spread * noise) if base else spread * noise
        out[name] = __import__('jax').numpy.asarray(drawn.astype(out[name].dtype))
    for name, factor in factors.items():
        out[name] = (out[name] * factor).astype(out[name].dtype)
    return out
```

```python
import concourse.bass as bass
from concourse import mybir
from contextlib import ExitStack
import numpy as np

F32 = mybir.dt.float32
I32 = mybir.dt.int32
U32 = mybir.dt.uint32
ALU = mybir.AluOpType
ACT = mybir.ActivationFunctionType
AX = mybir.AxisListType

P = 128
DM = 1024
KT = DM // P
SEQ, DEC, PAST = 512, 32, 128
TOK = SEQ + DEC
ROWS = [128, 128, 128, 128, 32]
NT = len(ROWS)
DEPTH = 2
ALPHA = float((2 * DEPTH) ** 0.25)
EPS = 1e-5
NE, DE = 32, 256
NG, EPG = 4, 8
SLOTS = 64
OVER = 2 * TOK // SLOTS + 1
MAXB = NE + OVER
EXTRA = [2, 5, 8, 11]
PEELED = 12
BIG = 1e30
HALF = DM // 2
MH, MN, MR, MV = 8, 64, 32, 64
QW, QR = MN + MR, 256
AW, MW = QR + P + MR, 512
SCALE = float((MN + MR) ** -0.5)
GH, GK, GV, GR = 4, 64, 128, 16


def put(table, name, array):
    a = np.zeros((P, array.shape[1]), np.float32)
    a[:array.shape[0]] = array
    table[name] = a


def constant_table():
    c = {}
    i = np.arange(P)
    put(c, "ident", np.eye(P))
    put(c, "tri_strict", (i[:, None] < i[None, :]) * 1.0)
    put(c, "tri_incl", (i[:, None] <= i[None, :]) * 1.0)
    put(c, "ones", np.ones((P, P)))
    put(c, "iota", np.tile(np.arange(P)[None, :], (P, 1)))
    put(c, "iota_slot", np.tile((np.arange(P) % SLOTS)[None, :], (P, 1)))
    tok = np.arange(NT)[None, :] * P + i[:, None]
    valid = tok < TOK
    put(c, "valid", valid * 1.0)
    put(c, "assignment", ((2 * tok[:, :, None] + np.arange(2) + 1) * valid[:, :, None]).reshape(P, 2 * NT))
    put(c, "fills", np.tile(np.arange(9)[None, :] * SLOTS, (P, 1)))
    put(c, "pairs", np.tile(np.arange(OVER // 2)[None, :] * 2.0, (P, 1)))
    put(c, "half", (i[:, None] >= SLOTS) * 1.0)
    chunk = i // 64
    put(c, "gate_sum", ((i[:, None] <= i[None, :]) & (chunk[:, None] == chunk[None, :])) / 16.0)
    for w in (2, 4, 8, 16):
        inside = (i[:, None] <= i[None, :]) & (i[:, None] > i[None, :] - w)
        count = np.minimum(i[None, :] + 1, w)
        put(c, f"first{w}", inside / count - np.eye(P))
        put(c, f"window{w}", inside / w - np.eye(P))
        before = (i[:, None] - P) > (i[None, :] - w)
        put(c, f"before{w}", before / w)
        put(c, f"history{w}", ((np.arange(15)[:, None] - 15) > (np.arange(DEC)[None, :] - w)) / w)
    put(c, "causal", ((i[:, None] <= i[None, :]) & (chunk[:, None] == chunk[None, :])) * 1.0)
    inv = (10000.0 ** (-np.arange(16, dtype=np.float32) * 2.0 / 32)).astype(np.float32)
    pos = np.concatenate([np.arange(SEQ), PAST + np.arange(DEC)])
    pos = np.concatenate([pos, np.zeros(NT * P - TOK)]).astype(np.float32)
    ang = (pos[:, None] * inv[None, :]).astype(np.float32).reshape(NT, P, 16).transpose(1, 0, 2)
    put(c, "upto", (i[:, None] <= i[None, :]) * 1.0)
    put(c, "cos", np.cos(ang).reshape(P, NT * 16))
    put(c, "sin", np.sin(ang).reshape(P, NT * 16))
    groups = {"all": ["ident"], "route": ["tri_strict", "tri_incl", "ones", "iota", "iota_slot", "valid", "assignment", "fills", "pairs", "half"],
              "rope": ["cos", "sin", "upto"]}
    groups["even"] = [n for n in c if all(n not in g for g in groups.values())]
    c = {n: c[n] for g in ("all", "route", "even", "rope") for n in groups[g]}
    at, places = 0, {}
    for g in ("all", "route", "even", "rope"):
        first = at
        for name in groups[g]:
            places[name] = (at - first, c[name].shape[1])
            at += c[name].shape[1]
        places["group " + g] = (first, at - first)
    return np.ascontiguousarray(np.concatenate(list(c.values()), 1).astype(np.float32)), places


class Constants:

    def __init__(self, nc, ctx, S, group, name):
        first, width = S.places["group " + group]
        self.places, self.tile = S.places, ctx.enter_context(nc.sbuf_tensor(name, [P, width], F32))
        self.source = S.d["constants"][:, first:first + width]

    def __call__(self, name):
        at, width = self.places[name]
        return self.tile[:, at:at + width]


class Stage(ExitStack):

    def __init__(self, nc, prefix):
        super().__init__()
        self.nc, self.prefix, self.sems = nc, prefix, []

    def sb(self, name, shape, dt=F32):
        return self.enter_context(self.nc.sbuf_tensor(self.prefix + name, shape, dt))

    def sem(self, name):
        self.sems.append(self.nc.alloc_semaphore(self.prefix + "s_" + name))
        return self.sems[-1]

    def __exit__(self, *exc):
        out = super().__exit__(*exc)
        if exc[0] is None and self.sems:
            self.nc.clear_and_free_semaphores(self.sems)
            self.nc.all_engine_barrier()
        return out


class Chain:

    def __init__(self, sem):
        self.sem, self.n = sem, 0

    def inc(self, ins):
        ins.then_inc(self.sem, 1)
        self.n += 1
        return self.n


class Norm:

    def __init__(self, nc, sb, sem, name):
        self.nc = nc
        self.g, self.b = sb(name + "_g", [P, DM]), sb(name + "_b", [P, DM])
        self.st, self.mv = sb(name + "_st", [P, 2, 12]), sb(name + "_mv", [P, 2, 2])
        self.ve, self.rstd = (sb(name + s, [P, 2]) for s in ("_ve", "_rstd"))
        self.var, self.root, self.centred, self.scaled, self.done = (sem(name + s) for s in ("_var", "_root", "_centred", "_scaled", "_done"))
        self.chain = Chain(sem(name + "_dve"))

    def link(self, dve, ins):
        dve.wait_ge(self.chain.sem, self.chain.inc(ins))

    def vector(self, dve, t, n, src, dst):
        V, i = self.nc.vector, t % 2
        for h in range(2):
            ins = V.bn_stats(self.st[0:n, i, 6 * h:6 * h + 6], src[0:n, h * HALF:(h + 1) * HALF])
        self.link(dve, ins)
        self.link(dve, V.bn_aggr(self.mv[0:n, i, :], self.st[0:n, i, :]))
        self.link(dve, V.tensor_scalar(self.ve[0:n, i:i + 1], self.mv[0:n, i, 1:2], EPS, None, ALU.add))
        V.reciprocal(self.ve[0:n, i:i + 1], self.ve[0:n, i:i + 1]).then_inc(self.var, 1)
        V.scalar_tensor_tensor(src[0:n, :], src[0:n, :], self.mv[0:n, i, 0:1], self.g[0:n, :], ALU.subtract, ALU.mult).then_inc(self.centred, 1)
        if t == NT - 1:
            dve.wait_ge(self.root, t + 1)
            dve.wait_ge(self.centred, t + 1)
            dve.wait_ge(self.done, t)
            V.scalar_tensor_tensor(dst[0:n, :], src[0:n, :], self.rstd[0:n, i:i + 1], self.b[0:n, :], ALU.mult, ALU.add).then_inc(self.done, 1)

    def scalar(self, act, t, n):
        A, i = self.nc.scalar, t % 2
        act.wait_ge(self.var, t + 1)
        A.activation(self.rstd[0:n, i:i + 1], self.ve[0:n, i:i + 1], ACT.Sqrt).then_inc(self.root, 1)

    def pool(self, pool, t, n, src, dst):
        G, i = self.nc.gpsimd, t % 2
        if t < NT - 1:
            pool.wait_ge(self.root, t + 1)
            pool.wait_ge(self.centred, t + 1)
            G.tensor_scalar(src[0:n, :], src[0:n, :], self.rstd[0:n, i:i + 1], None, ALU.mult).then_inc(self.scaled, 1)
            pool.wait_ge(self.scaled, t + 1)
            G.tensor_tensor(dst[0:n, :], src[0:n, :], self.b[0:n, :], ALU.add).then_inc(self.done, 1)


def out_products(T, lower, upper, t, catT, wo):
    n = ROWS[t]
    if t < 4:
        for h, bank in enumerate((lower, upper)):
            for k in range(KT):
                mm = T.matmul(bank[0:n, :], catT[:, k, 0:n], wo[:, k, h * HALF:(h + 1) * HALF], start=(k == 0), stop=(k == KT - 1))
    else:
        for k in range(KT):
            for q in range(4):
                mm = T.matmul(lower[DEC * q:DEC * (q + 1), 0:256], catT[:, k, 0:n], wo[:, k, q * 256:(q + 1) * 256], start=(k == 0), stop=(k == KT - 1))
    return mm


def residual(V, lower, upper, t, x_tok, s):
    n = ROWS[t]
    parts = [(lower[0:n, :], HALF), (upper[0:n, :], HALF)] if t < 4 else [(lower[DEC * q:DEC * (q + 1), 0:256], 256) for q in range(4)]
    for i, (y, width) in enumerate(parts):
        cols = slice(i * width, (i + 1) * width)
        ins = V.scalar_tensor_tensor(s[0:n, cols], x_tok[0:n, t, cols], ALPHA, y, ALU.mult, ALU.add)
    return ins


def even_mixer(nc, S):
    bank, x_tok, ident = S.bank, S.x_tok, S.ident("ident")
    QK = 2 * GH * GK
    VW = GH * GV
    COLS = [0, QK, QK + VW, QK + 2 * VW + GR]
    GCOL = QK + 2 * VW
    CH = [(0, 64), (64, 128)]
    with Stage(nc, "m0_") as ctx:
        sb, sem = ctx.sb, ctx.sem
        C = Constants(nc, ctx, S, "even", "m0_const")
        w = [sb(f"w{c}", [P, KT, 512]) for c in range(4)]
        wg = sb("wg", [P, KT, GR])
        wo = sb("wo", [P, KT, DM])
        xT = sb("xT", [P, KT, TOK])
        gT = sb("gT", [32, TOK])
        wgu = sb("wgu", [GR + 1, GH * GK])
        pw = sb("pw", [P, 4, P])
        pscale = sb("pscale", [P, 4])
        gn = sb("gn", [P, GV])
        hist = sb("hist", [15, 512])
        state = sb("state", [P, 2, 2, GV])
        state_s = sb("state_s", [P, 2, 2, GV])
        qk = sb("qk", [P, 2, QK])
        v = sb("v", [P, 2, VW])
        r = sb("r", [P, 2, VW])
        xp = sb("xp", [P, 3, 512])
        za = sb("za", [P, 256])
        zb = sb("zb", [P, 256])
        la = zb
        bT = sb("bT", [P, 2, P])
        dm_ = sb("dmid", [P, 2, P])
        de = sb("dend", [P, 2, P])
        e1 = sb("e1", [P, 4, 2, P])
        q1 = sb("q1", [P, 2, 2, P])
        k1, k2 = e1[:, 1, :, :], e1[:, 2, :, :]
        q2 = sb("q2", [P, 2, P])
        k2t = sb("k2t", [P, 256])
        sT = sb("sT", [P, GH, P])
        ssq = sb("ssq", [P, GH])
        rs = sb("rs", [P, GH])
        sq = sb("sq", [P, GV])
        co = sb("co", [P, VW])
        er = co
        mixT = sb("mixT", [P, 4, P])
        catT = sb("catT", [P, KT, P])
        s = sb("s", [P, DM])
        ln = Norm(nc, sb, sem, "mix")

        x_in, c_in, g_in, small = sem("x_in"), sem("c_in"), sem("g_in"), sem("small")
        w_in = [sem(f"w_in{c}") for c in range(4)]
        wo_in, st_out = sem("wo_in"), sem("st_out")
        p_xT, a_xT, p_g, a_g = sem("p_xT"), sem("a_xT"), sem("p_g"), sem("a_g")
        p_in, in_sb = sem("p_in"), sem("in_sb")
        p_z, d_la, p_b, d_q, p_s, d_s = sem("p_z"), sem("d_la"), sem("p_b"), sem("d_q"), sem("p_s"), sem("d_s")
        p_k2, a_k2, p_mix, a_mix, p_pool, a_pool = sem("p_k2"), sem("a_k2"), sem("p_mix"), sem("a_mix"), sem("p_pool"), sem("a_pool")
        p_sps, p_oc, d_st, d_o, p_c, a_c = sem("p_sps"), sem("p_oc"), sem("d_st"), sem("d_o"), sem("p_c"), sem("a_c")
        p_y, d_y, a_gate, d_gate, a_exp, d_d, a_sq, d_sq, a_rs = (sem(x) for x in ("p_y", "d_y", "a_gate", "d_gate", "a_exp", "d_d", "a_sq", "d_sq", "a_rs"))
        a_er, d_r, g_r, d_zero = sem("a_er"), sem("d_r"), sem("g_r"), sem("d_zero")
        dch, ach = Chain(sem("d_chain")), Chain(sem("a_chain"))
        NCH = [2, 2, 2, 2, 1]
        CDONE = [0, 2, 4, 6, 8, 9]
        block = ctx.enter_context(nc.Block(no_gpsimd_drain=True))
        D = S.d

        @block.sync
        def _(sp):
            sp.dma_start(x_tok[:, 0:2, :], D["x_prompt"][0, 0:256, :].rearrange("(t p) d -> p t d", p=P)).then_inc(x_in, 16)
            sp.dma_start(S.ident.tile[:], S.ident.source).then_inc(c_in, 16)
            sp.dma_start(x_tok[:, 2:4, :], D["x_prompt"][0, 256:512, :].rearrange("(t p) d -> p t d", p=P)).then_inc(x_in, 16)
            sp.dma_start(x_tok[0:DEC, 4, :], D["x_sample"][0]).then_inc(x_in, 16)
            win = D["w_in_even"][0].rearrange("(k p) n -> p k n", p=P)
            sp.dma_start(wg[:], win[:, :, GCOL:GCOL + GR]).then_inc(g_in, 16)
            for c in range(4):
                sp.dma_start(w[c][:], win[:, :, COLS[c]:COLS[c] + 512]).then_inc(w_in[c], 16)
            sp.dma_start(wo[:], D["w_out_even"][0].rearrange("(k p) n -> p k n", p=P)).then_inc(wo_in, 16)
            for t, dst in ((3, S.o["gla_state_prompt"]), (4, S.o["gla_state_sample"])):
                sp.wait_ge(d_st, CDONE[t + 1])
                src = state if t == 3 else state_s
                for h in range(2):
                    sp.dma_start(dst[0, 0].rearrange("(m h) k v -> h k m v", h=2)[h], src[64 * h:64 * h + 64, :, h, :]).then_inc(S.out_done, 16)
            for t in range(NT):
                sp.wait_ge(ln.done, t + 1)
                n = ROWS[t]
                sp.dma_start(S.x_rows.rearrange("(t h) c -> t (h c)", h=2)[t * P:t * P + n, :], x_tok[0:n, t, :]).then_inc(st_out, 16)
            sp.wait_ge(st_out, 16 * NT)

        @block.scalar
        def _(act):
            A = nc.scalar

            def alink(ins):
                act.wait_ge(ach.sem, ach.inc(ins))

            act.dma_start(C.tile[:], C.source).then_inc(small, 16)
            act.dma_start(wgu[0:GR, :], D["w_gate_up"][0]).then_inc(small, 16)
            act.dma_start(wgu[GR:GR + 1, :], D["b_gate"][0:1, :]).then_inc(small, 16)
            act.dma_start(pw[:], D["pool_w"][0].rearrange("g c d -> c g d")).then_inc(small, 16)
            act.dma_start(pscale[:], D["pool_scale"]).then_inc(small, 16)
            act.dma_start(gn[:], D["gla_norm_g"][0:1, :].to_broadcast([P, GV])).then_inc(small, 16)
            act.dma_start(hist[:], D["state_pool"][0, 0]).then_inc(small, 16)
            act.wait_ge(d_zero, 3)
            for h in range(2):
                act.dma_start(state_s[64 * h:64 * h + 64, :, h, :], D["state_gla"][0, 0].rearrange("(m h) k v -> h k m v", h=2)[h]).then_inc(small, 16)
            act.dma_start(ln.g[:], D["ln_mix_g"][0:1, :].to_broadcast([P, DM])).then_inc(small, 16)
            act.dma_start(ln.b[:], D["ln_mix_b"][0:1, :].to_broadcast([P, DM])).then_inc(small, 16)

            for i in range(2 * NT):
                t, h = i // 2, i % 2
                n = ROWS[t]
                act.wait_ge(p_xT, i + 1)
                A.activation(xT[:, 4 * h:4 * h + 4, t * P:t * P + n], bank[i % 4][:].rearrange("p (k n) -> p k n", k=4)[:, :, 0:n], ACT.Copy).then_inc(a_xT, 1)
            act.wait_ge(p_g, 1)
            for h in range(2):
                ins = A.activation(gT[0:GR, h * 272:(h + 1) * 272], bank[4 + h][0:GR, 0:272], ACT.Copy)
            ins.then_inc(a_g, 1)

            def evacuate(t, c):
                n = ROWS[t]
                act.wait_ge(p_in, 4 * t + c + 1)
                if t >= 2:
                    if c == 0:
                        act.wait_ge(p_b, t - 1)
                    elif c == 1:
                        act.wait_ge(p_oc, CDONE[t - 1])
                    elif c == 2:
                        act.wait_ge(d_o, t - 1)
                if c == 3 and t >= 3:
                    act.wait_ge(p_mix, t - 1)
                dst = (qk[0:n, t % 2, :], v[0:n, t % 2, :], r[0:n, t % 2, :], xp[0:n, t % 3, :])[c]
                src = bank[c % 2][0:n, :] if t < 4 else bank[0][DEC * c:DEC * (c + 1), :]
                A.activation(dst, src, ACT.Copy).then_inc(in_sb, 1)

            for c in range(4):
                evacuate(0, c)
            for t, n in enumerate(ROWS):
                nxt = t + 1 < NT
                act.wait_ge(p_z, t + 1)
                if t >= 1:
                    act.wait_ge(d_la, t)
                alink(A.activation(za[0:n, :], bank[4][0:n, 0:256], ACT.Abs))
                if t >= 1:
                    act.wait_ge(p_b, t)
                alink(A.activation(zb[0:n, :], za[0:n, :], ACT.Exp, scale=-1.0))
                A.activation(za[0:n, :], zb[0:n, :], ACT.Ln, bias=1.0).then_inc(a_gate, 1)
                if nxt:
                    evacuate(t + 1, 0)
                act.wait_ge(d_d, t + 1)
                if t >= 1:
                    act.wait_ge(d_st, CDONE[t])
                    act.wait_ge(p_k2, t)
                A.activation(e1[:, 0, :, 0:n], dm_[:, :, 0:n], ACT.Exp)
                A.activation(e1[:, 1, :, 0:n], dm_[:, :, 0:n], ACT.Exp, scale=-1.0)
                A.activation(e1[:, 2, :, 0:n], de[:, :, 0:n], ACT.Exp)
                A.activation(e1[:, 3, :, 0:n], bT[:, :, 0:n], ACT.Exp).then_inc(a_exp, 1)
                if nxt:
                    evacuate(t + 1, 1)
                act.wait_ge(in_sb, 4 * t + 3)
                if t >= 1:
                    act.wait_ge(p_c, t)
                A.activation(er[0:n, :], r[0:n, t % 2, :], ACT.Exp, scale=-1.0).then_inc(a_er, 1)
                act.wait_ge(p_k2, t + 1)
                A.activation(k2t[0:n, :], bank[4][0:n, 0:256], ACT.Copy).then_inc(a_k2, 1)
                if nxt:
                    evacuate(t + 1, 2)
                act.wait_ge(p_mix, t + 1)
                A.activation(mixT[:, :, 0:n], bank[6][:].rearrange("p (g n) -> p g n", g=4)[:, :, 0:n], ACT.Copy).then_inc(a_mix, 1)
                act.wait_ge(p_pool, t + 1)
                if t >= 1:
                    act.wait_ge(p_y, t)
                for g in range(4):
                    ins = A.activation(catT[:, 4 + g, 0:n], bank[6][:, g * P:g * P + n], ACT.Copy, scale=pscale[:, g:g + 1])
                ins.then_inc(a_pool, 1)
                if nxt:
                    evacuate(t + 1, 3)
                act.wait_ge(p_oc, CDONE[t + 1])
                for h in range(GH):
                    if h or t:
                        act.wait_ge(a_sq, GH * t + h)
                    A.activation(sq[0:n, :], bank[7][0:n, h * GV:(h + 1) * GV], ACT.Square, accum_out=ssq[0:n, h:h + 1]).then_inc(a_sq, 1)
                act.wait_ge(d_sq, t + 1)
                A.activation(rs[0:n, :], ssq[0:n, :], ACT.Sqrt).then_inc(a_rs, 1)
                act.wait_ge(p_c, t + 1)
                A.activation(catT[:, 0:4, 0:n], bank[6][:].rearrange("p (g n) -> p g n", g=4)[:, :, 0:n], ACT.Copy).then_inc(a_c, 1)
                ln.scalar(act, t, n)

        @block.vector
        def _(dve):
            V = nc.vector

            def link(ins):
                dve.wait_ge(dch.sem, dch.inc(ins))

            V.memset(gT[:], 1.0).then_inc(d_zero, 1)
            V.memset(state[:], 0.0).then_inc(d_zero, 1)
            V.memset(state_s[:], 0.0).then_inc(d_zero, 1)
            V.memset(q1[:], 0.0)
            link(V.memset(sT[:], 0.0))
            dve.wait_ge(small, 176)
            for t, n in enumerate(ROWS):
                nch, w_ = NCH[t], min(64, n)
                st = state if t < 4 else state_s
                dve.wait_ge(a_gate, t + 1)
                if t >= 1:
                    dve.wait_ge(p_b, t)
                V.scalar_tensor_tensor(la[0:n, :], bank[4][0:n, 0:256], 0.0, za[0:n, :], ALU.min, ALU.subtract).then_inc(d_la, 1)
                dve.wait_ge(p_b, t + 1)
                if t >= 1:
                    dve.wait_ge(a_exp, t)
                link(V.tensor_copy(bT[:, :, 0:n], bank[4][:, 256:512].rearrange("p (m n) -> p m n", m=2)[:, :, 0:n]))
                for m in range(2):
                    b4 = bT[:, m, 0:n].rearrange("p (c i) -> p c i", i=w_)
                    V.tensor_tensor(dm_[:, m, 0:n].rearrange("p (c i) -> p c i", i=w_), b4, b4[:, :, w_ // 2 - 1:w_ // 2].to_broadcast([P, nch, w_]), ALU.subtract)
                    ins = V.tensor_tensor(de[:, m, 0:n].rearrange("p (c i) -> p c i", i=w_), b4[:, :, w_ - 1:w_].to_broadcast([P, nch, w_]), b4, ALU.subtract)
                link(ins)
                V.tensor_scalar(dm_[:, :, 0:n], dm_[:, :, 0:n], 80.0, -80.0, ALU.min, ALU.max).then_inc(d_d, 1)
                dve.wait_ge(a_exp, t + 1)
                z5 = bank[5][:].rearrange("p (m n) -> p m n", m=4)
                if t >= 1:
                    dve.wait_ge(p_oc, CDONE[t])
                for h in range(2):
                    hs = slice(64 * h, 64 * h + 64)
                    V.scalar_tensor_tensor(q1[hs, :, h, 0:n], z5[hs, 0:2, 0:n], GK ** -0.5, e1[hs, 0, :, 0:n], ALU.mult, ALU.mult)
                V.scalar_tensor_tensor(q2[:, :, 0:n], z5[:, 0:2, 0:n], GK ** -0.5, e1[:, 3, :, 0:n], ALU.mult, ALU.mult)
                V.tensor_tensor(k1[:, :, 0:n], z5[:, 2:4, 0:n], e1[:, 1, :, 0:n], ALU.mult)
                link(V.tensor_tensor(k2[:, :, 0:n], z5[:, 2:4, 0:n], e1[:, 2, :, 0:n], ALU.mult))
                dve.sem_inc(d_q, 1)
                dve.wait_ge(a_er, t + 1)
                link(V.tensor_scalar(er[0:n, :], er[0:n, :], 1.0, None, ALU.add))
                link(V.reciprocal(er[0:n, :], er[0:n, :]))
                V.tensor_tensor(r[0:n, t % 2, :], r[0:n, t % 2, :], er[0:n, :], ALU.mult).then_inc(d_r, 1)
                dve.wait_ge(p_s, t + 1)
                for h in range(GH):
                    ins = V.copy_predicated(sT[0:n, h, 0:n], C("causal")[0:n, 0:n].bitcast(U32), bank[6][0:n, h * P:h * P + n])
                ins.then_inc(d_s, 1)
                for c in range(nch):
                    dve.wait_ge(p_sps, t + 1)
                    dve.wait_ge(p_oc, CDONE[t] + c + 1)
                    for m in range(2):
                        for h in range(2):
                            hs = slice(64 * h, 64 * h + 64)
                            ins = V.scalar_tensor_tensor(st[hs, m, h, :], st[hs, m, h, :], e1[hs, 3, m, c * 64 + w_ - 1:c * 64 + w_],
                                                         bank[5 - c][hs, (2 * m + h) * P:(2 * m + h + 1) * P], ALU.mult, ALU.add)
                    link(ins)
                    dve.sem_inc(d_st, 1)
                dve.wait_ge(a_sq, GH * (t + 1))
                link(V.tensor_scalar(ssq[0:n, :], ssq[0:n, :], 1.0 / GV, EPS, ALU.mult, ALU.add))
                link(V.reciprocal(ssq[0:n, :], ssq[0:n, :]))
                dve.sem_inc(d_sq, 1)
                dve.wait_ge(a_rs, t + 1)
                dve.wait_ge(g_r, t + 1)
                for h in range(GH):
                    hs = slice(h * GV, (h + 1) * GV)
                    ins = V.scalar_tensor_tensor(co[0:n, hs], bank[7][0:n, hs], rs[0:n, h:h + 1], r[0:n, t % 2, hs], ALU.mult, ALU.mult)
                ins.then_inc(d_o, 1)
                if t >= 1:
                    dve.wait_ge(ln.done, t)
                dve.wait_ge(p_y, t + 1)
                link(residual(V, bank[2], bank[3], t, x_tok, s))
                dve.sem_inc(d_y, 1)
                ln.vector(dve, t, n, s, x_tok[:, t, :])

        @block.gpsimd
        def _(pool):
            G = nc.gpsimd
            pool.wait_ge(small, 176)
            for t, n in enumerate(ROWS):
                pool.wait_ge(d_r, t + 1)
                G.tensor_tensor(r[0:n, t % 2, :].rearrange("p (h v) -> p h v", h=GH), r[0:n, t % 2, :].rearrange("p (h v) -> p h v", h=GH),
                                gn[0:n, :].unsqueeze(1).to_broadcast([n, GH, GV]), ALU.mult).then_inc(g_r, 1)
                if t >= 3:
                    pool.wait_ge(in_sb, 4 * t + 4)
                    dst = S.o["pool_state_prompt"] if t == 3 else S.o["pool_state_sample"]
                    pool.dma_start(dst[0, 0], xp[n - 15:n, t % 3, :]).then_inc(S.out_pool, 16)
                ln.pool(pool, t, n, s, x_tok[:, t, :])
            pool.wait_ge(ln.done, NT)
            pool.wait_ge(S.out_pool, 32)

        @block.tensor
        def _(pe):
            T = nc.tensor
            pe.wait_ge(c_in, 16)
            for t, n in enumerate(ROWS):
                if t == 0:
                    pe.wait_ge(x_in, 48)
                for h in range(2):
                    i = 2 * t + h
                    if i >= 4:
                        pe.wait_ge(a_xT, i - 3)
                    for q in range(4):
                        k = 4 * h + q
                        mm = T.transpose(bank[i % 4][:, q * P:q * P + n], x_tok[0:n, t, k * P:(k + 1) * P], ident[0:n, 0:n])
                    mm.then_inc(p_xT, 1)
            pe.wait_ge(a_xT, 2 * NT)
            pe.wait_ge(g_in, 16)
            for h in range(2):
                for k in range(KT):
                    mm = T.matmul(bank[4 + h][0:GR, 0:272], wg[:, k, :], xT[:, k, h * 272:(h + 1) * 272], start=(k == 0), stop=(k == KT - 1))
            mm.then_inc(p_g, 1)

            def project(t, c):
                n = ROWS[t]
                if t == 0:
                    pe.wait_ge(w_in[c], 16)
                if t == 4 and c > 0:
                    return
                if 4 * t + c >= 2:
                    pe.wait_ge(in_sb, 4 * t + c - 1)
                if t == 4:
                    for k in range(KT):
                        for g in range(4):
                            mm = T.matmul(bank[0][DEC * g:DEC * (g + 1), :], xT[:, k, t * P:t * P + n], w[g][:, k, :], start=(k == 0), stop=(k == KT - 1))
                    mm.then_inc(p_in, 4)
                    return
                for k in range(KT):
                    mm = T.matmul(bank[c % 2][0:n, :], xT[:, k, t * P:t * P + n], w[c][:, k, :], start=(k == 0), stop=(k == KT - 1))
                mm.then_inc(p_in, 1)

            for c in range(4):
                project(0, c)
            pe.wait_ge(a_g, 1)
            pe.wait_ge(small, 176)
            for t, n in enumerate(ROWS):
                nch, w_ = NCH[t], min(64, n)
                st = state if t < 4 else state_s
                nxt = t + 1 < NT
                if t >= 1:
                    pe.wait_ge(d_st, CDONE[t])
                T.matmul(bank[4][0:n, 0:256], gT[0:GR + 1, t * P:t * P + n], wgu[:], start=True, stop=True).then_inc(p_z, 1)
                if nxt:
                    project(t + 1, 0)
                pe.wait_ge(d_la, t + 1)
                pe.wait_ge(in_sb, 4 * t + 1)
                for m in range(2):
                    T.matmul(bank[4][:, 256 + m * P:256 + m * P + n], la[0:n, m * P:(m + 1) * P], C("gate_sum")[0:n, 0:n], start=True, stop=True)
                if t >= 1:
                    pe.wait_ge(d_st, CDONE[t])
                for m in range(4):
                    mm = T.transpose(bank[5][:, m * P:m * P + n], qk[0:n, t % 2, m * P:(m + 1) * P], ident[0:n, 0:n])
                mm.then_inc(p_b, 1)
                if nxt:
                    project(t + 1, 1)
                pe.wait_ge(d_q, t + 1)
                if t >= 1:
                    pe.wait_ge(a_c, t)
                for m in range(2):
                    mm = T.matmul(bank[6][0:n, 2 * m * P:2 * (m + 1) * P].rearrange("p (h n) -> p h n", h=2)[:, :, 0:n], k1[:, m, 0:n], q1[:, m, :, 0:n],
                                  start=(m == 0), stop=(m == 1), skip_group_check=True)
                mm.then_inc(p_s, 1)
                for m in range(2):
                    mm = T.transpose(bank[4][0:n, m * P:(m + 1) * P], k2[:, m, 0:n], ident)
                mm.then_inc(p_k2, 1)
                if nxt:
                    project(t + 1, 2)
                pe.wait_ge(in_sb, 4 * t + 2)
                pe.wait_ge(d_s, t + 1)
                if t >= 1:
                    pe.wait_ge(d_o, t)
                for h in range(GH):
                    T.matmul(bank[7][0:n, h * GV:(h + 1) * GV], sT[0:n, h, 0:n], v[0:n, t % 2, h * GV:(h + 1) * GV], start=(h == 0), stop=False, skip_group_check=True)
                pe.wait_ge(a_k2, t + 1)
                for c in range(nch):
                    for m in range(2):
                        mm = T.matmul(bank[5 - c][:, m * 256:(m + 1) * 256], k2t[c * 64:c * 64 + w_, m * P:(m + 1) * P],
                                      v[c * 64:c * 64 + w_, t % 2, m * 256:(m + 1) * 256], start=(m == 0), stop=(m == 1), skip_group_check=True)
                mm.then_inc(p_sps, 1)
                pe.wait_ge(in_sb, 4 * t + 4)
                for g, win in enumerate((2, 4, 8, 16)):
                    now = C(f"first{win}" if t == 0 else f"window{win}")[0:n, 0:n]
                    parts = [(xp[0:n, t % 3, g * P:(g + 1) * P], now)]
                    if 0 < t < 4:
                        parts.append((xp[:, (t - 1) % 3, g * P:(g + 1) * P], C(f"before{win}")))
                    elif t == 4:
                        parts.append((hist[:, g * P:(g + 1) * P], C(f"history{win}")[0:15, :]))
                    for i, (rows, window) in enumerate(parts):
                        mm = T.matmul(bank[6][:, g * P:g * P + n], rows, window, start=(g == 0 and i == 0), stop=(g == 3 and i == len(parts) - 1), skip_group_check=True)
                mm.then_inc(p_mix, 1)
                pe.wait_ge(a_mix, t + 1)
                for g in range(4):
                    mm = T.matmul(bank[6][:, g * P:g * P + n], pw[:, g, :], mixT[:, g, 0:n], start=(g == 0), stop=(g == 3), skip_group_check=True)
                mm.then_inc(p_pool, 1)
                for c in range(nch):
                    if t == 0 and c == 0:
                        pe.wait_ge(d_zero, 2)
                    elif CDONE[t] + c > 0:
                        pe.wait_ge(d_st, CDONE[t] + c)
                    for m in range(2):
                        mm = T.matmul(bank[7][c * 64:c * 64 + w_, m * 256:(m + 1) * 256], q2[:, m, c * 64:c * 64 + w_],
                                      st[:, m, :, :], start=False, stop=(c == nch - 1 and m == 1), skip_group_check=True)
                    mm.then_inc(p_oc, 1)
                if nxt:
                    project(t + 1, 3)
                pe.wait_ge(d_o, t + 1)
                pe.wait_ge(a_pool, t + 1)
                for m in range(4):
                    mm = T.transpose(bank[6][:, m * P:m * P + n], co[0:n, m * P:(m + 1) * P], ident[0:n, 0:n])
                mm.then_inc(p_c, 1)
                pe.wait_ge(a_c, t + 1)
                pe.wait_ge(wo_in, 16)
                if t >= 1:
                    pe.wait_ge(d_y, t)
                mm = out_products(T, bank[2], bank[3], t, catT, wo)
                mm.then_inc(p_y, 1)


def odd_mixer(nc, S):
    bank, x_tok, ident, D = S.bank, S.x_tok, S.ident("ident"), S.d
    KEYS = SEQ + PAST + DEC
    FIRST, FW = [0, AW, AW + MW], [AW, MW, MW]
    KPOS = [0, 128, 256, 384, SEQ + PAST]
    with Stage(nc, "m1_") as ctx:
        sb = ctx.sb
        qT = sb("qT", [QW, MH, TOK])
        kT = sb("kT", [QW, MH, KEYS])
        val = sb("val", [P, NT + 1, MH * MV])
        u = sb("u", [P, NT, MW])

        with Stage(nc, "m1w_") as wc, ExitStack() as inner:
            w = [wc.sb(f"w{c}", [P, KT, FW[c]]) for c in range(3)]
            xT = wc.sb("xT", [P, KT, TOK])
            w_in = [wc.sem(f"w_in{c}") for c in range(3)]

            def load_w(sp):
                win = D["w_in_odd"][0].rearrange("(k p) n -> p k n", p=P)
                for c in range(3):
                    sp.dma_start(w[c][:], win[:, :, FIRST[c]:FIRST[c] + FW[c]]).then_inc(w_in[c], 16)

            combine(nc, S, 0, (xT, load_w))
            pc = inner.enter_context(Stage(nc, "m1p_"))
            pb, sem = pc.sb, pc.sem
            C = Constants(nc, pc, S, "rope", "m1_const")
            wuq = pb("wuq", [P, 2, MH * QW])
            wuk = pb("wuk", [P, MH * MN])
            wuv = pb("wuv", [P, MH * MV])
            qg = pb("qg", [P, QR])
            kg = pb("kg", [P, P])
            vg = pb("vg", [P, MW])
            vb = pb("vb", [P, MW])
            ws = pb("ws", [P, 4, P])
            wsT = pb("wsT", [P, 4, P])
            bs = pb("bs", [P, 4])
            lat = pb("lat", [P, 2, AW])
            sq = pb("sq", [P, QR])
            ss = pb("ss", [P, 2, 2])
            rs = pb("rs", [P, 2, 2])
            cqn = pb("cqn", [P, 2, QR])
            ckvn = pb("ckvn", [P, NT + 1, P])
            kst = pb("kst", [P, NT + 1, QW])
            rt = pb("rt", [P, 4, MR // 2])
            cqT = pb("cqT", [P, 2, P])
            ckvT = pb("ckvT", [P, KEYS])
            qr = pb("qr", [P, MH, QW])
            qt = pb("qt", [P, 4, MH, MR // 2])
            gv = pb("gv", [P, 2, MW])
            vst = pb("vst", [P, 6])
            vmv = pb("vmv", [P, 2])
            vve = pb("vve", [P, 1])
            vrs = pb("vrs", [P, 1])
            small = sem("small")
            cache_in, ws_in = sem("cache_in"), sem("ws_in")
            p_in, in_sb = sem("p_in"), sem("in_sb")
            p_ws, d_ws, a_ss, d_ss, a_rs, d_n = sem("p_ws"), sem("d_ws"), sem("a_ss"), sem("d_ss"), sem("a_rs"), sem("d_n")
            p_small, a_cqT, p_uq, a_q, d_rope, p_qT, a_qT = (sem(x) for x in ("p_small", "a_cqT", "p_uq", "a_q", "d_rope", "p_qT", "a_qT"))
            d_kpe, d_vv, a_vrs, d_vs, g_vn, p_gate, d_gated = (sem(x) for x in ("d_kpe", "d_vv", "a_vrs", "d_vs", "g_vn", "p_gate", "d_gated"))
            p_k, a_k, p_val, d_val, d_zero = sem("p_k"), sem("a_k"), sem("p_val"), sem("d_val"), sem("d_zero")
            dch, ach, gch = Chain(sem("d_chain")), Chain(sem("a_chain")), Chain(sem("g_chain"))
            block = pc.enter_context(nc.Block(no_gpsimd_drain=True))

            @block.sync
            def _(sp):
                for t, n in enumerate(ROWS):
                    sp.wait_ge(d_n, t + 1)
                    sp.wait_ge(d_kpe, t + 1)
                    part = (lambda a: a[0, 0, t * P:t * P + n, :]) if t < 4 else (lambda a: a[0, 0])
                    which = "prompt" if t < 4 else "sample"
                    sp.dma_start(part(S.o["mla_ckv_" + which]), ckvn[0:n, t, :]).then_inc(S.out_done, 16)
                    sp.dma_start(part(S.o["mla_kpe_" + which]), kst[0:n, t, MN:QW]).then_inc(S.out_done, 16)
                sp.wait_ge(g_vn, NT)
                sp.dma_start(S.o["gmlp_v_sample"][0, 0], gv[0:DEC, (NT - 1) % 2, :]).then_inc(S.out_done, 16)
                sp.wait_ge(S.out_done, S.OUT_ODD)

            @block.scalar
            def _(act):
                A = nc.scalar

                def alink(ins):
                    act.wait_ge(ach.sem, ach.inc(ins))

                act.dma_start(ws[:], D["gmlp_ws"][0].rearrange("g t s -> t g s")).then_inc(ws_in, 16)
                act.dma_start(C.tile[:], C.source).then_inc(ws_in, 16)
                act.dma_start(ckvn[:, NT, :], D["cache_mla_ckv"][0, 0]).then_inc(cache_in, 16)
                act.wait_ge(d_zero, 1)
                act.dma_start(kst[:, NT, MN:QW], D["cache_mla_kpe"][0, 0]).then_inc(cache_in, 16)
                for dst, src in ((qg, D["mla_q_norm_g"][0:1, :].to_broadcast([P, QR])), (kg, D["mla_kv_norm_g"][0:1, :].to_broadcast([P, P])),
                                 (vg, D["gmlp_norm_g"][0:1, :].to_broadcast([P, MW])), (vb, D["gmlp_norm_b"][0:1, :].to_broadcast([P, MW])),
                                 (wuq, D["mla_w_uq"][0].rearrange("(k p) n -> p k n", p=P)), (wuk, D["mla_w_uk"][0]), (wuv, D["mla_w_uv"][0]),
                                 (bs, D["gmlp_bs"])):
                    act.dma_start(dst[:], src).then_inc(small, 16)

                def evacuate(t, c):
                    n, i = ROWS[t], 3 * t + c
                    act.wait_ge(p_in, i + 1)
                    src = bank[i % 2][0:n, 0:FW[c]] if t < 4 else bank[0][DEC * c:DEC * (c + 1), 0:FW[c]]
                    if c == 0:
                        if t >= 2:
                            act.wait_ge(d_kpe, t - 1)
                            act.wait_ge(d_n, t - 1)
                        A.activation(lat[0:n, t % 2, :], src, ACT.Copy).then_inc(in_sb, 1)
                    elif c == 1:
                        A.activation(u[0:n, t, :], src, ACT.Gelu_apprx_tanh).then_inc(in_sb, 1)
                    else:
                        if t >= 2:
                            act.wait_ge(p_gate, t - 1)
                        A.activation(gv[0:n, t % 2, :], src, ACT.Gelu_apprx_tanh).then_inc(in_sb, 1)

                def mean_squares(t):
                    n = ROWS[t]
                    act.wait_ge(in_sb, 3 * t + 1)
                    if t >= 1:
                        act.wait_ge(d_ss, t)
                    if t >= 2:
                        act.wait_ge(d_n, t - 1)
                    alink(A.activation(sq[0:n, :], lat[0:n, t % 2, 0:QR], ACT.Square, accum_out=ss[0:n, t % 2, 0:1]))
                    A.activation(sq[0:n, 0:P], lat[0:n, t % 2, QR:QR + P], ACT.Square, accum_out=ss[0:n, t % 2, 1:2]).then_inc(a_ss, 1)

                def deviations(t):
                    n = ROWS[t]
                    act.wait_ge(d_ss, t + 1)
                    A.activation(rs[0:n, t % 2, :], ss[0:n, t % 2, :], ACT.Sqrt).then_inc(a_rs, 1)
                    act.wait_ge(d_vv, t + 1)
                    A.activation(vrs[0:n, :], vve[0:n, :], ACT.Sqrt).then_inc(a_vrs, 1)

                for c in range(3):
                    evacuate(0, c)
                mean_squares(0)
                for t, n in enumerate(ROWS):
                    nxt = t + 1 < NT
                    deviations(t)
                    if nxt:
                        evacuate(t + 1, 0)
                    act.wait_ge(p_small, t + 1)
                    if t >= 1:
                        act.wait_ge(p_uq, t)
                    A.activation(cqT[:, :, 0:n], bank[3][:, 0:256].rearrange("p (k n) -> p k n", k=2)[:, :, 0:n], ACT.Copy)
                    A.activation(ckvT[:, KPOS[t]:KPOS[t] + n], bank[3][:, 256:256 + n], ACT.Copy).then_inc(a_cqT, 1)
                    if nxt:
                        evacuate(t + 1, 1)
                    act.wait_ge(p_uq, t + 1)
                    if t >= 1:
                        act.wait_ge(p_qT, t)
                    for h in range(2):
                        ins = A.activation(qr[0:n, 4 * h:4 * h + 4, :].rearrange("p h d -> p (h d)"), bank[4 + h][0:n, 0:4 * QW], ACT.Copy)
                    ins.then_inc(a_q, 1)
                    if nxt:
                        evacuate(t + 1, 2)
                        mean_squares(t + 1)
                    act.wait_ge(p_qT, t + 1)
                    for h in range(2):
                        ins = A.activation(qT[:, 4 * h:4 * h + 4, t * P:t * P + n], bank[6 + h][0:QW, :].rearrange("p (h n) -> p h n", h=4)[:, :, 0:n], ACT.Copy)
                    ins.then_inc(a_qT, 1)
                for i in range(8):
                    pair, part = i // 2, i % 2
                    keys = slice(0, SEQ) if part == 0 else slice(SEQ, KEYS)
                    width = keys.stop - keys.start
                    act.wait_ge(p_k, i + 1)
                    A.activation(kT[0:MN, 2 * pair, keys], bank[i % 4][0:MN, 0:width], ACT.Copy)
                    A.activation(kT[0:MN, 2 * pair + 1, keys], bank[i % 4][MN:P, 0:width], ACT.Copy).then_inc(a_k, 1)

            @block.vector
            def _(dve):
                V = nc.vector

                def link(ins):
                    dve.wait_ge(dch.sem, dch.inc(ins))

                link(V.memset(kst[:], 0.0))
                dve.sem_inc(d_zero, 1)
                link(V.memset(wsT[:], 0.0))
                dve.wait_ge(p_ws, 1)
                for g in range(4):
                    ins = V.copy_predicated(wsT[:, g, :], C("upto")[:].bitcast(U32), bank[7][:, g * P:(g + 1) * P])
                link(ins)
                dve.sem_inc(d_ws, 1)
                dve.wait_ge(small, 128)

                def rotated_keys(slot, rows):
                    at = KPOS[slot] if slot < NT else SEQ
                    return V.tensor_copy(kT[MN:QW, :, at:at + rows], bank[3][MN:QW, 384:384 + rows].unsqueeze(1).to_broadcast([MR, MH, rows]))

                def statistics(t):
                    n = ROWS[t]
                    dve.wait_ge(a_ss, t + 1)
                    V.tensor_scalar(ss[0:n, t % 2, 0:1], ss[0:n, t % 2, 0:1], 1.0 / QR, EPS, ALU.mult, ALU.add)
                    link(V.tensor_scalar(ss[0:n, t % 2, 1:2], ss[0:n, t % 2, 1:2], 1.0 / P, EPS, ALU.mult, ALU.add))
                    V.reciprocal(ss[0:n, t % 2, :], ss[0:n, t % 2, :]).then_inc(d_ss, 1)
                    dve.wait_ge(in_sb, 3 * t + 3)
                    link(V.bn_stats(vst[0:n, :], gv[0:n, t % 2, :]))
                    link(V.bn_aggr(vmv[0:n, :], vst[0:n, :]))
                    link(V.tensor_scalar(vve[0:n, :], vmv[0:n, 1:2], EPS, None, ALU.add))
                    V.reciprocal(vve[0:n, :], vve[0:n, :]).then_inc(d_vv, 1)

                def rotate(dst, x1, x2, tmp, cos, sin):
                    V.tensor_tensor(tmp[0], x1, cos, ALU.mult)
                    V.tensor_tensor(tmp[1], x2, sin, ALU.mult)
                    V.tensor_tensor(tmp[2], x1, sin, ALU.mult)
                    link(V.tensor_tensor(tmp[3], x2, cos, ALU.mult))
                    V.tensor_tensor(dst[0], tmp[0], tmp[1], ALU.subtract)
                    return V.tensor_tensor(dst[1], tmp[2], tmp[3], ALU.add)

                R2 = MR // 2
                for t, n in enumerate(ROWS):
                    i = t % 2
                    cos, sin = C("cos")[0:n, t * R2:(t + 1) * R2], C("sin")[0:n, t * R2:(t + 1) * R2]
                    statistics(t)
                    dve.wait_ge(a_rs, t + 1)
                    if t >= 2:
                        dve.wait_ge(p_small, t - 1)
                    V.scalar_tensor_tensor(cqn[0:n, i, :], lat[0:n, i, 0:QR], rs[0:n, i, 0:1], qg[0:n, :], ALU.mult, ALU.mult)
                    V.scalar_tensor_tensor(ckvn[0:n, t, :], lat[0:n, i, QR:QR + P], rs[0:n, i, 1:2], kg[0:n, :], ALU.mult, ALU.mult).then_inc(d_n, 1)
                    at = QR + P
                    rotate((kst[0:n, t, MN:MN + R2], kst[0:n, t, MN + R2:QW]), lat[0:n, i, at:at + R2], lat[0:n, i, at + R2:AW],
                           [rt[0:n, k, :] for k in range(4)], cos, sin).then_inc(d_kpe, 1)
                    dve.wait_ge(a_vrs, t + 1)
                    V.tensor_scalar(gv[0:n, i, :], gv[0:n, i, :], vmv[0:n, 0:1], vrs[0:n, :], ALU.subtract, ALU.mult).then_inc(d_vs, 1)
                    dve.wait_ge(a_cqT, t + 1)
                    rotated_keys(t, n).then_inc(d_val, 1)
                    dve.wait_ge(a_q, t + 1)
                    lo, hi = qr[0:n, :, MN:MN + R2], qr[0:n, :, MN + R2:QW]
                    rotate((lo, hi), lo, hi, [qt[0:n, k, :, :] for k in range(4)], cos.unsqueeze(1).to_broadcast([n, MH, R2]),
                           sin.unsqueeze(1).to_broadcast([n, MH, R2])).then_inc(d_rope, 1)
                    dve.wait_ge(p_gate, t + 1)
                    for g in range(4):
                        gs = slice(g * P, (g + 1) * P)
                        ins = V.scalar_tensor_tensor(u[0:n, t, gs], bank[2][0:n, gs], bs[0:n, g:g + 1], u[0:n, t, gs], ALU.add, ALU.mult)
                    ins.then_inc(d_gated, 1)
                dve.wait_ge(p_small, NT + 1)
                V.tensor_copy(ckvT[:, SEQ:SEQ + PAST], bank[3][:, 256:384]).then_inc(d_val, 1)
                rotated_keys(NT, PAST).then_inc(d_val, 1)
                for i, (slot, rows) in enumerate([(t, P) for t in range(4)] + [(4, PAST), (5, DEC)]):
                    dve.wait_ge(p_val, i + 1)
                    V.tensor_copy(val[0:rows, slot, :], bank[4 + i % 4][0:rows, :]).then_inc(d_val, 1)

            @block.gpsimd
            def _(pool):
                G = nc.gpsimd
                pool.wait_ge(small, 128)
                for t, n in enumerate(ROWS):
                    i = t % 2
                    pool.wait_ge(d_vs, t + 1)
                    pool.wait_ge(gch.sem, gch.inc(G.tensor_tensor(gv[0:n, i, :], gv[0:n, i, :], vg[0:n, :], ALU.mult)))
                    G.tensor_tensor(gv[0:n, i, :], gv[0:n, i, :], vb[0:n, :], ALU.add).then_inc(g_vn, 1)
                pool.wait_ge(g_vn, NT)

            @block.tensor
            def _(pe):
                T = nc.tensor
                def project(t, c):
                    n, i = ROWS[t], 3 * t + c
                    if t == 0:
                        pe.wait_ge(w_in[c], 16)
                    if t == 4 and c > 0:
                        return
                    if i >= 2:
                        pe.wait_ge(in_sb, i - 1)
                    if t == 4:
                        for k in range(KT):
                            for g in range(3):
                                mm = T.matmul(bank[0][DEC * g:DEC * (g + 1), 0:FW[g]], xT[:, k, t * P:t * P + n], w[g][:, k, :], start=(k == 0), stop=(k == KT - 1))
                        mm.then_inc(p_in, 3)
                        return
                    for k in range(KT):
                        mm = T.matmul(bank[i % 2][0:n, 0:FW[c]], xT[:, k, t * P:t * P + n], w[c][:, k, :], start=(k == 0), stop=(k == KT - 1))
                    mm.then_inc(p_in, 1)

                def small_transposes(slot, rows, latents):
                    if latents:
                        for k in range(2):
                            T.transpose(bank[3][:, k * P:k * P + rows], cqn[0:rows, slot % 2, k * P:(k + 1) * P], ident[0:rows, 0:rows])
                    T.transpose(bank[3][:, 256:256 + rows], ckvn[0:rows, slot, :], ident[0:rows, 0:rows])
                    T.transpose(bank[3][0:QW, 384:384 + rows], kst[0:rows, slot, :], ident[0:rows, 0:rows]).then_inc(p_small, 1)

                for c in range(3):
                    project(0, c)
                pe.wait_ge(ws_in, 32)
                for g in range(4):
                    mm = T.transpose(bank[7][:, g * P:(g + 1) * P], ws[:, g, :], ident)
                mm.then_inc(p_ws, 1)
                pe.wait_ge(small, 128)
                for t, n in enumerate(ROWS):
                    nxt = t + 1 < NT
                    if nxt:
                        project(t + 1, 0)
                    pe.wait_ge(d_n, t + 1)
                    pe.wait_ge(d_kpe, t + 1)
                    if t >= 1:
                        pe.wait_ge(d_val, t)
                    small_transposes(t, n, True)
                    if nxt:
                        project(t + 1, 1)
                    pe.wait_ge(a_cqT, t + 1)
                    if t >= 1:
                        pe.wait_ge(a_q, t)
                    for h in range(2):
                        for k in range(2):
                            mm = T.matmul(bank[4 + h][0:n, 0:4 * QW], cqT[:, k, 0:n], wuq[:, k, h * 4 * QW:(h + 1) * 4 * QW], start=(k == 0), stop=(k == 1))
                    mm.then_inc(p_uq, 1)
                    if nxt:
                        project(t + 1, 2)
                    pe.wait_ge(g_vn, t + 1)
                    pe.wait_ge(d_ws, 1)
                    if t >= 1:
                        pe.wait_ge(d_gated, t)
                    for g in range(4):
                        mm = T.matmul(bank[2][0:n, g * P:(g + 1) * P], wsT[0:n, g, 0:n], gv[0:n, t % 2, g * P:(g + 1) * P],
                                      start=(g == 0), stop=(g == 3), skip_group_check=True)
                    mm.then_inc(p_gate, 1)
                    pe.wait_ge(d_rope, t + 1)
                    if t >= 1:
                        pe.wait_ge(a_qT, t)
                    for h in range(MH):
                        mm = T.transpose(bank[6 + h // 4][0:QW, (h % 4) * P:(h % 4) * P + n], qr[0:n, h, :], ident[0:n, 0:n])
                    mm.then_inc(p_qT, 1)
                pe.wait_ge(cache_in, 32)
                pe.wait_ge(d_val, NT)
                small_transposes(NT, PAST, False)
                pe.wait_ge(d_val, NT + 1)
                pe.wait_ge(in_sb, 3 * NT)
                for i in range(8):
                    pair, part = i // 2, i % 2
                    keys = slice(0, SEQ) if part == 0 else slice(SEQ, KEYS)
                    if i >= 4:
                        pe.wait_ge(a_k, i - 3)
                    if i == 3:
                        pe.wait_ge(d_val, NT + 2)
                    if i == 2:
                        pe.wait_ge(d_gated, NT)
                    T.matmul(bank[i % 4][:, 0:keys.stop - keys.start], wuk[:, pair * P:(pair + 1) * P], ckvT[:, keys], start=True, stop=True).then_inc(p_k, 1)
                pe.wait_ge(a_qT, NT)
                for i, (at, rows) in enumerate([(0, P), (128, P), (256, P), (384, P), (SEQ, PAST), (SEQ + PAST, DEC)]):
                    if i >= 4:
                        pe.wait_ge(d_val, NT + 2 + i - 3)
                    T.matmul(bank[4 + i % 4][0:rows, :], ckvT[:, at:at + rows], wuv[:], start=True, stop=True).then_inc(p_val, 1)

        with Stage(nc, "m1a_") as ac:
            ab, sem = ac.sb, ac.sem
            wo = ab("wo", [P, KT, DM])
            pr = ab("pr", [P, 2, SEQ])
            pT = ab("pT", [P, 2, 4, P])
            mx = ab("mx", [P, 2])
            nb = ab("nb", [P, 2])
            den = ab("den", [P, 2, MH])
            ao = ab("ao", [P, MH, MV])
            catT = ab("catT", [P, KT, P])
            s = ab("s", [P, DM])
            ln = Norm(nc, ab, sem, "mix")
            wo_in, ln_in, st_out = sem("wo_in"), sem("ln_in"), sem("st_out")
            p_s, d_mx, d_nb, a_p, p_pT, d_pT, p_o, d_o, p_c, a_c, p_y, d_y = (
                sem(x) for x in ("p_s", "d_mx", "d_nb", "a_p", "p_pT", "d_pT", "p_o", "d_o", "p_c", "a_c", "p_y", "d_y"))
            dch = Chain(sem("d_chain"))
            items = [(t, h) for t in range(NT) for h in range(MH)]
            KB = [[(k, k * P, P) for k in range(t + 1)] for t in range(4)] + [[(4, SEQ, PAST), (5, SEQ + PAST, DEC)]]
            WIDTH = [sum(r for _, _, r in b) for b in KB]
            OUT_AT = 2
            block = ac.enter_context(nc.Block(no_gpsimd_drain=True))

            @block.sync
            def _(sp):
                sp.dma_start(wo[:], D["w_out_odd"][0].rearrange("(k p) n -> p k n", p=P)).then_inc(wo_in, 16)
                sp.dma_start(ln.g[:], D["ln_mix_g"][1:2, :].to_broadcast([P, DM])).then_inc(ln_in, 16)
                sp.dma_start(ln.b[:], D["ln_mix_b"][1:2, :].to_broadcast([P, DM])).then_inc(ln_in, 16)
                for t, n in enumerate(ROWS):
                    sp.wait_ge(ln.done, t + 1)
                    sp.dma_start(S.x_rows.rearrange("(t h) c -> t (h c)", h=2)[t * P:t * P + n, :], x_tok[0:n, t, :]).then_inc(st_out, 16)
                sp.wait_ge(st_out, 16 * NT)

            def out_after(i):
                t, h = items[i]
                return t - 1 if t >= 1 and h == OUT_AT else None

            @block.tensor
            def _(pe):
                T = nc.tensor

                def scores(i):
                    t, h = items[i]
                    n, first = ROWS[t], KB[t][0][1]
                    if i >= 3:
                        pe.wait_ge(a_p, i - 2)
                    T.matmul(bank[i % 3][0:n, 0:WIDTH[t]], qT[:, h, t * P:t * P + n], kT[:, h, first:first + WIDTH[t]], start=True, stop=True).then_inc(p_s, 1)

                def turn(i):
                    t, h = items[i]
                    n = ROWS[t]
                    pe.wait_ge(a_p, i + 1)
                    if i >= 2:
                        pe.wait_ge(d_pT, i - 1)
                    for b, (_, at, rows) in enumerate(KB[t]):
                        mm = T.transpose(bank[3 + i % 2][0:rows, b * P:b * P + n], pr[0:n, i % 2, b * P:b * P + rows], ident[0:n, 0:n])
                    mm.then_inc(p_pT, 1)

                def weigh(i):
                    t, h = items[i]
                    n = ROWS[t]
                    pe.wait_ge(d_pT, i + 1)
                    if h == 0 and t >= 1:
                        pe.wait_ge(d_o, t)
                    for b, (slot, _, rows) in enumerate(KB[t]):
                        mm = T.matmul(bank[5][0:n, h * MV:(h + 1) * MV], pT[0:rows, i % 2, b, 0:n], val[0:rows, slot, h * MV:(h + 1) * MV],
                                      start=(h == 0 and b == 0), stop=(h == MH - 1 and b == len(KB[t]) - 1), skip_group_check=True)
                    mm.then_inc(p_o, 1)

                def output(t):
                    n = ROWS[t]
                    pe.wait_ge(d_o, t + 1)
                    if t >= 1:
                        pe.wait_ge(d_y, t)
                    else:
                        pe.wait_ge(wo_in, 16)
                    for k in range(KT):
                        src = ao[0:n, 2 * k:2 * k + 2, :].rearrange("p h d -> p (h d)") if k < 4 else u[0:n, t, (k - 4) * P:(k - 3) * P]
                        mm = T.transpose(bank[6 + k // 4][:, (k % 4) * P:(k % 4) * P + n], src, ident[0:n, 0:n])
                    mm.then_inc(p_c, 1)
                    pe.wait_ge(a_c, t + 1)
                    mm = out_products(T, bank[6], bank[7], t, catT, wo)
                    mm.then_inc(p_y, 1)

                scores(0)
                for i in range(len(items)):
                    if i + 1 < len(items):
                        scores(i + 1)
                    if i >= 1:
                        weigh(i - 1)
                    turn(i)
                    if out_after(i) is not None:
                        output(out_after(i))
                weigh(len(items) - 1)
                output(NT - 1)

            @block.scalar
            def _(act):
                A = nc.scalar

                def output(t):
                    n = ROWS[t]
                    act.wait_ge(p_c, t + 1)
                    if t >= 1:
                        act.wait_ge(p_y, t)
                    for h in range(2):
                        ins = A.activation(catT[:, 4 * h:4 * h + 4, 0:n], bank[6 + h][:].rearrange("p (k n) -> p k n", k=4)[:, :, 0:n], ACT.Copy)
                    ins.then_inc(a_c, 1)
                    ln.scalar(act, t, n)

                for i, (t, h) in enumerate(items):
                    n = ROWS[t]
                    act.wait_ge(d_nb, i + 1)
                    if i >= 2:
                        act.wait_ge(p_pT, i - 1)
                    if h == 0 and t >= 2:
                        act.wait_ge(d_o, t - 1)
                    A.activation(pr[0:n, i % 2, 0:WIDTH[t]], bank[i % 3][0:n, 0:WIDTH[t]], ACT.Exp, bias=nb[0:n, i % 2:i % 2 + 1], scale=SCALE,
                                 accum_out=den[0:n, t % 2, h:h + 1]).then_inc(a_p, 1)
                    if out_after(i) is not None:
                        output(out_after(i))
                output(NT - 1)

            @block.vector
            def _(dve):
                V = nc.vector

                def link(ins):
                    dve.wait_ge(dch.sem, dch.inc(ins))

                def maximum(i):
                    t, h = items[i]
                    n, j = ROWS[t], i % 2
                    dve.wait_ge(p_s, i + 1)
                    if t < 4:
                        link(V.memset(bank[i % 3][0:64, WIDTH[t] - 64:WIDTH[t]], -BIG))
                    if i >= 2:
                        dve.wait_ge(a_p, i - 1)
                    link(V.reduce_max(mx[0:n, j:j + 1], bank[i % 3][0:n, 0:WIDTH[t]], AX.X))
                    V.tensor_scalar(nb[0:n, j:j + 1], mx[0:n, j:j + 1], -SCALE, None, ALU.mult).then_inc(d_nb, 1)

                def turned(i):
                    t, h = items[i]
                    n = ROWS[t]
                    dve.wait_ge(p_pT, i + 1)
                    if i >= 2:
                        dve.wait_ge(p_o, i - 1)
                    if t < 4:
                        V.tensor_copy(pT[:, i % 2, 0:t + 1, 0:n], bank[3 + i % 2][:].rearrange("p (b n) -> p b n", b=4)[:, 0:t + 1, 0:n]).then_inc(d_pT, 1)
                    else:
                        V.tensor_copy(pT[:, i % 2, 0, 0:n], bank[3 + i % 2][:, 0:n])
                        V.tensor_copy(pT[0:DEC, i % 2, 1, 0:n], bank[3 + i % 2][0:DEC, P:P + n]).then_inc(d_pT, 1)

                def heads(t):
                    n = ROWS[t]
                    dve.wait_ge(p_o, MH * (t + 1))
                    if t >= 1:
                        dve.wait_ge(p_c, t)
                    link(V.reciprocal(den[0:n, t % 2, :], den[0:n, t % 2, :]))
                    V.tensor_tensor(ao[0:n, :, :], bank[5][0:n, :].rearrange("p (h d) -> p h d", h=MH),
                                    den[0:n, t % 2, :].unsqueeze(2).to_broadcast([n, MH, MV]), ALU.mult).then_inc(d_o, 1)

                def output(t):
                    n = ROWS[t]
                    dve.wait_ge(p_y, t + 1)
                    if t >= 1:
                        dve.wait_ge(ln.done, t)
                    link(residual(V, bank[6], bank[7], t, x_tok, s))
                    dve.sem_inc(d_y, 1)
                    ln.vector(dve, t, n, s, x_tok[:, t, :])

                dve.wait_ge(ln_in, 32)
                maximum(0)
                for i in range(len(items)):
                    t, h = items[i]
                    if i + 1 < len(items):
                        maximum(i + 1)
                    if h == 1 and t >= 1:
                        heads(t - 1)
                    turned(i)
                    if out_after(i) is not None:
                        output(out_after(i))
                heads(NT - 1)
                output(NT - 1)

            @block.gpsimd
            def _(pool):
                pool.wait_ge(ln_in, 32)
                for t, n in enumerate(ROWS):
                    ln.pool(pool, t, n, s, x_tok[:, t, :])
                pool.wait_ge(ln.done, NT)


def moe(nc, S, layer):
    bank, x_tok, ident, gates = S.bank, S.x_tok, S.ident("ident"), S.gates
    L = f"l{layer}_"
    with Stage(nc, L) as ctx:
        sb = ctx.sb
        w13 = sb("w13", [P, 2 + len(EXTRA), 2, 2, 4, DE])
        w2s = sb("w2s", [P, 2 + len(EXTRA), 2, DM])
        meta = sb("meta", [1, 64], I32)
        gidx = sb("gidx", [P, MAXB + 2], I32)
        sidx = sb("sidx", [P, MAXB + 2], I32)
        w13_in = [ctx.sem(f"w13_in{j}") for j in range(2 + len(EXTRA))]
        w2_in = [ctx.sem(f"w2_in{j}") for j in range(2 + len(EXTRA))]
        w1d, w3d, w2d = S.d["expert_w1"], S.d["expert_w3"], S.d["expert_w2"]
        place, turn, loads = {}, {}, [0, 0]
        for m in range(PEELED):
            place[m] = 2 + EXTRA.index(m) if m in EXTRA else sum(loads) % 2
            turn[m] = 1
            if m not in EXTRA:
                loads[place[m]] += 1
                turn[m] = loads[place[m]]
        RINGED = PEELED // 2 - loads[0]

        def load13(sp, e, j):
            for i, w in enumerate((w1d, w3d)):
                sp.dma_start(w13[:, j, i, :, :, :], w[layer, bass.ds(e, 1), :, :].rearrange("e (h p k) n -> p (e h) k n", h=2, k=4)).then_inc(w13_in[j], 16)

        def load2(sp, e, j):
            sp.dma_start(w2s[:, j, :, :], w2d[layer, bass.ds(e, 1), :, :].rearrange("e (p f) n -> p (e f) n", f=2)).then_inc(w2_in[j], 16)

        with Stage(nc, L) as rc:
            rb, rs = rc.sb, rc.sem
            C = Constants(nc, rc, S, "route", L + "const")
            xT = rb("r_xT", [P, KT, TOK])
            wr = rb("r_w", [P, KT, NG + NE])
            bias = rb("r_b", [P, NG + NE])
            lT = rb("r_lT", [NG + NE, TOK])
            lg = rb("r_lg", [P, NT, NG + NE])
            g8 = rb("r_g8", [P, NT, 8])
            gm = rb("r_gm", [P, NT, 8])
            gi = rb("r_gi", [P, NT, 8], U32)
            gsel = rb("r_gsel", [P, NT])
            pen = rb("r_pen", [P, NT, NG])
            em = rb("r_em", [P, NT, NE])
            ev = rb("r_ev", [P, NT, 8])
            ei = rb("r_ei", [P, NT, 8], U32)
            esel = rb("r_esel", [P, NT, 2])
            ge = rb("r_ge", [P, NT, NG])
            gp = rb("r_gp", [P, NT])
            dv = rb("r_dv", [P, NT])
            ed = rb("r_ed", [P, NT])
            rden = rb("r_rden", [P, NT])
            oh = rb("r_oh", [P, NT, 2, NE])
            A = rb("r_A", [P, NT, NE])
            pre = rb("r_pre", [P, NT + 1, NE])
            rank = rb("r_rank", [P, NT * NE], I32)
            fl = rb("r_fl", [P, NT * NE], I32)
            po = rb("r_po", [P, NT * NE], I32)
            blk = rb("r_blk", [P, NT, NE])
            pos = rb("r_pos", [P, NT, NE])
            prod = rb("r_prod", [P, NT, 2, NE])
            later = prod[:, :, 0, :]
            bsel = rb("r_bsel", [P, 2 * NT])
            psel = rb("r_psel", [P, 2 * NT])
            free = xT[:].rearrange("p k n -> p (k n)")
            widths = [2 * NT * P, 2 * NT * MAXB, 2 * NT * MAXB]
            ohp, ohb, val = (free[:, sum(widths[:i]):sum(widths[:i + 1])].rearrange("p (i n) -> p i n", i=2 * NT) for i in range(3))
            cnt = rb("r_cnt", [NE, 1])
            cmp9 = rb("r_cmp9", [NE, 9])
            nblk = rb("r_nblk", [NE, 1])
            nblkb = rb("r_nblkb", [NE, P])
            bend = rb("r_bend", [NE, 1])
            cmpb = rb("r_cmpb", [NE, OVER])
            base = rb("r_base", [P, NE])
            row = rb("r_row", [1, 64])
            tmp1 = rb("r_tmp1", [1, 64])
            nb1 = rb("r_nb1", [1, 1])
            vf = rb("r_vf", [P, MAXB])
            pad = rb("r_pad", [P, MAXB])
            vi = rb("r_vi", [P, MAXB], I32)
            gf = rb("r_gf", [P, MAXB])
            w_in, p_tr, a_xT = rs("w_in"), rs("p_tr"), rs("a_xT")
            p_log, d_lT, p_lg, d_ready, p_ready = rs("p_log"), rs("d_lT"), rs("p_lg"), rs("d_ready"), rs("p_ready")
            a_ready, dch = rs("a_ready"), Chain(rs("d_chain"))
            block = rc.enter_context(nc.Block(no_gpsimd_drain=True))

            @block.sync
            def _(sp):
                sp.dma_start(C.tile[:], C.source).then_inc(w_in, 16)
                sp.dma_start(wr[:, :, 0:NG], S.d["router_group_w"][layer].rearrange("(k p) n -> p k n", p=P)).then_inc(w_in, 16)
                sp.dma_start(wr[:, :, NG:], S.d["router_expert_w"][layer].rearrange("(k p) n -> p k n", p=P)).then_inc(w_in, 16)
                sp.dma_start(bias[:, 0:NG], S.d["router_group_b"][layer:layer + 1, :].to_broadcast([P, NG])).then_inc(w_in, 16)
                sp.dma_start(bias[:, NG:], S.d["router_expert_b"][layer:layer + 1, :].to_broadcast([P, NE])).then_inc(w_in, 16)
                for m in range(PEELED):
                    if turn[m] == 1:
                        load13(sp, m, place[m])
                        load2(sp, m, place[m])

            @block.tensor
            def _(pe):
                for t, n in enumerate(ROWS):
                    for h in range(2):
                        i = 2 * t + h
                        if i >= 4:
                            pe.wait_ge(a_xT, i - 3)
                        for q in range(4):
                            k = 4 * h + q
                            mm = nc.tensor.transpose(bank[i % 4][:, q * P:q * P + n], x_tok[0:n, t, k * P:(k + 1) * P], ident[0:n, 0:n])
                        mm.then_inc(p_tr, 1)
                pe.wait_ge(a_xT, 2 * NT)
                pe.wait_ge(w_in, 80)
                for h in range(2):
                    for k in range(KT):
                        mm = nc.tensor.matmul(bank[4 + h][0:NG + NE, 0:TOK // 2], wr[:, k, :], xT[:, k, h * (TOK // 2):(h + 1) * (TOK // 2)],
                                              start=(k == 0), stop=(k == KT - 1))
                    mm.then_inc(p_log, 1)
                pe.wait_ge(d_lT, 2)
                for t, n in enumerate(ROWS):
                    mm = nc.tensor.transpose(bank[6][0:n, t * 36:(t + 1) * 36], lT[:, t * P:t * P + n], ident[0:36, 0:36])
                mm.then_inc(p_lg, 1)
                pe.wait_ge(d_ready, 1)
                nc.tensor.matmul(bank[0][:, 0:NT * NE], C("tri_strict"), A[:].rearrange("p t e -> p (t e)"), start=True, stop=False)
                mm = nc.tensor.matmul(bank[0][:, 0:NT * NE], C("ones"), pre[:, 0:NT, :].rearrange("p t e -> p (t e)"), start=False, stop=True)
                mm = nc.tensor.matmul(bank[1][0:NE, 0:1], pre[:, NT, :], C("ones")[:, 0:1], start=True, stop=True)
                mm.then_inc(p_ready, 1)
                pe.wait_ge(d_ready, 2)
                nc.tensor.matmul(bank[2][:, 0:NE], nblkb[:], C("tri_strict")[0:NE, 0:NE], start=True, stop=True)
                nc.tensor.matmul(bank[3][0:NE, 0:1], C("tri_incl")[0:NE, 0:NE], nblk[:], start=True, stop=True).then_inc(p_ready, 1)
                pe.wait_ge(d_ready, 3)
                nc.tensor.matmul(bank[4][0:1, 0:OVER], C("ones")[0:NE, 0:1], cmpb[:], start=True, stop=True).then_inc(p_ready, 1)
                pe.wait_ge(d_ready, 4)
                for i in range(2 * NT):
                    mm = nc.tensor.matmul(bank[5][:, 0:MAXB], ohp[:, i, :], val[:, i, :], start=(i == 0), stop=(i == 2 * NT - 1))
                mm.then_inc(p_ready, 1)

            @block.scalar
            def _(act):
                for i in range(2 * NT):
                    t, h = i // 2, i % 2
                    n = ROWS[t]
                    act.wait_ge(p_tr, i + 1)
                    nc.scalar.activation(xT[:, 4 * h:4 * h + 4, t * P:t * P + n],
                                         bank[i % 4][:].rearrange("p (k n) -> p k n", k=4)[:, :, 0:n], ACT.Copy).then_inc(a_xT, 1)
                act.wait_ge(a_ready, 1)
                nc.scalar.activation(ge[:], ge[:], ACT.Exp).then_inc(p_lg, 1)
                nc.scalar.activation(ed[:], dv[:], ACT.Exp).then_inc(p_lg, 1)

            @block.vector
            def _(dve):
                V = nc.vector

                def link(ins):
                    dve.wait_ge(dch.sem, dch.inc(ins))

                for h in range(2):
                    dve.wait_ge(p_log, h + 1)
                    V.tensor_copy(lT[:, h * (TOK // 2):(h + 1) * (TOK // 2)], bank[4 + h][0:36, 0:TOK // 2]).then_inc(d_lT, 1)
                link(V.memset(g8[:], -BIG))
                link(V.memset(lg[:], 0.0))
                dve.wait_ge(p_lg, 1)
                dve.wait_ge(w_in, 80)
                V.tensor_tensor(lg[:, 0:4, :], bank[6][:, 0:144].rearrange("p (t n) -> p t n", t=4),
                                bias[:].unsqueeze(1).to_broadcast([P, 4, 36]), ALU.add)
                link(V.tensor_tensor(lg[0:DEC, 4, :], bank[6][0:DEC, 144:180], bias[0:DEC, :], ALU.add))
                link(V.tensor_copy(g8[:, :, 0:NG], lg[:, :, 0:NG]))
                for t in range(NT):
                    ins = V.max(gm[:, t, :], g8[:, t, :])
                link(ins)
                for t in range(NT):
                    ins = V.max_index(gi[:, t, :], gm[:, t, :], g8[:, t, :])
                link(ins)
                link(V.tensor_copy(gsel[:], gi[:, :, 0]))
                link(V.tensor_tensor(pen[:], C("iota")[:, 0:NG].unsqueeze(1).to_broadcast([P, NT, NG]),
                                     gsel[:].unsqueeze(2).to_broadcast([P, NT, NG]), ALU.is_equal))
                link(V.tensor_scalar(pen[:], pen[:], BIG, -BIG, ALU.mult, ALU.add))
                for t in range(NT):
                    ins = V.tensor_tensor(em[:, t, :].rearrange("p (g e) -> p g e", g=NG), lg[:, t, NG:].rearrange("p (g e) -> p g e", g=NG),
                                          pen[:, t, :].unsqueeze(2).to_broadcast([P, NG, EPG]), ALU.add)
                link(ins)
                for t in range(NT):
                    ins = V.max(ev[:, t, :], em[:, t, :])
                link(ins)
                for t in range(NT):
                    ins = V.max_index(ei[:, t, :], ev[:, t, :], em[:, t, :])
                link(ins)
                V.tensor_tensor(ge[:], g8[:, :, 0:NG], gm[:, :, 0:1].to_broadcast([P, NT, NG]), ALU.subtract)
                link(V.tensor_tensor(dv[:], ev[:, :, 1], ev[:, :, 0], ALU.subtract))
                link(V.tensor_copy(esel[:], ei[:, :, 0:2]))
                dve.sem_inc(a_ready, 1)
                for k in range(2):
                    ins = V.tensor_tensor(oh[:, :, k, :], C("iota")[:, 0:NE].unsqueeze(1).to_broadcast([P, NT, NE]),
                                          esel[:, :, k:k + 1].to_broadcast([P, NT, NE]), ALU.is_equal)
                link(ins)
                for k in range(2):
                    ins = V.tensor_tensor(oh[:, :, k, :], oh[:, :, k, :], C("valid").unsqueeze(2).to_broadcast([P, NT, NE]), ALU.mult)
                link(ins)
                link(V.tensor_tensor(A[:], oh[:, :, 0, :], oh[:, :, 1, :], ALU.add))
                link(V.memset(pre[:, 0, :], 0.0))
                for t in range(NT):
                    link(V.tensor_tensor(pre[:, t + 1, :], pre[:, t, :], A[:, t, :], ALU.add))
                dve.sem_inc(d_ready, 1)
                dve.wait_ge(p_lg, 3)
                V.tensor_scalar(rden[:], ed[:], 1.0, None, ALU.add)
                link(V.reduce_sum(gp[:], ge[:], AX.X))
                link(V.tensor_tensor(rden[:], rden[:], gp[:], ALU.mult))
                link(V.reciprocal(gates[:, :, 0], rden[:]))
                link(V.tensor_tensor(gates[:, :, 1], gates[:, :, 0], ed[:], ALU.mult))
                dve.wait_ge(p_ready, 1)
                link(V.tensor_copy(cnt[:], bank[1][0:NE, 0:1]))
                link(V.tensor_scalar(cmp9[:], C("fills")[0:NE, :], cnt[:], None, ALU.is_lt))
                link(V.reduce_sum(nblk[:], cmp9[:, 1:9], AX.X))
                V.tensor_copy(nblkb[:], nblk[:].to_broadcast([NE, P])).then_inc(d_ready, 1)
                link(V.tensor_copy(rank[:], bank[0][:, 0:NT * NE]))
                V.tensor_scalar(fl[:], rank[:], 6, None, ALU.arith_shift_right)
                link(V.tensor_scalar(po[:], rank[:], SLOTS - 1, None, ALU.bitwise_and))
                dve.wait_ge(p_ready, 2)
                link(V.tensor_copy(bend[:], bank[3][0:NE, 0:1]))
                V.tensor_scalar(cmpb[:], C("iota")[0:NE, 0:OVER], bend[:], None, ALU.is_ge).then_inc(d_ready, 1)
                V.tensor_copy(pos[:].rearrange("p t e -> p (t e)"), po[:])
                link(V.tensor_copy(blk[:].rearrange("p t e -> p (t e)"), fl[:]))
                link(V.scalar_tensor_tensor(base[:], C("iota")[:, 0:NE], -1.0, bank[2][:, 0:NE], ALU.mult, ALU.add))
                link(V.scalar_tensor_tensor(later, blk[:], float(NE - 1), base[:].unsqueeze(1).to_broadcast([P, NT, NE]), ALU.add, ALU.add))
                link(V.scalar_tensor_tensor(blk[:], blk[:], 1.0, later, ALU.is_ge, ALU.mult))
                link(V.tensor_tensor(blk[:], blk[:], C("iota")[:, 0:NE].unsqueeze(1).to_broadcast([P, NT, NE]), ALU.add))
                for src, dst in ((blk, bsel), (pos, psel)):
                    for k in range(2):
                        ins = V.tensor_tensor(prod[:, :, k, :], oh[:, :, k, :], src[:], ALU.mult)
                    link(ins)
                    link(V.reduce_sum(dst[:].rearrange("p (t k) -> p t k", k=2), prod[:], AX.X))
                V.tensor_tensor(ohp, C("iota_slot").unsqueeze(1).to_broadcast([P, 2 * NT, P]),
                                psel[:].unsqueeze(2).to_broadcast([P, 2 * NT, P]), ALU.is_equal)
                link(V.tensor_tensor(ohb, C("iota")[:, 0:MAXB].unsqueeze(1).to_broadcast([P, 2 * NT, MAXB]),
                                     bsel[:].unsqueeze(2).to_broadcast([P, 2 * NT, MAXB]), ALU.is_equal))
                V.tensor_tensor(val, ohb, C("assignment").unsqueeze(2).to_broadcast([P, 2 * NT, MAXB]), ALU.mult).then_inc(d_ready, 1)
                dve.wait_ge(p_ready, 3)
                link(V.tensor_copy(row[:, 0:OVER], bank[4][0:1, 0:OVER]))
                link(V.tensor_scalar(tmp1[:, 0:OVER], row[:, 0:OVER], float(NE), None, ALU.is_lt))
                link(V.reduce_sum(nb1[:], tmp1[:, 0:OVER], AX.X))
                link(V.tensor_scalar(tmp1[:, 0:OVER // 2], C("pairs")[0:1, :], nb1[:], None, ALU.is_lt))
                link(V.reduce_sum(nb1[:], tmp1[:, 0:OVER // 2], AX.X))
                V.tensor_scalar(meta[:, MAXB:MAXB + 1], nb1[:], 2.0, float(NE - 4), ALU.mult, ALU.add)
                V.tensor_copy(meta[:, 0:NE], C("iota")[0:1, 0:NE])
                link(V.tensor_scalar(meta[:, NE:MAXB], row[:, 0:OVER], float(NE - 1), None, ALU.min))
                dve.wait_ge(p_ready, 4)
                V.tensor_scalar(vf[:], bank[5][:, 0:MAXB], -1.0, None, ALU.add)
                link(V.tensor_scalar(pad[:], bank[5][:, 0:MAXB], 0.5, 131072.0, ALU.is_lt, ALU.mult))
                link(V.tensor_tensor(vf[:], vf[:], pad[:], ALU.add))
                link(V.tensor_copy(vi[:], vf[:]))
                link(V.tensor_scalar(vi[:], vi[:], -2, None, ALU.bitwise_and))
                link(V.tensor_copy(gf[:], vi[:]))
                V.tensor_scalar(gidx[:, 0:MAXB], gf[:], C("half"), None, ALU.add)
                link(V.tensor_scalar(vf[:], vf[:], 2.0, None, ALU.mult))
                link(V.tensor_scalar(sidx[:, 0:MAXB], vf[:], C("half"), None, ALU.add))

        with Stage(nc, L) as ec:
            eb, es = ec.sb, ec.sem
            xg = eb("e_xg", [P, 2, HALF])
            xTs = eb("e_xT", [P, 2, 4, P])
            up = eb("e_up", [SLOTS, 2, 512])
            hsum = eb("e_hsum", [SLOTS, 2, 512])
            sil = eb("e_sil", [SLOTS, 2, DE])
            hid = eb("e_hid", [SLOTS, 2, DE])
            hidT = eb("e_hidT", [P, 2, 2, SLOTS])
            ysb = eb("e_y", [P, 2, HALF])
            gcur = eb("e_gcur", [P, 2], I32)
            scur = eb("e_scur", [P, 2], I32)
            xg_in = [es(f"xg_in{j}") for j in range(2)]
            y_out = [es(f"y_out{j}") for j in range(2)]
            xT_ps, xT_sb, h_ps, h_up, h_sum = es("xT_ps"), es("xT_sb"), es("h_ps"), es("h_up"), es("h_sum")
            h_sil, hid_sb, hT_ps, hT_sb, y_ps, y_sb = es("h_sil"), es("hid_sb"), es("hT_ps"), es("hT_sb"), es("y_ps"), es("y_sb")
            xg_zero, going, g_cp, s_cp = es("xg_zero"), es("going"), es("g_cp"), es("s_cp")
            block = ec.enter_context(nc.Block(no_gpsimd_drain=True))

            @block.sync
            def _(sp):
                last = {j: j for j in range(2)}
                for m in range(PEELED):
                    if turn[m] > 1:
                        j = place[m]
                        sp.wait_ge(h_ps, last[j] + 1)
                        load13(sp, m, j)
                        sp.wait_ge(y_ps, last[j] + 1)
                        load2(sp, m, j)
                    if m not in EXTRA:
                        last[place[m]] = m

                def next_load(b, j, done):
                    sp.wait_ge(h_ps, done)
                    e = sp.value_load(meta[0:1, bass.ds(b + j, 1)], min_val=0, max_val=NE - 1)
                    load13(sp, e, j)
                    sp.wait_ge(y_ps, done)
                    load2(sp, e, j)

                for j in range(2):
                    next_load(PEELED, j, last[j] + 1)
                tail = sp.value_load(meta[0:1, MAXB:MAXB + 1], min_val=NE - 4, max_val=MAXB - 4)
                with sp.Fori(PEELED + 2, tail + 4, 2) as b:
                    for j in range(2):
                        next_load(b, j, b + j - 1)

            @block.gpsimd
            def _(pool):
                tail = pool.value_load(meta[0:1, MAXB:MAXB + 1], min_val=NE - 4, max_val=MAXB - 4)
                nc.gpsimd.memset(xg[:], 0.0).then_inc(xg_zero, 1)
                pool.wait_ge(xg_zero, 1)
                nc.gpsimd.memset(gcur[:], 0).then_inc(xT_ps, 2)

                gather_bound, scatter_bound = pool.to_reg(2 * TOK - 1), pool.to_reg(4 * TOK - 1)

                def gather(b, j):
                    m = b + j
                    pool.wait_ge(xT_ps, m + 1)
                    nc.gpsimd.tensor_copy(gcur[:, j:j + 1], gidx[:, bass.ds(m, 1)]).then_inc(g_cp, 1)
                    pool.wait_ge(g_cp, m + 1)
                    pool.sem_inc(going, 1)
                    nc.gpsimd.indirect_dma_start(
                        out=xg[:, j, :], out_offset=None, in_=S.x_rows,
                        in_offset=bass.IndirectOffsetOnAxis(ap=gcur[:, j:j + 1].bitcast(U32), axis=0),
                        bounds_check=gather_bound, oob_is_err=False).then_inc(xg_in[j], 16)

                def scatter(b, j, first=False):
                    m = b + j
                    if not first:
                        pool.wait_ge(y_out[j], b * 8)
                    nc.gpsimd.tensor_copy(scur[:, j:j + 1], sidx[:, bass.ds(m, 1)]).then_inc(s_cp, 1)
                    pool.wait_ge(s_cp, m + 1)
                    pool.wait_ge(y_sb, m + 3)
                    pool.sem_inc(going, 1)
                    nc.gpsimd.indirect_dma_start(
                        out=S.y_rows, out_offset=bass.IndirectOffsetOnAxis(ap=scur[:, j:j + 1].bitcast(U32), axis=0),
                        in_=ysb[:, j, :], in_offset=None,
                        bounds_check=scatter_bound, oob_is_err=False).then_inc(y_out[j], 16)

                gather(0, 0)
                gather(0, 1)
                gather(2, 0)
                gather(2, 1)
                scatter(0, 0, first=True)
                gather(4, 0)
                scatter(0, 1, first=True)
                with pool.Fori(2, tail, 2) as b:
                    gather(b + 2, 1)
                    scatter(b, 0)
                    gather(b + 4, 0)
                    scatter(b, 1)
                gather(tail + 2, 1)
                scatter(tail, 0)
                scatter(tail, 1)
                for j in range(2):
                    scatter(tail + 2, j)
                for j in range(2):
                    pool.wait_ge(y_out[j], tail * 8 + 32)

            @block.tensor
            def _(pe):
                tail = pe.value_load(meta[0:1, MAXB:MAXB + 1], min_val=NE - 4, max_val=MAXB - 4)

                def x_transposes(b, j):
                    pe.wait_ge(xg_in[j], b * 8 + 16)
                    for q in range(4):
                        mm = nc.tensor.transpose(bank[j][:, q * P:(q + 1) * P], xg[:, j, q:HALF:4], ident)
                    mm.then_inc(xT_ps, 1)

                def up_products(b, j):
                    m = b + j
                    at, loads = (place[m], 32 * turn[m]) if isinstance(b, int) and b < PEELED else (j, b * 16 + 32 - 32 * RINGED)
                    pe.wait_ge(w13_in[at], loads)
                    pe.wait_ge(xT_sb, m + 1)
                    pe.wait_ge(h_sum, m + 1)
                    for q in range(4):
                        for h in range(2):
                            mm = nc.tensor.matmul(bank[2 + j][SLOTS * h:SLOTS * (h + 1), :], xTs[:, j, q, SLOTS * h:SLOTS * (h + 1)],
                                                  w13[:, at, :, h, q, :], start=(q == 0), stop=(q == 3))
                    mm.then_inc(h_ps, 1)

                def hid_ready(b, j):
                    pe.wait_ge(hid_sb, b + j + 1)

                def hid_transposes(j):
                    for f in range(2):
                        mm = nc.tensor.transpose(bank[4 + j][:, f * SLOTS:(f + 1) * SLOTS], hid[:, j, f:DE:2], ident[0:SLOTS, 0:SLOTS])
                    mm.then_inc(hT_ps, 1)

                def down_products(b, j):
                    at, loads = (place[b + j], 16 * turn[b + j]) if isinstance(b, int) and b < PEELED else (j, b * 8 + 16 - 16 * RINGED)
                    pe.wait_ge(w2_in[at], loads)
                    pe.wait_ge(hT_sb, b + j + 1)
                    pe.wait_ge(y_sb, b + j + 1)
                    for f in range(2):
                        for h in range(2):
                            mm = nc.tensor.matmul(bank[6 + j][SLOTS * h:SLOTS * (h + 1), :], hidT[:, j, f, :],
                                                  w2s[:, at, f, h * HALF:(h + 1) * HALF], start=(f == 0), stop=(f == 1))
                    mm.then_inc(y_ps, 1)

                x_transposes(0, 0)
                x_transposes(0, 1)
                up_products(0, 0)
                def pair(b):
                    up_products(b, 1)
                    hid_ready(b, 0)
                    x_transposes(b + 2, 0)
                    hid_transposes(0)
                    down_products(b, 0)
                    up_products(b + 2, 0)
                    hid_ready(b, 1)
                    x_transposes(b + 2, 1)
                    hid_transposes(1)
                    down_products(b, 1)

                for b in range(0, PEELED, 2):
                    pair(b)
                with pe.Fori(PEELED, tail + 2, 2) as b:
                    pair(b)
                hid_ready(tail + 2, 0)
                up_products(tail + 2, 1)
                hid_transposes(0)
                hid_ready(tail + 2, 1)
                down_products(tail + 2, 0)
                hid_transposes(1)
                down_products(tail + 2, 1)

            @block.scalar
            def _(act):
                tail = act.value_load(meta[0:1, MAXB:MAXB + 1], min_val=NE - 4, max_val=MAXB - 4)

                def x_copy(b, j):
                    act.wait_ge(xT_ps, b + j + 3)
                    nc.scalar.activation(xTs[:, j, :, :].rearrange("p k n -> p (k n)"), bank[j][:], ACT.Copy).then_inc(xT_sb, 1)

                def hidden(b, j):
                    m = b + j
                    act.wait_ge(h_ps, m + 1)
                    nc.scalar.activation(up[:, j, :], bank[2 + j][SLOTS:P, :], ACT.Copy).then_inc(h_up, 1)
                    act.wait_ge(h_sum, m + 3)
                    nc.scalar.activation(sil[:, j, :], hsum[:, j, 0:DE], ACT.Silu).then_inc(h_sil, 1)

                x_copy(0, 0)
                x_copy(0, 1)
                hidden(0, 0)
                with act.Fori(0, tail + 2, 2) as b:
                    hidden(b, 1)
                    x_copy(b + 2, 0)
                    hidden(b + 2, 0)
                    x_copy(b + 2, 1)
                hidden(tail + 2, 1)

            @block.vector
            def _(dve):
                tail = dve.value_load(meta[0:1, MAXB:MAXB + 1], min_val=NE - 4, max_val=MAXB - 4)
                nc.vector.memset(hsum[:, 0, 0:1], 0.0).then_inc(h_sum, 2)
                nc.vector.memset(ysb[:, 0, 0:1], 0.0).then_inc(y_sb, 2)
                dve.wait_ge(h_sum, 2)
                dve.wait_ge(y_sb, 2)

                def hidden(b, j):
                    m = b + j
                    dve.wait_ge(h_up, m + 1)
                    nc.vector.tensor_tensor(hsum[:, j, :], bank[2 + j][0:SLOTS, :], up[:, j, :], ALU.add).then_inc(h_sum, 1)
                    dve.wait_ge(h_sil, m + 1)
                    nc.vector.tensor_tensor(hid[:, j, :], sil[:, j, :], hsum[:, j, DE:2 * DE], ALU.mult).then_inc(hid_sb, 1)

                def hid_copy(b, j):
                    dve.wait_ge(hT_ps, b + j + 1)
                    nc.vector.tensor_copy(hidT[:, j, :, :].rearrange("p f n -> p (f n)"), bank[4 + j][:, 0:P]).then_inc(hT_sb, 1)

                def y_copy(b, j, first=False):
                    dve.wait_ge(y_ps, b + j + 1)
                    if not first:
                        dve.wait_ge(y_out[j], b * 8)
                    nc.vector.tensor_copy(ysb[:, j, :], bank[6 + j][:]).then_inc(y_sb, 1)

                def pair(b, first=False):
                    hid_copy(b, 0)
                    hidden(b, 1)
                    y_copy(b, 0, first)
                    hid_copy(b, 1)
                    hidden(b + 2, 0)
                    y_copy(b, 1, first)

                hidden(0, 0)
                pair(0, first=True)
                with dve.Fori(2, tail + 2, 2) as b:
                    pair(b)
                hid_copy(tail + 2, 0)
                hidden(tail + 2, 1)
                y_copy(tail + 2, 0)
                hid_copy(tail + 2, 1)
                y_copy(tail + 2, 1)


def combine(nc, S, layer, turned=None):
    bank, x_tok, ident, gates = S.bank, S.x_tok, S.ident("ident"), S.gates
    with Stage(nc, f"c{layer}_") as cc:
        cb, cs = cc.sb, cc.sem
        yin = cb("y", [P, 3, 2, DM])
        s = cb("s", [P, 2, DM])
        ln = Norm(nc, cb, cs, "ffn")
        y_in = [cs(f"y_in{j}") for j in range(3)]
        ln_w, summed, first, p_xT, a_xT = cs("ln_w"), cs("summed"), cs("first"), cs("p_xT"), cs("a_xT")
        block = cc.enter_context(nc.Block(no_gpsimd_drain=True))

        @block.sync
        def _(sp):
            for t, n in enumerate(ROWS):
                if t >= 3:
                    sp.wait_ge(summed, t - 2)
                sp.dma_start(yin[0:n, t % 3, :, :], S.y_pairs[t * P:t * P + n, :, :]).then_inc(y_in[t % 3], 16)
                if t == 0:
                    sp.dma_start(ln.g[:], S.d["ln_ffn_g"][layer:layer + 1, :].to_broadcast([P, DM])).then_inc(ln_w, 16)
                    sp.dma_start(ln.b[:], S.d["ln_ffn_b"][layer:layer + 1, :].to_broadcast([P, DM])).then_inc(ln_w, 16)
            if turned:
                turned[1](sp)
            if layer == DEPTH - 1:
                for t, n in enumerate(ROWS):
                    sp.wait_ge(ln.done, t + 1)
                    dst = S.o["y_prompt"][0, t * P:t * P + n, :] if t < 4 else S.o["y_sample"][0, :, :]
                    sp.dma_start(dst, x_tok[0:n, t, :]).then_inc(S.out_done, 16)

        @block.scalar
        def _(act):
            A = nc.scalar

            def weigh(t):
                n = ROWS[t]
                act.wait_ge(y_in[t % 3], 16 * (t // 3 + 1))
                if t >= 2:
                    act.wait_ge(ln.done, t - 1)
                A.activation(s[0:n, t % 2, :], yin[0:n, t % 3, 0, :], ACT.Copy, scale=gates[0:n, t, 0:1]).then_inc(first, 1)

            def turn(t):
                n = ROWS[t]
                for h in range(2):
                    act.wait_ge(p_xT, 2 * t + h + 1)
                    A.activation(turned[0][:, 4 * h:4 * h + 4, t * P:t * P + n],
                                 bank[(2 * t + h) % 4][:].rearrange("p (k n) -> p k n", k=4)[:, :, 0:n], ACT.Copy).then_inc(a_xT, 1)

            weigh(0)
            weigh(1)
            for t, n in enumerate(ROWS):
                ln.scalar(act, t, n)
                if turned and t >= 1:
                    turn(t - 1)
                if t + 2 < NT:
                    weigh(t + 2)
            if turned:
                turn(NT - 1)

        @block.vector
        def _(dve):
            V = nc.vector
            for t, n in enumerate(ROWS):
                src = s[0:n, t % 2, :]
                dve.wait_ge(y_in[t % 3], 16 * (t // 3 + 1))
                dve.wait_ge(first, t + 1)
                ln.link(dve, V.scalar_tensor_tensor(src, yin[0:n, t % 3, 1, :], gates[0:n, t, 1:2], src, ALU.mult, ALU.add))
                dve.sem_inc(summed, 1)
                ln.link(dve, V.scalar_tensor_tensor(src, x_tok[0:n, t, :], ALPHA, src, ALU.mult, ALU.add))
                if t == 0:
                    dve.wait_ge(ln_w, 32)
                ln.vector(dve, t, n, s[:, t % 2, :], x_tok[:, t, :])

        @block.gpsimd
        def _(pool):
            pool.wait_ge(ln_w, 32)
            for t, n in enumerate(ROWS):
                ln.pool(pool, t, n, s[:, t % 2, :], x_tok[:, t, :])
            pool.wait_ge(ln.done, NT)

        @block.tensor
        def _(pe):
            if turned:
                for t, n in enumerate(ROWS):
                    pe.wait_ge(ln.done, t + 1)
                    for h in range(2):
                        i = 2 * t + h
                        if i >= 4:
                            pe.wait_ge(a_xT, i - 3)
                        for q in range(4):
                            k = 4 * h + q
                            mm = nc.tensor.transpose(bank[i % 4][:, q * P:q * P + n], x_tok[0:n, t, k * P:(k + 1) * P], ident[0:n, 0:n])
                        mm.then_inc(p_xT, 1)


def stream_step(nc, d, o, places):
    with ExitStack() as ctx:
        S = State()
        S.d, S.o, S.places = d, o, places
        S.x_tok = ctx.enter_context(nc.sbuf_tensor("x_tok", [P, NT, DM], F32))
        S.ident = Constants(nc, ctx, S, "all", "ident")
        S.bank = [ctx.enter_context(nc.psum_tensor(f"bank{i}", [P, 512], F32)) for i in range(8)]
        S.gates = ctx.enter_context(nc.sbuf_tensor("gates", [P, NT, 2], F32))
        S.out_done = ctx.enter_context(nc.semaphore("out_done"))
        S.out_pool = ctx.enter_context(nc.semaphore("out_pool"))
        S.x_rows = nc.dram_tensor("x_rows", [2 * TOK, HALF], F32, kind="Internal").ap()
        S.y_rows = nc.dram_tensor("y_rows", [4 * TOK, HALF], F32, kind="Internal").ap()
        S.y_pairs = S.y_rows.rearrange("(t k h) c -> t k (h c)", k=2, h=2)
        S.OUT_ODD = 16 * (4 + 2 * NT + 1)
        even_mixer(nc, S)
        moe(nc, S, 0)
        odd_mixer(nc, S)
        moe(nc, S, 1)
        combine(nc, S, 1)
        with nc.Block(no_gpsimd_drain=True) as block:
            @block.sync
            def _(sp):
                sp.wait_ge(S.out_done, S.OUT_ODD + 16 * NT)
                sp.wait_ge(S.out_pool, 32)


class State:
    pass


_OUTS = [("y_prompt", (1, SEQ, DM)), ("y_sample", (1, DEC, DM)),
         ("gla_state_prompt", (1, 1, GH, GK, GV)), ("gla_state_sample", (1, 1, GH, GK, GV)),
         ("pool_state_prompt", (1, 1, 15, 512)), ("pool_state_sample", (1, 1, 15, 512)),
         ("mla_ckv_prompt", (1, 1, SEQ, P)), ("mla_ckv_sample", (1, 1, DEC, P)),
         ("mla_kpe_prompt", (1, 1, SEQ, MR)), ("mla_kpe_sample", (1, 1, DEC, MR)),
         ("gmlp_v_sample", (1, 1, DEC, MW))]


def kernel(**inputs):
    import numpy as _np
    import concourse.bacc as _bacc
    from concourse import mybir as _mybir
    from concourse.bass_utils import run_bass_kernel_spmd as _run

    table, places = constant_table()
    laid = {name: _np.ascontiguousarray(a) for name, a in inputs.items()}
    laid["pool_scale"] = _np.ascontiguousarray(_np.asarray(inputs["pool_scale"]).reshape(4, P).T)
    laid["gmlp_bs"] = _np.ascontiguousarray(_np.asarray(inputs["gmlp_bs"])[0].T)
    laid["constants"] = table

    nc = _bacc.Bacc("TRN2", target_bir_lowering=False, num_devices=1)
    arrays, d, o = {}, {}, {}
    for name, a in laid.items():
        arrays[f"in_{name}"] = a
        d[name] = nc.dram_tensor(f"in_{name}", a.shape, _mybir.dt.from_np(a.dtype), kind="ExternalInput").ap()
    for name, shape in _OUTS:
        o[name] = nc.dram_tensor(f"out_{name}", shape, F32, kind="ExternalOutput").ap()
    stream_step(nc, d, o, places)
    r = _run(nc, [arrays], core_ids=[0])
    return tuple(r.results[0][f"out_{name}"] for name, _ in _OUTS)
```

```python
import concourse.bass as bass
from concourse import mybir
from contextlib import ExitStack
import numpy as np

F32 = mybir.dt.float32
I32 = mybir.dt.int32
U32 = mybir.dt.uint32
ALU = mybir.AluOpType
ACT = mybir.ActivationFunctionType
AX = mybir.AxisListType

P = 128
DM = 1024
KT = DM // P
SEQ, DEC, PAST = 512, 32, 128
TOK = SEQ + DEC
ROWS = [128, 128, 128, 128, 32]
NT = len(ROWS)
DEPTH = 2
ALPHA = float((2 * DEPTH) ** 0.25)
EPS = 1e-5
NE, DE = 32, 256
NG, EPG = 4, 8
SLOTS = 64
OVER = 2 * TOK // SLOTS + 1
MAXB = NE + OVER
EXTRA = [2, 5, 8, 11]
PEELED = 12
BIG = 1e30
HALF = DM // 2
MH, MN, MR, MV = 8, 64, 32, 64
QW, QR = MN + MR, 256
AW, MW = QR + P + MR, 512
SCALE = float((MN + MR) ** -0.5)
GH, GK, GV, GR = 4, 64, 128, 16


def put(table, name, array):
    a = np.zeros((P, array.shape[1]), np.float32)
    a[:array.shape[0]] = array
    table[name] = a


def constant_table():
    c = {}
    i = np.arange(P)
    put(c, "ident", np.eye(P))
    put(c, "tri_strict", (i[:, None] < i[None, :]) * 1.0)
    put(c, "tri_incl", (i[:, None] <= i[None, :]) * 1.0)
    put(c, "ones", np.ones((P, P)))
    put(c, "iota", np.tile(np.arange(P)[None, :], (P, 1)))
    put(c, "iota_slot", np.tile((np.arange(P) % SLOTS)[None, :], (P, 1)))
    tok = np.arange(NT)[None, :] * P + i[:, None]
    valid = tok < TOK
    put(c, "valid", valid * 1.0)
    put(c, "assignment", ((2 * tok[:, :, None] + np.arange(2) + 1) * valid[:, :, None]).reshape(P, 2 * NT))
    put(c, "fills", np.tile(np.arange(9)[None, :] * SLOTS, (P, 1)))
    put(c, "pairs", np.tile(np.arange(OVER // 2)[None, :] * 2.0, (P, 1)))
    put(c, "half", (i[:, None] >= SLOTS) * 1.0)
    chunk = i // 64
    put(c, "gate_sum", ((i[:, None] <= i[None, :]) & (chunk[:, None] == chunk[None, :])) / 16.0)
    for w in (2, 4, 8, 16):
        inside = (i[:, None] <= i[None, :]) & (i[:, None] > i[None, :] - w)
        count = np.minimum(i[None, :] + 1, w)
        put(c, f"first{w}", inside / count - np.eye(P))
        put(c, f"window{w}", inside / w - np.eye(P))
        before = (i[:, None] - P) > (i[None, :] - w)
        put(c, f"before{w}", before / w)
        put(c, f"history{w}", ((np.arange(15)[:, None] - 15) > (np.arange(DEC)[None, :] - w)) / w)
    put(c, "causal", ((i[:, None] <= i[None, :]) & (chunk[:, None] == chunk[None, :])) * 1.0)
    inv = (10000.0 ** (-np.arange(16, dtype=np.float32) * 2.0 / 32)).astype(np.float32)
    pos = np.concatenate([np.arange(SEQ), PAST + np.arange(DEC)])
    pos = np.concatenate([pos, np.zeros(NT * P - TOK)]).astype(np.float32)
    ang = (pos[:, None] * inv[None, :]).astype(np.float32).reshape(NT, P, 16).transpose(1, 0, 2)
    put(c, "upto", (i[:, None] <= i[None, :]) * 1.0)
    put(c, "cos", np.cos(ang).reshape(P, NT * 16))
    put(c, "sin", np.sin(ang).reshape(P, NT * 16))
    groups = {"all": ["ident"], "route": ["tri_strict", "tri_incl", "ones", "iota", "iota_slot", "valid", "assignment", "fills", "pairs", "half"],
              "rope": ["cos", "sin", "upto"]}
    groups["even"] = [n for n in c if all(n not in g for g in groups.values())]
    c = {n: c[n] for g in ("all", "route", "even", "rope") for n in groups[g]}
    at, places = 0, {}
    for g in ("all", "route", "even", "rope"):
        first = at
        for name in groups[g]:
            places[name] = (at - first, c[name].shape[1])
            at += c[name].shape[1]
        places["group " + g] = (first, at - first)
    return np.ascontiguousarray(np.concatenate(list(c.values()), 1).astype(np.float32)), places


class Constants:

    def __init__(self, nc, ctx, S, group, name):
        first, width = S.places["group " + group]
        self.places, self.tile = S.places, ctx.enter_context(nc.sbuf_tensor(name, [P, width], F32))
        self.source = S.d["constants"][:, first:first + width]

    def __call__(self, name):
        at, width = self.places[name]
        return self.tile[:, at:at + width]


class Stage(ExitStack):

    def __init__(self, nc, prefix):
        super().__init__()
        self.nc, self.prefix, self.sems = nc, prefix, []

    def sb(self, name, shape, dt=F32):
        return self.enter_context(self.nc.sbuf_tensor(self.prefix + name, shape, dt))

    def sem(self, name):
        self.sems.append(self.nc.alloc_semaphore(self.prefix + "s_" + name))
        return self.sems[-1]

    def __exit__(self, *exc):
        out = super().__exit__(*exc)
        if exc[0] is None and self.sems:
            self.nc.clear_and_free_semaphores(self.sems)
            self.nc.all_engine_barrier()
        return out


class Chain:

    def __init__(self, sem):
        self.sem, self.n = sem, 0

    def inc(self, ins):
        ins.then_inc(self.sem, 1)
        self.n += 1
        return self.n


class Norm:

    def __init__(self, nc, sb, sem, name, ring=2, by_act=False):
        self.nc, self.ring = nc, ring
        self.by_act = by_act
        if by_act:
            self.neg, self.shift = sb(name + "_neg", [P, ring]), sb(name + "_shift", [P, ring])
            self.shifted, self.gained = sem(name + "_shifted"), sem(name + "_gained")
        self.g, self.b = sb(name + "_g", [P, DM]), sb(name + "_b", [P, DM])
        self.st, self.mv = sb(name + "_st", [P, ring, 12]), sb(name + "_mv", [P, ring, 2])
        self.ve, self.rstd = (sb(name + s, [P, ring]) for s in ("_ve", "_rstd"))
        self.var, self.root, self.centred, self.scaled, self.done = (sem(name + s) for s in ("_var", "_root", "_centred", "_scaled", "_done"))
        self.chain = Chain(sem(name + "_dve"))

    def link(self, dve, ins):
        dve.wait_ge(self.chain.sem, self.chain.inc(ins))

    def vector(self, dve, t, n, src, dst):
        self.statistics(dve, t, n, src)
        if self.by_act and t < NT - 1:
            return
        self.centre(dve, t, n, src)
        if t == NT - 1:
            dve.wait_ge(self.done, t)
            self.finish(dve, t, n, src, dst)

    def statistics(self, dve, t, n, src):
        V, i = self.nc.vector, t % self.ring
        for h in range(2):
            ins = V.bn_stats(self.st[0:n, i, 6 * h:6 * h + 6], src[0:n, h * HALF:(h + 1) * HALF])
        self.link(dve, ins)
        self.link(dve, V.bn_aggr(self.mv[0:n, i, :], self.st[0:n, i, :]))
        if self.by_act:
            V.tensor_scalar(self.neg[0:n, i:i + 1], self.mv[0:n, i, 0:1], -1.0, None, ALU.mult)
        self.link(dve, V.tensor_scalar(self.ve[0:n, i:i + 1], self.mv[0:n, i, 1:2], EPS, None, ALU.add))
        V.reciprocal(self.ve[0:n, i:i + 1], self.ve[0:n, i:i + 1]).then_inc(self.var, 1)

    def centre(self, dve, t, n, src):
        V, i = self.nc.vector, t % self.ring
        V.scalar_tensor_tensor(src[0:n, :], src[0:n, :], self.mv[0:n, i, 0:1], self.g[0:n, :], ALU.subtract, ALU.mult).then_inc(self.centred, 1)

    def finish(self, dve, t, n, src, dst):
        V, i = self.nc.vector, t % self.ring
        dve.wait_ge(self.root, t + 1)
        dve.wait_ge(self.centred, 1 if self.by_act else t + 1)
        V.scalar_tensor_tensor(dst[0:n, :], src[0:n, :], self.rstd[0:n, i:i + 1], self.b[0:n, :], ALU.mult, ALU.add).then_inc(self.done, 1)

    def scalar(self, act, t, n, src=None):
        A, i = self.nc.scalar, t % self.ring
        act.wait_ge(self.var, t + 1)
        A.activation(self.rstd[0:n, i:i + 1], self.ve[0:n, i:i + 1], ACT.Sqrt).then_inc(self.root, 1)
        if self.by_act and t < NT - 1:
            act.wait_ge(self.root, t + 1)
            A.activation(self.shift[0:n, i:i + 1], self.neg[0:n, i:i + 1], ACT.Copy, scale=self.rstd[0:n, i:i + 1]).then_inc(self.shifted, 1)
            act.wait_ge(self.shifted, t + 1)
            A.activation(src[0:n, :], src[0:n, :], ACT.Identity, bias=self.shift[0:n, i:i + 1], scale=self.rstd[0:n, i:i + 1]).then_inc(self.scaled, 1)

    def pool(self, pool, t, n, src, dst):
        G, i = self.nc.gpsimd, t % self.ring
        if t < NT - 1:
            if self.by_act:
                pool.wait_ge(self.scaled, t + 1)
                G.tensor_tensor(src[0:n, :], src[0:n, :], self.g[0:n, :], ALU.mult).then_inc(self.gained, 1)
                pool.wait_ge(self.gained, t + 1)
                G.tensor_tensor(dst[0:n, :], src[0:n, :], self.b[0:n, :], ALU.add).then_inc(self.done, 1)
                return
            pool.wait_ge(self.root, t + 1)
            pool.wait_ge(self.centred, t + 1)
            G.tensor_scalar(src[0:n, :], src[0:n, :], self.rstd[0:n, i:i + 1], None, ALU.mult).then_inc(self.scaled, 1)
            pool.wait_ge(self.scaled, t + 1)
            G.tensor_tensor(dst[0:n, :], src[0:n, :], self.b[0:n, :], ALU.add).then_inc(self.done, 1)


class Weights(Stage):

    W13, W2 = KT * 2 * DE, 2 * DM

    def __init__(self, nc, S, layer):
        super().__init__(nc, f"w{layer}_")
        self.S, self.layer, self.more = S, layer, None
        self.in13 = [self.sem(f"in13_{j}") for j in range(2 + len(EXTRA))]
        self.in2 = [self.sem(f"in2_{j}") for j in range(2 + len(EXTRA))]
        self.place, self.turn, loads = {}, {}, [0, 0]
        for m in range(PEELED):
            self.place[m] = 2 + EXTRA.index(m) if m in EXTRA else sum(loads) % 2
            self.turn[m] = 1
            if m not in EXTRA:
                loads[self.place[m]] += 1
                self.turn[m] = loads[self.place[m]]
        self.short = PEELED // 2 - loads[0]

    def at(self, j):
        size = self.W13 + self.W2
        return self.S.shared[:, j * size:(j + 1) * size] if j < 2 else self.more[:, (j - 2) * size:(j - 1) * size]

    def w13(self, j):
        return self.at(j)[:, 0:self.W13].rearrange("p (i h k n) -> p i h k n", i=2, h=2, k=4)

    def w2(self, j):
        return self.at(j)[:, self.W13:].rearrange("p (f n) -> p f n", f=2)

    def load13(self, sp, e, j):
        for i, name in enumerate(("expert_w1", "expert_w3")):
            sp.dma_start(self.w13(j)[:, i, :, :, :], self.S.d[name][self.layer, bass.ds(e, 1), :, :].rearrange("e (h p k) n -> p (e h) k n", h=2, k=4)).then_inc(self.in13[j], 16)

    def load2(self, sp, e, j):
        sp.dma_start(self.w2(j), self.S.d["expert_w2"][self.layer, bass.ds(e, 1), :, :].rearrange("e (p f) n -> p (e f) n", f=2)).then_inc(self.in2[j], 16)

    def load_first(self, sp, places):
        for m in range(PEELED):
            if self.turn[m] == 1 and self.place[m] in places:
                self.load13(sp, m, self.place[m])
                self.load2(sp, m, self.place[m])


def out_products(T, lower, upper, t, catT, wo, rows):
    n = ROWS[t]
    if t < 4:
        for h, bank in enumerate((lower, upper)):
            for k in rows:
                mm = T.matmul(bank[0:n, :], catT[:, k, 0:n], wo[:, k, h * HALF:(h + 1) * HALF], start=(k == 4), stop=(k == 3))
    else:
        for k in rows:
            for q in range(4):
                mm = T.matmul(lower[DEC * q:DEC * (q + 1), 0:256], catT[:, k, 0:n], wo[:, k, q * 256:(q + 1) * 256], start=(k == 4), stop=(k == 3))
    return mm


def residual(V, lower, upper, t, x_tok, s):
    n = ROWS[t]
    parts = [(lower[0:n, :], HALF), (upper[0:n, :], HALF)] if t < 4 else [(lower[DEC * q:DEC * (q + 1), 0:256], 256) for q in range(4)]
    for i, (y, width) in enumerate(parts):
        cols = slice(i * width, (i + 1) * width)
        ins = V.scalar_tensor_tensor(s[0:n, cols], x_tok[0:n, t, cols], ALPHA, y, ALU.mult, ALU.add)
    return ins


def even_mixer(nc, S, W):
    bank, x_tok, ident = S.bank, S.x_tok, S.ident("ident")
    QK = 2 * GH * GK
    VW = GH * GV
    COLS = [0, QK, QK + VW, QK + 2 * VW + GR]
    GCOL = QK + 2 * VW
    CH = [(0, 64), (64, 128)]
    with Stage(nc, "m0_") as ctx:
        sb, sem = ctx.sb, ctx.sem
        C = Constants(nc, ctx, S, "even", "m0_const")
        w = [S.shared[:, c * KT * 512:(c + 1) * KT * 512].rearrange("p (k n) -> p k n", k=KT) for c in range(4)]
        wg = sb("wg", [P, KT, GR])
        wo = sb("wo", [P, KT, DM])
        xT = sb("xT", [P, KT, TOK])
        gT = sb("gT", [32, TOK])
        wgu = sb("wgu", [GR + 1, GH * GK])
        pw = sb("pw", [P, 4, P])
        pscale = sb("pscale", [P, 4])
        gn = sb("gn", [P, GV])
        hist = sb("hist", [15, 512])
        state = sb("state", [P, 2, 2, GV])
        state_s = sb("state_s", [P, 2, 2, GV])
        qk = sb("qk", [P, 2, QK])
        v = sb("v", [P, 2, VW])
        r = sb("r", [P, 2, VW])
        xp = sb("xp", [P, 3, 512])
        za = sb("za", [P, 256])
        zb = sb("zb", [P, 256])
        la = zb
        bT = sb("bT", [P, 2, P])
        dm_ = sb("dmid", [P, 2, P])
        de = sb("dend", [P, 2, P])
        e1 = sb("e1", [P, 4, 2, P])
        q1 = sb("q1", [P, 2, 2, P])
        k1, k2 = e1[:, 1, :, :], e1[:, 2, :, :]
        q2 = sb("q2", [P, 2, P])
        k2t = sb("k2t", [P, 256])
        sT = sb("sT", [P, GH, P])
        ssq = sb("ssq", [P, GH])
        rs = sb("rs", [P, GH])
        sq = S.shared[:, 4 * KT * 512:4 * KT * 512 + GV]
        co = sb("co", [P, VW])
        er = co
        mixT = sb("mixT", [P, 4, P])
        catT = sb("catT", [P, KT, P])
        s = sb("s", [P, DM])
        ln = Norm(nc, sb, sem, "mix")

        x_in, c_in, g_in, small = sem("x_in"), sem("c_in"), sem("g_in"), sem("small")
        w_in = [sem(f"w_in{c}") for c in range(4)]
        wo_in = sem("wo_in")
        p_xT, a_xT, p_g, a_g = sem("p_xT"), sem("a_xT"), sem("p_g"), sem("a_g")
        p_in, in_sb = sem("p_in"), sem("in_sb")
        p_z, d_la, p_b, d_q, p_s, d_s = sem("p_z"), sem("d_la"), sem("p_b"), sem("d_q"), sem("p_s"), sem("d_s")
        p_k2, a_k2, p_mix, a_mix, p_pool, a_pool = sem("p_k2"), sem("a_k2"), sem("p_mix"), sem("a_mix"), sem("p_pool"), sem("a_pool")
        p_sps, p_oc, d_st, d_o, p_c, a_c = sem("p_sps"), sem("p_oc"), sem("d_st"), sem("d_o"), sem("p_c"), sem("a_c")
        p_y, d_y, a_gate, d_gate, a_exp, d_d, a_sq, d_sq, a_rs = (sem(x) for x in ("p_y", "d_y", "a_gate", "d_gate", "a_exp", "d_d", "a_sq", "d_sq", "a_rs"))
        a_er, d_r, g_r, d_zero = sem("a_er"), sem("d_r"), sem("g_r"), sem("d_zero")
        dch, ach = Chain(sem("d_chain")), Chain(sem("a_chain"))
        NCH = [2, 2, 2, 2, 1]
        CDONE = [0, 2, 4, 6, 8, 9]
        block = ctx.enter_context(nc.Block(no_gpsimd_drain=True))
        D = S.d

        @block.sync
        def _(sp):
            sp.dma_start(x_tok[:, 0:2, :], D["x_prompt"][0, 0:256, :].rearrange("(t p) d -> p t d", p=P)).then_inc(x_in, 16)
            sp.dma_start(S.ident.tile[:], S.ident.source).then_inc(c_in, 16)
            sp.dma_start(x_tok[:, 2:4, :], D["x_prompt"][0, 256:512, :].rearrange("(t p) d -> p t d", p=P)).then_inc(x_in, 16)
            sp.dma_start(x_tok[0:DEC, 4, :], D["x_sample"][0]).then_inc(x_in, 16)
            win = D["w_in_even"][0].rearrange("(k p) n -> p k n", p=P)
            sp.dma_start(wg[:], win[:, :, GCOL:GCOL + GR]).then_inc(g_in, 16)
            for c in range(4):
                sp.dma_start(w[c], win[:, :, COLS[c]:COLS[c] + 512]).then_inc(w_in[c], 16)
            sp.dma_start(wo[:], D["w_out_even"][0].rearrange("(k p) n -> p k n", p=P)).then_inc(wo_in, 16)
            sp.wait_ge(p_in, 4 * NT)
            W.load_first(sp, range(2))
            for t, dst in ((3, S.o["gla_state_prompt"]), (4, S.o["gla_state_sample"])):
                sp.wait_ge(d_st, CDONE[t + 1])
                src = state if t == 3 else state_s
                for h in range(2):
                    sp.dma_start(dst[0, 0].rearrange("(m h) k v -> h k m v", h=2)[h], src[64 * h:64 * h + 64, :, h, :]).then_inc(S.out_done, 16)
            for t in range(NT):
                sp.wait_ge(ln.done, t + 1)
                n = ROWS[t]
                sp.dma_start(S.x_rows.rearrange("(t h) c -> t (h c)", h=2)[t * P:t * P + n, :], x_tok[0:n, t, :]).then_inc(S.x_stored, 16)

            sp.wait_ge(S.out_done, 64)

        @block.scalar
        def _(act):
            A = nc.scalar

            def alink(ins):
                act.wait_ge(ach.sem, ach.inc(ins))

            act.dma_start(C.tile[:], C.source).then_inc(small, 16)
            act.dma_start(wgu[0:GR, :], D["w_gate_up"][0]).then_inc(small, 16)
            act.dma_start(wgu[GR:GR + 1, :], D["b_gate"][0:1, :]).then_inc(small, 16)
            act.dma_start(pw[:], D["pool_w"][0].rearrange("g c d -> c g d")).then_inc(small, 16)
            act.dma_start(pscale[:], D["pool_scale"]).then_inc(small, 16)
            act.dma_start(gn[:], D["gla_norm_g"][0:1, :].to_broadcast([P, GV])).then_inc(small, 16)
            act.dma_start(hist[:], D["state_pool"][0, 0]).then_inc(small, 16)
            act.wait_ge(d_zero, 3)
            for h in range(2):
                act.dma_start(state_s[64 * h:64 * h + 64, :, h, :], D["state_gla"][0, 0].rearrange("(m h) k v -> h k m v", h=2)[h]).then_inc(small, 16)
            act.dma_start(ln.g[:], D["ln_mix_g"][0:1, :].to_broadcast([P, DM])).then_inc(small, 16)
            act.dma_start(ln.b[:], D["ln_mix_b"][0:1, :].to_broadcast([P, DM])).then_inc(small, 16)

            for i in range(2 * NT):
                t, h = i // 2, i % 2
                n = ROWS[t]
                act.wait_ge(p_xT, i + 1)
                A.activation(xT[:, 4 * h:4 * h + 4, t * P:t * P + n], bank[i % 4][:].rearrange("p (k n) -> p k n", k=4)[:, :, 0:n], ACT.Copy).then_inc(a_xT, 1)
            act.wait_ge(p_g, 1)
            for h in range(2):
                ins = A.activation(gT[0:GR, h * 272:(h + 1) * 272], bank[4 + h][0:GR, 0:272], ACT.Copy)
            ins.then_inc(a_g, 1)

            def evacuate(t, c):
                n = ROWS[t]
                act.wait_ge(p_in, 4 * t + c + 1)
                if t >= 2:
                    if c == 0:
                        act.wait_ge(p_b, t - 1)
                    elif c == 1:
                        act.wait_ge(p_oc, CDONE[t - 1])
                    elif c == 2:
                        act.wait_ge(d_o, t - 1)
                if c == 3 and t >= 3:
                    act.wait_ge(p_mix, t - 1)
                dst = (qk[0:n, t % 2, :], v[0:n, t % 2, :], r[0:n, t % 2, :], xp[0:n, t % 3, :])[c]
                src = bank[c % 2][0:n, :] if t < 4 else bank[0][DEC * c:DEC * (c + 1), :]
                A.activation(dst, src, ACT.Copy).then_inc(in_sb, 1)

            for c in range(4):
                evacuate(0, c)
            for t, n in enumerate(ROWS):
                nxt = t + 1 < NT
                act.wait_ge(p_z, t + 1)
                if t >= 1:
                    act.wait_ge(d_la, t)
                alink(A.activation(za[0:n, :], bank[4][0:n, 0:256], ACT.Abs))
                if t >= 1:
                    act.wait_ge(p_b, t)
                alink(A.activation(zb[0:n, :], za[0:n, :], ACT.Exp, scale=-1.0))
                A.activation(za[0:n, :], zb[0:n, :], ACT.Ln, bias=1.0).then_inc(a_gate, 1)
                if nxt:
                    evacuate(t + 1, 0)
                act.wait_ge(d_d, t + 1)
                if t >= 1:
                    act.wait_ge(d_st, CDONE[t])
                    act.wait_ge(p_k2, t)
                A.activation(e1[:, 0, :, 0:n], dm_[:, :, 0:n], ACT.Exp)
                A.activation(e1[:, 1, :, 0:n], dm_[:, :, 0:n], ACT.Exp, scale=-1.0)
                A.activation(e1[:, 2, :, 0:n], de[:, :, 0:n], ACT.Exp)
                A.activation(e1[:, 3, :, 0:n], bT[:, :, 0:n], ACT.Exp).then_inc(a_exp, 1)
                if nxt:
                    evacuate(t + 1, 1)
                act.wait_ge(in_sb, 4 * t + 3)
                if t >= 1:
                    act.wait_ge(p_c, t)
                A.activation(er[0:n, :], r[0:n, t % 2, :], ACT.Exp, scale=-1.0).then_inc(a_er, 1)
                act.wait_ge(p_k2, t + 1)
                A.activation(k2t[0:n, :], bank[4][0:n, 0:256], ACT.Copy).then_inc(a_k2, 1)
                if nxt:
                    evacuate(t + 1, 2)
                act.wait_ge(p_mix, t + 1)
                A.activation(mixT[:, :, 0:n], bank[6][:].rearrange("p (g n) -> p g n", g=4)[:, :, 0:n], ACT.Copy).then_inc(a_mix, 1)
                act.wait_ge(p_pool, t + 1)
                if t >= 1:
                    act.wait_ge(p_y, t)
                for g in range(4):
                    ins = A.activation(catT[:, 4 + g, 0:n], bank[6][:, g * P:g * P + n], ACT.Copy, scale=pscale[:, g:g + 1])
                ins.then_inc(a_pool, 1)
                if nxt:
                    evacuate(t + 1, 3)
                act.wait_ge(p_oc, CDONE[t + 1])
                for h in range(GH):
                    if h or t:
                        act.wait_ge(a_sq, GH * t + h)
                    A.activation(sq[0:n, :], bank[7][0:n, h * GV:(h + 1) * GV], ACT.Square, accum_out=ssq[0:n, h:h + 1]).then_inc(a_sq, 1)
                act.wait_ge(d_sq, t + 1)
                A.activation(rs[0:n, :], ssq[0:n, :], ACT.Sqrt).then_inc(a_rs, 1)
                act.wait_ge(p_c, t + 1)
                A.activation(catT[:, 0:4, 0:n], bank[6][:].rearrange("p (g n) -> p g n", g=4)[:, :, 0:n], ACT.Copy).then_inc(a_c, 1)
                ln.scalar(act, t, n)

        @block.vector
        def _(dve):
            V = nc.vector

            def link(ins):
                dve.wait_ge(dch.sem, dch.inc(ins))

            V.memset(gT[:], 1.0).then_inc(d_zero, 1)
            V.memset(state[:], 0.0).then_inc(d_zero, 1)
            V.memset(state_s[:], 0.0).then_inc(d_zero, 1)
            V.memset(q1[:], 0.0)
            link(V.memset(sT[:], 0.0))
            dve.wait_ge(small, 176)
            for t, n in enumerate(ROWS):
                nch, w_ = NCH[t], min(64, n)
                st = state if t < 4 else state_s
                dve.wait_ge(a_gate, t + 1)
                if t >= 1:
                    dve.wait_ge(p_b, t)
                V.scalar_tensor_tensor(la[0:n, :], bank[4][0:n, 0:256], 0.0, za[0:n, :], ALU.min, ALU.subtract).then_inc(d_la, 1)
                dve.wait_ge(p_b, t + 1)
                if t >= 1:
                    dve.wait_ge(a_exp, t)
                link(V.tensor_copy(bT[:, :, 0:n], bank[4][:, 256:512].rearrange("p (m n) -> p m n", m=2)[:, :, 0:n]))
                for m in range(2):
                    b4 = bT[:, m, 0:n].rearrange("p (c i) -> p c i", i=w_)
                    V.tensor_tensor(dm_[:, m, 0:n].rearrange("p (c i) -> p c i", i=w_), b4, b4[:, :, w_ // 2 - 1:w_ // 2].to_broadcast([P, nch, w_]), ALU.subtract)
                    ins = V.tensor_tensor(de[:, m, 0:n].rearrange("p (c i) -> p c i", i=w_), b4[:, :, w_ - 1:w_].to_broadcast([P, nch, w_]), b4, ALU.subtract)
                link(ins)
                V.tensor_scalar(dm_[:, :, 0:n], dm_[:, :, 0:n], 80.0, -80.0, ALU.min, ALU.max).then_inc(d_d, 1)
                dve.wait_ge(a_exp, t + 1)
                z5 = bank[5][:].rearrange("p (m n) -> p m n", m=4)
                if t >= 1:
                    dve.wait_ge(p_oc, CDONE[t])
                for h in range(2):
                    hs = slice(64 * h, 64 * h + 64)
                    V.scalar_tensor_tensor(q1[hs, :, h, 0:n], z5[hs, 0:2, 0:n], GK ** -0.5, e1[hs, 0, :, 0:n], ALU.mult, ALU.mult)
                V.scalar_tensor_tensor(q2[:, :, 0:n], z5[:, 0:2, 0:n], GK ** -0.5, e1[:, 3, :, 0:n], ALU.mult, ALU.mult)
                V.tensor_tensor(k1[:, :, 0:n], z5[:, 2:4, 0:n], e1[:, 1, :, 0:n], ALU.mult)
                link(V.tensor_tensor(k2[:, :, 0:n], z5[:, 2:4, 0:n], e1[:, 2, :, 0:n], ALU.mult))
                dve.sem_inc(d_q, 1)
                dve.wait_ge(a_er, t + 1)
                link(V.tensor_scalar(er[0:n, :], er[0:n, :], 1.0, None, ALU.add))
                link(V.reciprocal(er[0:n, :], er[0:n, :]))
                V.tensor_tensor(r[0:n, t % 2, :], r[0:n, t % 2, :], er[0:n, :], ALU.mult).then_inc(d_r, 1)
                dve.wait_ge(p_s, t + 1)
                for h in range(GH):
                    ins = V.copy_predicated(sT[0:n, h, 0:n], C("causal")[0:n, 0:n].bitcast(U32), bank[6][0:n, h * P:h * P + n])
                ins.then_inc(d_s, 1)
                for c in range(nch):
                    dve.wait_ge(p_sps, t + 1)
                    dve.wait_ge(p_oc, CDONE[t] + c + 1)
                    for m in range(2):
                        for h in range(2):
                            hs = slice(64 * h, 64 * h + 64)
                            ins = V.scalar_tensor_tensor(st[hs, m, h, :], st[hs, m, h, :], e1[hs, 3, m, c * 64 + w_ - 1:c * 64 + w_],
                                                         bank[5 - c][hs, (2 * m + h) * P:(2 * m + h + 1) * P], ALU.mult, ALU.add)
                    link(ins)
                    dve.sem_inc(d_st, 1)
                dve.wait_ge(a_sq, GH * (t + 1))
                link(V.tensor_scalar(ssq[0:n, :], ssq[0:n, :], 1.0 / GV, EPS, ALU.mult, ALU.add))
                link(V.reciprocal(ssq[0:n, :], ssq[0:n, :]))
                dve.sem_inc(d_sq, 1)
                dve.wait_ge(a_rs, t + 1)
                dve.wait_ge(g_r, t + 1)
                for h in range(GH):
                    hs = slice(h * GV, (h + 1) * GV)
                    ins = V.scalar_tensor_tensor(co[0:n, hs], bank[7][0:n, hs], rs[0:n, h:h + 1], r[0:n, t % 2, hs], ALU.mult, ALU.mult)
                ins.then_inc(d_o, 1)
                if t >= 1:
                    dve.wait_ge(ln.done, t)
                dve.wait_ge(p_y, t + 1)
                link(residual(V, bank[2], bank[3], t, x_tok, s))
                dve.sem_inc(d_y, 1)
                ln.vector(dve, t, n, s, x_tok[:, t, :])

        @block.gpsimd
        def _(pool):
            G = nc.gpsimd
            pool.wait_ge(small, 176)
            for t, n in enumerate(ROWS):
                pool.wait_ge(d_r, t + 1)
                G.tensor_tensor(r[0:n, t % 2, :].rearrange("p (h v) -> p h v", h=GH), r[0:n, t % 2, :].rearrange("p (h v) -> p h v", h=GH),
                                gn[0:n, :].unsqueeze(1).to_broadcast([n, GH, GV]), ALU.mult).then_inc(g_r, 1)
                if t >= 3:
                    pool.wait_ge(in_sb, 4 * t + 4)
                    dst = S.o["pool_state_prompt"] if t == 3 else S.o["pool_state_sample"]
                    pool.dma_start(dst[0, 0], xp[n - 15:n, t % 3, :]).then_inc(S.out_pool, 16)
                ln.pool(pool, t, n, s, x_tok[:, t, :])
            pool.wait_ge(ln.done, NT)
            pool.wait_ge(S.out_pool, 32)

        @block.tensor
        def _(pe):
            T = nc.tensor
            pe.wait_ge(c_in, 16)
            for t, n in enumerate(ROWS):
                if t == 0:
                    pe.wait_ge(x_in, 48)
                for h in range(2):
                    i = 2 * t + h
                    if i >= 4:
                        pe.wait_ge(a_xT, i - 3)
                    for q in range(4):
                        k = 4 * h + q
                        mm = T.transpose(bank[i % 4][:, q * P:q * P + n], x_tok[0:n, t, k * P:(k + 1) * P], ident[0:n, 0:n])
                    mm.then_inc(p_xT, 1)
            pe.wait_ge(a_xT, 2 * NT)
            pe.wait_ge(g_in, 16)
            for h in range(2):
                for k in range(KT):
                    mm = T.matmul(bank[4 + h][0:GR, 0:272], wg[:, k, :], xT[:, k, h * 272:(h + 1) * 272], start=(k == 0), stop=(k == KT - 1))
            mm.then_inc(p_g, 1)

            def project(t, c):
                n = ROWS[t]
                if t == 0:
                    pe.wait_ge(w_in[c], 16)
                if t == 4 and c > 0:
                    return
                if 4 * t + c >= 2:
                    pe.wait_ge(in_sb, 4 * t + c - 1)
                if t == 4:
                    for k in range(KT):
                        for g in range(4):
                            mm = T.matmul(bank[0][DEC * g:DEC * (g + 1), :], xT[:, k, t * P:t * P + n], w[g][:, k, :], start=(k == 0), stop=(k == KT - 1))
                    mm.then_inc(p_in, 4)
                    return
                for k in range(KT):
                    mm = T.matmul(bank[c % 2][0:n, :], xT[:, k, t * P:t * P + n], w[c][:, k, :], start=(k == 0), stop=(k == KT - 1))
                mm.then_inc(p_in, 1)

            for c in range(4):
                project(0, c)
            pe.wait_ge(a_g, 1)
            pe.wait_ge(small, 176)
            for t, n in enumerate(ROWS):
                nch, w_ = NCH[t], min(64, n)
                st = state if t < 4 else state_s
                nxt = t + 1 < NT
                if t >= 1:
                    pe.wait_ge(d_st, CDONE[t])
                T.matmul(bank[4][0:n, 0:256], gT[0:GR + 1, t * P:t * P + n], wgu[:], start=True, stop=True).then_inc(p_z, 1)
                if nxt:
                    project(t + 1, 0)
                pe.wait_ge(d_la, t + 1)
                pe.wait_ge(in_sb, 4 * t + 1)
                for m in range(2):
                    T.matmul(bank[4][:, 256 + m * P:256 + m * P + n], la[0:n, m * P:(m + 1) * P], C("gate_sum")[0:n, 0:n], start=True, stop=True)
                if t >= 1:
                    pe.wait_ge(d_st, CDONE[t])
                for m in range(4):
                    mm = T.transpose(bank[5][:, m * P:m * P + n], qk[0:n, t % 2, m * P:(m + 1) * P], ident[0:n, 0:n])
                mm.then_inc(p_b, 1)
                if nxt:
                    project(t + 1, 1)
                pe.wait_ge(d_q, t + 1)
                if t >= 1:
                    pe.wait_ge(a_c, t)
                for m in range(2):
                    mm = T.matmul(bank[6][0:n, 2 * m * P:2 * (m + 1) * P].rearrange("p (h n) -> p h n", h=2)[:, :, 0:n], k1[:, m, 0:n], q1[:, m, :, 0:n],
                                  start=(m == 0), stop=(m == 1), skip_group_check=True)
                mm.then_inc(p_s, 1)
                for m in range(2):
                    mm = T.transpose(bank[4][0:n, m * P:(m + 1) * P], k2[:, m, 0:n], ident)
                mm.then_inc(p_k2, 1)
                if nxt:
                    project(t + 1, 2)
                pe.wait_ge(in_sb, 4 * t + 2)
                pe.wait_ge(d_s, t + 1)
                if t >= 1:
                    pe.wait_ge(d_o, t)
                for h in range(GH):
                    T.matmul(bank[7][0:n, h * GV:(h + 1) * GV], sT[0:n, h, 0:n], v[0:n, t % 2, h * GV:(h + 1) * GV], start=(h == 0), stop=False, skip_group_check=True)
                pe.wait_ge(a_k2, t + 1)
                for c in range(nch):
                    for m in range(2):
                        mm = T.matmul(bank[5 - c][:, m * 256:(m + 1) * 256], k2t[c * 64:c * 64 + w_, m * P:(m + 1) * P],
                                      v[c * 64:c * 64 + w_, t % 2, m * 256:(m + 1) * 256], start=(m == 0), stop=(m == 1), skip_group_check=True)
                mm.then_inc(p_sps, 1)
                pe.wait_ge(in_sb, 4 * t + 4)
                for g, win in enumerate((2, 4, 8, 16)):
                    now = C(f"first{win}" if t == 0 else f"window{win}")[0:n, 0:n]
                    parts = [(xp[0:n, t % 3, g * P:(g + 1) * P], now)]
                    if 0 < t < 4:
                        parts.append((xp[:, (t - 1) % 3, g * P:(g + 1) * P], C(f"before{win}")))
                    elif t == 4:
                        parts.append((hist[:, g * P:(g + 1) * P], C(f"history{win}")[0:15, :]))
                    for i, (rows, window) in enumerate(parts):
                        mm = T.matmul(bank[6][:, g * P:g * P + n], rows, window, start=(g == 0 and i == 0), stop=(g == 3 and i == len(parts) - 1), skip_group_check=True)
                mm.then_inc(p_mix, 1)
                pe.wait_ge(a_mix, t + 1)
                for g in range(4):
                    mm = T.matmul(bank[6][:, g * P:g * P + n], pw[:, g, :], mixT[:, g, 0:n], start=(g == 0), stop=(g == 3), skip_group_check=True)
                mm.then_inc(p_pool, 1)
                for c in range(nch):
                    if t == 0 and c == 0:
                        pe.wait_ge(d_zero, 2)
                    elif CDONE[t] + c > 0:
                        pe.wait_ge(d_st, CDONE[t] + c)
                    for m in range(2):
                        mm = T.matmul(bank[7][c * 64:c * 64 + w_, m * 256:(m + 1) * 256], q2[:, m, c * 64:c * 64 + w_],
                                      st[:, m, :, :], start=False, stop=(c == nch - 1 and m == 1), skip_group_check=True)
                    mm.then_inc(p_oc, 1)
                if nxt:
                    project(t + 1, 3)
                pe.wait_ge(a_pool, t + 1)
                pe.wait_ge(wo_in, 16)
                if t >= 1:
                    pe.wait_ge(d_y, t)
                out_products(T, bank[2], bank[3], t, catT, wo, range(4, 8))
                pe.wait_ge(d_o, t + 1)
                for m in range(4):
                    mm = T.transpose(bank[6][:, m * P:m * P + n], co[0:n, m * P:(m + 1) * P], ident[0:n, 0:n])
                mm.then_inc(p_c, 1)
                pe.wait_ge(a_c, t + 1)
                mm = out_products(T, bank[2], bank[3], t, catT, wo, range(0, 4))
                mm.then_inc(p_y, 1)


def odd_mixer(nc, S, W):
    bank, x_tok, ident, D = S.bank, S.x_tok, S.ident("ident"), S.d
    KEYS = SEQ + PAST + DEC
    FIRST, FW = [0, AW, AW + MW], [AW, MW, MW]
    KPOS = [0, 128, 256, 384, SEQ + PAST]
    with Stage(nc, "m1_") as ctx:
        sb = ctx.sb
        qT = sb("qT", [P, MH, TOK])
        kT = sb("kT", [P, MH, KEYS])
        val = sb("val", [P, NT + 1, MH * MV])
        u = sb("u", [P, NT, MW])

        with Stage(nc, "m1w_") as wc, ExitStack() as inner:
            w = [S.shared[:, KT * FIRST[c]:KT * (FIRST[c] + FW[c])].rearrange("p (k n) -> p k n", k=KT) for c in range(3)]
            at = KT * (FIRST[2] + FW[2])
            xT = S.shared[:, at:at + KT * TOK].rearrange("p (k n) -> p k n", k=KT)
            w_in = [wc.sem(f"w_in{c}") for c in range(3)]

            def load_w(sp):
                win = D["w_in_odd"][0].rearrange("(k p) n -> p k n", p=P)
                for c in range(3):
                    sp.dma_start(w[c], win[:, :, FIRST[c]:FIRST[c] + FW[c]]).then_inc(w_in[c], 16)

            combine(nc, S, 0, (xT, load_w))
            pc = inner.enter_context(Stage(nc, "m1p_"))
            pb, sem = pc.sb, pc.sem
            C = Constants(nc, pc, S, "rope", "m1_const")
            wuq = pb("wuq", [P, 2, MH * QW])
            wuk = pb("wuk", [P, MH * MN])
            wuv = pb("wuv", [P, MH * MV])
            qg = pb("qg", [P, QR])
            kg = pb("kg", [P, P])
            vg = pb("vg", [P, MW])
            vb = pb("vb", [P, MW])
            ws = pb("ws", [P, 4, P])
            wsT = pb("wsT", [P, 4, P])
            bs = pb("bs", [P, 4])
            lat = pb("lat", [P, 2, AW])
            sq = pb("sq", [P, QR])
            ss = pb("ss", [P, 2, 2])
            rs = pb("rs", [P, 2, 2])
            cqn = pb("cqn", [P, 2, QR])
            ckvn = pb("ckvn", [P, NT + 1, P])
            kst = pb("kst", [P, NT + 1, QW])
            rt = pb("rt", [P, 4, MR // 2])
            cqT = pb("cqT", [P, 2, P])
            ckvT = pb("ckvT", [P, KEYS])
            qr = pb("qr", [P, MH, QW])
            qt = pb("qt", [P, 4, MH, MR // 2])
            gv = pb("gv", [P, 2, MW])
            vst = pb("vst", [P, 6])
            vmv = pb("vmv", [P, 2])
            vve = pb("vve", [P, 1])
            vrs = pb("vrs", [P, 1])
            small, g_zero = sem("small"), sem("g_zero")
            cache_in, ws_in = sem("cache_in"), sem("ws_in")
            p_in, in_sb = sem("p_in"), sem("in_sb")
            p_ws, d_ws, a_ss, d_ss, a_rs, d_n = sem("p_ws"), sem("d_ws"), sem("a_ss"), sem("d_ss"), sem("a_rs"), sem("d_n")
            p_small, a_cqT, p_uq, a_q, d_rope, p_qT, a_qT = (sem(x) for x in ("p_small", "a_cqT", "p_uq", "a_q", "d_rope", "p_qT", "a_qT"))
            d_kpe, d_vv, a_vrs, d_vs, g_vn, p_gate, d_gated = (sem(x) for x in ("d_kpe", "d_vv", "a_vrs", "d_vs", "g_vn", "p_gate", "d_gated"))
            p_k, a_k, p_val, d_val, d_zero = sem("p_k"), sem("a_k"), sem("p_val"), sem("d_val"), sem("d_zero")
            dch, ach, gch = Chain(sem("d_chain")), Chain(sem("a_chain")), Chain(sem("g_chain"))
            block = pc.enter_context(nc.Block(no_gpsimd_drain=True))

            @block.sync
            def _(sp):
                for t, n in enumerate(ROWS):
                    sp.wait_ge(d_n, t + 1)
                    sp.wait_ge(d_kpe, t + 1)
                    part = (lambda a: a[0, 0, t * P:t * P + n, :]) if t < 4 else (lambda a: a[0, 0])
                    which = "prompt" if t < 4 else "sample"
                    sp.dma_start(part(S.o["mla_ckv_" + which]), ckvn[0:n, t, :]).then_inc(S.out_done, 16)
                    sp.dma_start(part(S.o["mla_kpe_" + which]), kst[0:n, t, MN:QW]).then_inc(S.out_done, 16)
                sp.wait_ge(g_vn, NT)
                sp.dma_start(S.o["gmlp_v_sample"][0, 0], gv[0:DEC, (NT - 1) % 2, :]).then_inc(S.out_done, 16)
                sp.wait_ge(S.out_done, S.OUT_ODD)

            @block.scalar
            def _(act):
                A = nc.scalar

                def alink(ins):
                    act.wait_ge(ach.sem, ach.inc(ins))

                act.dma_start(ws[:], D["gmlp_ws"][0].rearrange("g t s -> t g s")).then_inc(ws_in, 16)
                act.dma_start(C.tile[:], C.source).then_inc(ws_in, 16)
                act.dma_start(ckvn[:, NT, :], D["cache_mla_ckv"][0, 0]).then_inc(cache_in, 16)
                act.wait_ge(d_zero, 1)
                act.dma_start(kst[:, NT, MN:QW], D["cache_mla_kpe"][0, 0]).then_inc(cache_in, 16)
                for dst, src in ((qg, D["mla_q_norm_g"][0:1, :].to_broadcast([P, QR])), (kg, D["mla_kv_norm_g"][0:1, :].to_broadcast([P, P])),
                                 (vg, D["gmlp_norm_g"][0:1, :].to_broadcast([P, MW])), (vb, D["gmlp_norm_b"][0:1, :].to_broadcast([P, MW])),
                                 (wuq, D["mla_w_uq"][0].rearrange("(k p) n -> p k n", p=P)), (wuk, D["mla_w_uk"][0]), (wuv, D["mla_w_uv"][0]),
                                 (bs, D["gmlp_bs"])):
                    act.dma_start(dst[:], src).then_inc(small, 16)

                def evacuate(t, c):
                    n, i = ROWS[t], 3 * t + c
                    act.wait_ge(p_in, i + 1)
                    src = bank[i % 2][0:n, 0:FW[c]] if t < 4 else bank[0][DEC * c:DEC * (c + 1), 0:FW[c]]
                    if c == 0:
                        if t >= 2:
                            act.wait_ge(d_kpe, t - 1)
                            act.wait_ge(d_n, t - 1)
                        A.activation(lat[0:n, t % 2, :], src, ACT.Copy).then_inc(in_sb, 1)
                    elif c == 1:
                        A.activation(u[0:n, t, :], src, ACT.Gelu_apprx_tanh).then_inc(in_sb, 1)
                    else:
                        if t >= 2:
                            act.wait_ge(p_gate, t - 1)
                        A.activation(gv[0:n, t % 2, :], src, ACT.Gelu_apprx_tanh).then_inc(in_sb, 1)

                def mean_squares(t):
                    n = ROWS[t]
                    act.wait_ge(in_sb, 3 * t + 1)
                    if t >= 1:
                        act.wait_ge(d_ss, t)
                    if t >= 2:
                        act.wait_ge(d_n, t - 1)
                    alink(A.activation(sq[0:n, :], lat[0:n, t % 2, 0:QR], ACT.Square, accum_out=ss[0:n, t % 2, 0:1]))
                    A.activation(sq[0:n, 0:P], lat[0:n, t % 2, QR:QR + P], ACT.Square, accum_out=ss[0:n, t % 2, 1:2]).then_inc(a_ss, 1)

                def deviations(t):
                    n = ROWS[t]
                    act.wait_ge(d_ss, t + 1)
                    A.activation(rs[0:n, t % 2, :], ss[0:n, t % 2, :], ACT.Sqrt).then_inc(a_rs, 1)
                    act.wait_ge(d_vv, t + 1)
                    A.activation(vrs[0:n, :], vve[0:n, :], ACT.Sqrt).then_inc(a_vrs, 1)

                for c in range(3):
                    evacuate(0, c)
                mean_squares(0)
                for t, n in enumerate(ROWS):
                    nxt = t + 1 < NT
                    deviations(t)
                    if nxt:
                        evacuate(t + 1, 0)
                    act.wait_ge(p_small, t + 1)
                    if t >= 1:
                        act.wait_ge(p_uq, t)
                    A.activation(cqT[:, :, 0:n], bank[3][:, 0:256].rearrange("p (k n) -> p k n", k=2)[:, :, 0:n], ACT.Copy)
                    A.activation(ckvT[:, KPOS[t]:KPOS[t] + n], bank[3][:, 256:256 + n], ACT.Copy).then_inc(a_cqT, 1)
                    if nxt:
                        evacuate(t + 1, 1)
                    act.wait_ge(p_uq, t + 1)
                    if t >= 1:
                        act.wait_ge(p_qT, t)
                    for h in range(2):
                        ins = A.activation(qr[0:n, 4 * h:4 * h + 4, :].rearrange("p h d -> p (h d)"), bank[4 + h][0:n, 0:4 * QW], ACT.Copy)
                    ins.then_inc(a_q, 1)
                    if nxt:
                        evacuate(t + 1, 2)
                        mean_squares(t + 1)
                    act.wait_ge(p_qT, t + 1)
                    for h in range(2):
                        ins = A.activation(qT[0:QW, 4 * h:4 * h + 4, t * P:t * P + n], bank[6 + h][0:QW, :].rearrange("p (h n) -> p h n", h=4)[:, :, 0:n], ACT.Copy)
                    ins.then_inc(a_qT, 1)
                for i in range(8):
                    pair, part = i // 2, i % 2
                    keys = slice(0, SEQ) if part == 0 else slice(SEQ, KEYS)
                    width = keys.stop - keys.start
                    act.wait_ge(p_k, i + 1)
                    A.activation(kT[0:MN, 2 * pair, keys], bank[i % 4][0:MN, 0:width], ACT.Copy)
                    A.activation(kT[0:MN, 2 * pair + 1, keys], bank[i % 4][MN:P, 0:width], ACT.Copy).then_inc(a_k, 1)

            @block.vector
            def _(dve):
                V = nc.vector

                def link(ins):
                    dve.wait_ge(dch.sem, dch.inc(ins))

                link(V.memset(kst[:], 0.0))
                dve.sem_inc(d_zero, 1)
                link(V.memset(wsT[:], 0.0))
                dve.wait_ge(p_ws, 1)
                for g in range(4):
                    ins = V.copy_predicated(wsT[:, g, :], C("upto")[:].bitcast(U32), bank[7][:, g * P:(g + 1) * P])
                link(ins)
                dve.sem_inc(d_ws, 1)
                dve.wait_ge(small, 128)

                def rotated_keys(slot, rows):
                    at = KPOS[slot] if slot < NT else SEQ
                    return V.tensor_copy(kT[MN:QW, :, at:at + rows], bank[3][MN:QW, 384:384 + rows].unsqueeze(1).to_broadcast([MR, MH, rows]))

                def statistics(t):
                    n = ROWS[t]
                    dve.wait_ge(a_ss, t + 1)
                    V.tensor_scalar(ss[0:n, t % 2, 0:1], ss[0:n, t % 2, 0:1], 1.0 / QR, EPS, ALU.mult, ALU.add)
                    link(V.tensor_scalar(ss[0:n, t % 2, 1:2], ss[0:n, t % 2, 1:2], 1.0 / P, EPS, ALU.mult, ALU.add))
                    V.reciprocal(ss[0:n, t % 2, :], ss[0:n, t % 2, :]).then_inc(d_ss, 1)
                    dve.wait_ge(in_sb, 3 * t + 3)
                    link(V.bn_stats(vst[0:n, :], gv[0:n, t % 2, :]))
                    link(V.bn_aggr(vmv[0:n, :], vst[0:n, :]))
                    link(V.tensor_scalar(vve[0:n, :], vmv[0:n, 1:2], EPS, None, ALU.add))
                    V.reciprocal(vve[0:n, :], vve[0:n, :]).then_inc(d_vv, 1)

                def rotate(dst, x1, x2, tmp, cos, sin):
                    V.tensor_tensor(tmp[0], x1, cos, ALU.mult)
                    V.tensor_tensor(tmp[1], x2, sin, ALU.mult)
                    V.tensor_tensor(tmp[2], x1, sin, ALU.mult)
                    link(V.tensor_tensor(tmp[3], x2, cos, ALU.mult))
                    V.tensor_tensor(dst[0], tmp[0], tmp[1], ALU.subtract)
                    return V.tensor_tensor(dst[1], tmp[2], tmp[3], ALU.add)

                R2 = MR // 2
                for t, n in enumerate(ROWS):
                    i = t % 2
                    cos, sin = C("cos")[0:n, t * R2:(t + 1) * R2], C("sin")[0:n, t * R2:(t + 1) * R2]
                    statistics(t)
                    dve.wait_ge(a_rs, t + 1)
                    if t >= 2:
                        dve.wait_ge(p_small, t - 1)
                    V.scalar_tensor_tensor(cqn[0:n, i, :], lat[0:n, i, 0:QR], rs[0:n, i, 0:1], qg[0:n, :], ALU.mult, ALU.mult)
                    V.scalar_tensor_tensor(ckvn[0:n, t, :], lat[0:n, i, QR:QR + P], rs[0:n, i, 1:2], kg[0:n, :], ALU.mult, ALU.mult).then_inc(d_n, 1)
                    at = QR + P
                    rotate((kst[0:n, t, MN:MN + R2], kst[0:n, t, MN + R2:QW]), lat[0:n, i, at:at + R2], lat[0:n, i, at + R2:AW],
                           [rt[0:n, k, :] for k in range(4)], cos, sin).then_inc(d_kpe, 1)
                    dve.wait_ge(a_vrs, t + 1)
                    V.tensor_scalar(gv[0:n, i, :], gv[0:n, i, :], vmv[0:n, 0:1], vrs[0:n, :], ALU.subtract, ALU.mult).then_inc(d_vs, 1)
                    dve.wait_ge(a_cqT, t + 1)
                    rotated_keys(t, n).then_inc(d_val, 1)
                    dve.wait_ge(a_q, t + 1)
                    lo, hi = qr[0:n, :, MN:MN + R2], qr[0:n, :, MN + R2:QW]
                    rotate((lo, hi), lo, hi, [qt[0:n, k, :, :] for k in range(4)], cos.unsqueeze(1).to_broadcast([n, MH, R2]),
                           sin.unsqueeze(1).to_broadcast([n, MH, R2])).then_inc(d_rope, 1)
                    dve.wait_ge(p_gate, t + 1)
                    for g in range(4):
                        gs = slice(g * P, (g + 1) * P)
                        ins = V.scalar_tensor_tensor(u[0:n, t, gs], bank[2][0:n, gs], bs[0:n, g:g + 1], u[0:n, t, gs], ALU.add, ALU.mult)
                    ins.then_inc(d_gated, 1)
                dve.wait_ge(p_small, NT + 1)
                V.tensor_copy(ckvT[:, SEQ:SEQ + PAST], bank[3][:, 256:384]).then_inc(d_val, 1)
                rotated_keys(NT, PAST).then_inc(d_val, 1)
                for i, (slot, rows) in enumerate([(t, P) for t in range(4)] + [(4, PAST), (5, DEC)]):
                    dve.wait_ge(p_val, i + 1)
                    V.tensor_copy(val[0:rows, slot, :], bank[4 + i % 4][0:rows, :]).then_inc(d_val, 1)

            @block.gpsimd
            def _(pool):
                G = nc.gpsimd
                G.memset(qT[QW:P, :, :], 0.0).then_inc(g_zero, 1)
                G.memset(kT[QW:P, :, :], 0.0).then_inc(g_zero, 1)
                pool.wait_ge(g_zero, 2)
                pool.wait_ge(small, 128)
                for t, n in enumerate(ROWS):
                    i = t % 2
                    pool.wait_ge(d_vs, t + 1)
                    pool.wait_ge(gch.sem, gch.inc(G.tensor_tensor(gv[0:n, i, :], gv[0:n, i, :], vg[0:n, :], ALU.mult)))
                    G.tensor_tensor(gv[0:n, i, :], gv[0:n, i, :], vb[0:n, :], ALU.add).then_inc(g_vn, 1)
                pool.wait_ge(g_vn, NT)

            @block.tensor
            def _(pe):
                T = nc.tensor
                def project(t, c):
                    n, i = ROWS[t], 3 * t + c
                    if t == 0:
                        pe.wait_ge(w_in[c], 16)
                    if t == 4 and c > 0:
                        return
                    if i >= 2:
                        pe.wait_ge(in_sb, i - 1)
                    if t == 4:
                        for k in range(KT):
                            for g in range(3):
                                mm = T.matmul(bank[0][DEC * g:DEC * (g + 1), 0:FW[g]], xT[:, k, t * P:t * P + n], w[g][:, k, :], start=(k == 0), stop=(k == KT - 1))
                        mm.then_inc(p_in, 3)
                        return
                    for k in range(KT):
                        mm = T.matmul(bank[i % 2][0:n, 0:FW[c]], xT[:, k, t * P:t * P + n], w[c][:, k, :], start=(k == 0), stop=(k == KT - 1))
                    mm.then_inc(p_in, 1)

                def small_transposes(slot, rows, latents):
                    if latents:
                        for k in range(2):
                            T.transpose(bank[3][:, k * P:k * P + rows], cqn[0:rows, slot % 2, k * P:(k + 1) * P], ident[0:rows, 0:rows])
                    T.transpose(bank[3][:, 256:256 + rows], ckvn[0:rows, slot, :], ident[0:rows, 0:rows])
                    T.transpose(bank[3][0:QW, 384:384 + rows], kst[0:rows, slot, :], ident[0:rows, 0:rows]).then_inc(p_small, 1)

                for c in range(3):
                    project(0, c)
                pe.wait_ge(ws_in, 32)
                for g in range(4):
                    mm = T.transpose(bank[7][:, g * P:(g + 1) * P], ws[:, g, :], ident)
                mm.then_inc(p_ws, 1)
                pe.wait_ge(small, 128)
                for t, n in enumerate(ROWS):
                    nxt = t + 1 < NT
                    if nxt:
                        project(t + 1, 0)
                    pe.wait_ge(d_n, t + 1)
                    pe.wait_ge(d_kpe, t + 1)
                    if t >= 1:
                        pe.wait_ge(d_val, t)
                    small_transposes(t, n, True)
                    if nxt:
                        project(t + 1, 1)
                    pe.wait_ge(a_cqT, t + 1)
                    if t >= 1:
                        pe.wait_ge(a_q, t)
                    for h in range(2):
                        for k in range(2):
                            mm = T.matmul(bank[4 + h][0:n, 0:4 * QW], cqT[:, k, 0:n], wuq[:, k, h * 4 * QW:(h + 1) * 4 * QW], start=(k == 0), stop=(k == 1))
                    mm.then_inc(p_uq, 1)
                    if nxt:
                        project(t + 1, 2)
                    pe.wait_ge(g_vn, t + 1)
                    pe.wait_ge(d_ws, 1)
                    if t >= 1:
                        pe.wait_ge(d_gated, t)
                    for g in range(4):
                        mm = T.matmul(bank[2][0:n, g * P:(g + 1) * P], wsT[0:n, g, 0:n], gv[0:n, t % 2, g * P:(g + 1) * P],
                                      start=(g == 0), stop=(g == 3), skip_group_check=True)
                    mm.then_inc(p_gate, 1)
                    pe.wait_ge(d_rope, t + 1)
                    if t >= 1:
                        pe.wait_ge(a_qT, t)
                    for h in range(MH):
                        mm = T.transpose(bank[6 + h // 4][0:QW, (h % 4) * P:(h % 4) * P + n], qr[0:n, h, :], ident[0:n, 0:n])
                    mm.then_inc(p_qT, 1)
                pe.wait_ge(cache_in, 32)
                pe.wait_ge(d_val, NT)
                small_transposes(NT, PAST, False)
                pe.wait_ge(d_val, NT + 1)
                pe.wait_ge(in_sb, 3 * NT)
                for i in range(8):
                    pair, part = i // 2, i % 2
                    keys = slice(0, SEQ) if part == 0 else slice(SEQ, KEYS)
                    if i >= 4:
                        pe.wait_ge(a_k, i - 3)
                    if i == 3:
                        pe.wait_ge(d_val, NT + 2)
                    if i == 2:
                        pe.wait_ge(d_gated, NT)
                    T.matmul(bank[i % 4][:, 0:keys.stop - keys.start], wuk[:, pair * P:(pair + 1) * P], ckvT[:, keys], start=True, stop=True).then_inc(p_k, 1)
                pe.wait_ge(a_qT, NT)
                for i, (at, rows) in enumerate([(0, P), (128, P), (256, P), (384, P), (SEQ, PAST), (SEQ + PAST, DEC)]):
                    if i >= 4:
                        pe.wait_ge(d_val, NT + 2 + i - 3)
                    T.matmul(bank[4 + i % 4][0:rows, :], ckvT[:, at:at + rows], wuv[:], start=True, stop=True).then_inc(p_val, 1)

        with Stage(nc, "m1a_") as ac:
            ab, sem = ac.sb, ac.sem
            wo = ab("wo", [P, KT, DM])
            pr = ab("pr", [P, 3, SEQ])
            pT = ab("pT", [P, 4, 4, P])
            mx = ab("mx", [P, 3])
            nb = ab("nb", [P, 3])
            den = ab("den", [P, 3])
            diag = ab("diag", [P, 3, P])
            free = S.shared[:, 2 * (W.W13 + W.W2):]
            catT, s = free[:, 0:KT * P].rearrange("p (k n) -> p k n", k=KT), free[:, KT * P:KT * P + DM]
            ln = Norm(nc, ab, sem, "mix")
            wo_in, ln_in = sem("wo_in"), sem("ln_in")
            p_s, d_nb, a_p, d_den, g_diag, p_pT, d_pT, p_o, a_o, p_c, a_c, p_y, d_y = (
                sem(x) for x in ("p_s", "d_nb", "a_p", "d_den", "g_diag", "p_pT", "d_pT", "p_o", "a_o", "p_c", "a_c", "p_y", "d_y"))
            dch = Chain(sem("d_chain"))
            items = [(t, h) for t in range(NT) for h in range(MH)]
            KB = [[(k, k * P, P) for k in range(t + 1)] for t in range(4)] + [[(4, SEQ, PAST), (5, SEQ + PAST, DEC)]]
            WIDTH = [sum(r for _, _, r in b) for b in KB]
            OUT_AT = 2
            LN_AT = OUT_AT + 2
            N_ITEMS = len(items)

            def tile_before(i, head):
                t, h = items[i]
                return t - 1 if t >= 1 and h == head else None

            block = ac.enter_context(nc.Block(no_gpsimd_drain=True))

            @block.sync
            def _(sp):
                sp.dma_start(ln.g[:], D["ln_mix_g"][1:2, :].to_broadcast([P, DM])).then_inc(ln_in, 16)
                sp.dma_start(ln.b[:], D["ln_mix_b"][1:2, :].to_broadcast([P, DM])).then_inc(ln_in, 16)
                sp.dma_start(wo[:], D["w_out_odd"][0].rearrange("(k p) n -> p k n", p=P)).then_inc(wo_in, 16)
                W.load_first(sp, range(2))
                for t, n in enumerate(ROWS):
                    sp.wait_ge(ln.done, t + 1)
                    sp.dma_start(S.x_rows.rearrange("(t h) c -> t (h c)", h=2)[t * P:t * P + n, :], x_tok[0:n, t, :]).then_inc(S.x_stored, 16)
    
            @block.tensor
            def _(pe):
                T = nc.tensor

                def scores(i):
                    t, h = items[i]
                    n, first = ROWS[t], KB[t][0][1]
                    if i >= 3:
                        pe.wait_ge(a_p, i - 2)
                    T.matmul(bank[i % 3][0:n, 0:WIDTH[t]], qT[:, h, t * P:t * P + n], kT[:, h, first:first + WIDTH[t]], start=True, stop=True).then_inc(p_s, 1)

                def turn(i):
                    t, h = items[i]
                    n = ROWS[t]
                    pe.wait_ge(g_diag, i + 1)
                    if i >= 2:
                        pe.wait_ge(d_pT, i - 1)
                    for b, (_, at, rows) in enumerate(KB[t]):
                        mm = T.matmul(bank[3 + i % 2][0:rows, b * P:b * P + n], pr[0:n, i % 3, b * P:b * P + rows], diag[0:n, i % 3, 0:n],
                                      start=(b == 0), stop=(b == len(KB[t]) - 1), skip_group_check=True)
                    mm.then_inc(p_pT, 1)

                def weigh(pair):
                    t, h = items[2 * pair]
                    n = ROWS[t]
                    pe.wait_ge(d_pT, 2 * pair + 2)
                    if h == 0 and t >= 1:
                        pe.wait_ge(a_o, t)
                    for b, (slot, _, rows) in enumerate(KB[t]):
                        for e in range(2):
                            mm = T.matmul(bank[5][MV * e:MV * (e + 1), h // 2 * P:h // 2 * P + n], val[0:rows, slot, (h + e) * MV:(h + e + 1) * MV],
                                          pT[0:rows, (2 * pair + e) % 4, b, 0:n], start=(h == 0 and b == 0), stop=(h == MH - 2 and b == len(KB[t]) - 1),
                                          skip_group_check=True)
                    mm.then_inc(p_o, 1)

                def gated(t):
                    n = ROWS[t]
                    if t >= 1:
                        pe.wait_ge(d_y, t)
                    else:
                        pe.wait_ge(wo_in, 16)
                    for k in range(4):
                        mm = T.transpose(bank[6][:, k * P:k * P + n], u[0:n, t, k * P:(k + 1) * P], ident[0:n, 0:n])
                    mm.then_inc(p_c, 1)
                    pe.wait_ge(a_c, t + 1)
                    out_products(T, bank[6], bank[7], t, catT, wo, range(4, 8))

                def heads(t):
                    pe.wait_ge(a_o, t + 1)
                    mm = out_products(T, bank[6], bank[7], t, catT, wo, range(0, 4))
                    mm.then_inc(p_y, 1)

                scores(0)
                scores(1)
                for i in range(N_ITEMS):
                    if i + 2 < N_ITEMS:
                        scores(i + 2)
                    if i >= 2 and i % 2 == 0:
                        weigh(i // 2 - 1)
                    turn(i)
                    if tile_before(i, OUT_AT) is not None:
                        gated(tile_before(i, OUT_AT))
                        heads(tile_before(i, OUT_AT))
                gated(NT - 1)
                weigh(N_ITEMS // 2 - 1)
                heads(NT - 1)

            @block.scalar
            def _(act):
                A = nc.scalar

                def heads(t):
                    act.wait_ge(p_o, MH // 2 * (t + 1))
                    if t >= 1:
                        act.wait_ge(p_y, t)
                    n = ROWS[t]
                    A.activation(catT[:, 0:4, 0:n], bank[5][:].rearrange("p (k n) -> p k n", k=4)[:, :, 0:n], ACT.Copy).then_inc(a_o, 1)

                def gated(t):
                    n = ROWS[t]
                    act.wait_ge(p_c, t + 1)
                    if t >= 1:
                        act.wait_ge(p_y, t)
                    A.activation(catT[:, 4:8, 0:n], bank[6][:].rearrange("p (k n) -> p k n", k=4)[:, :, 0:n], ACT.Copy).then_inc(a_c, 1)

                for i, (t, h) in enumerate(items):
                    n = ROWS[t]
                    act.wait_ge(d_nb, i + 1)
                    if i >= 3:
                        act.wait_ge(p_pT, i - 2)
                        act.wait_ge(d_den, i - 2)
                    A.activation(pr[0:n, i % 3, 0:WIDTH[t]], bank[i % 3][0:n, 0:WIDTH[t]], ACT.Exp, bias=nb[0:n, i % 3:i % 3 + 1], scale=SCALE,
                                 accum_out=den[0:n, i % 3:i % 3 + 1]).then_inc(a_p, 1)
                    if tile_before(i, 1) is not None:
                        heads(t - 1)
                    if tile_before(i, OUT_AT) is not None:
                        gated(t - 1)
                    if tile_before(i, LN_AT + 1) is not None:
                        ln.scalar(act, t - 1, ROWS[t - 1])
                gated(NT - 1)
                heads(NT - 1)
                ln.scalar(act, NT - 1, DEC)

            @block.vector
            def _(dve):
                V = nc.vector

                def link(ins):
                    dve.wait_ge(dch.sem, dch.inc(ins))

                def maximum(i):
                    t, h = items[i]
                    n, j = ROWS[t], i % 3
                    dve.wait_ge(p_s, i + 1)
                    if t < 4:
                        link(V.memset(bank[j][0:64, WIDTH[t] - 64:WIDTH[t]], -BIG))
                    if i >= 3:
                        dve.wait_ge(a_p, i - 2)
                    link(V.reduce_max(mx[0:n, j:j + 1], bank[j][0:n, 0:WIDTH[t]], AX.X))
                    V.tensor_scalar(nb[0:n, j:j + 1], mx[0:n, j:j + 1], -SCALE, None, ALU.mult).then_inc(d_nb, 1)

                def denominator(i):
                    n, j = ROWS[items[i][0]], i % 3
                    dve.wait_ge(a_p, i + 1)
                    V.reciprocal(den[0:n, j:j + 1], den[0:n, j:j + 1]).then_inc(d_den, 1)

                def turned(i):
                    t, h = items[i]
                    n = ROWS[t]
                    dve.wait_ge(p_pT, i + 1)
                    if i >= 4:
                        dve.wait_ge(p_o, i // 2 - 1)
                    if t < 4:
                        V.tensor_copy(pT[:, i % 4, 0:t + 1, 0:n], bank[3 + i % 2][:].rearrange("p (b n) -> p b n", b=4)[:, 0:t + 1, 0:n]).then_inc(d_pT, 1)
                    else:
                        V.tensor_copy(pT[:, i % 4, 0, 0:n], bank[3 + i % 2][:, 0:n])
                        V.tensor_copy(pT[0:DEC, i % 4, 1, 0:n], bank[3 + i % 2][0:DEC, P:P + n]).then_inc(d_pT, 1)

                def output(t):
                    n = ROWS[t]
                    dve.wait_ge(p_y, t + 1)
                    if t >= 1:
                        dve.wait_ge(ln.done, t)
                    link(residual(V, bank[6], bank[7], t, x_tok, s))
                    dve.sem_inc(d_y, 1)

                maximum(0)
                maximum(1)
                denominator(0)
                for i in range(N_ITEMS):
                    t, h = items[i]
                    if tile_before(i, OUT_AT + 1) is not None:
                        output(t - 1)
                    if i + 2 < N_ITEMS:
                        maximum(i + 2)
                    turned(i)
                    if i + 1 < N_ITEMS:
                        denominator(i + 1)
                    if tile_before(i, LN_AT) is not None:
                        ln.statistics(dve, t - 1, ROWS[t - 1], s)
                    if tile_before(i, LN_AT + 1) is not None:
                        if t == 1:
                            dve.wait_ge(ln_in, 32)
                        ln.centre(dve, t - 1, ROWS[t - 1], s)
                    if tile_before(i, LN_AT + 3) is not None:
                        ln.finish(dve, t - 1, ROWS[t - 1], s, x_tok[:, t - 1, :])
                output(NT - 1)
                ln.vector(dve, NT - 1, DEC, s, x_tok[:, NT - 1, :])

            @block.gpsimd
            def _(pool):
                for i, (t, h) in enumerate(items):
                    n, j = ROWS[t], i % 3
                    pool.wait_ge(d_den, i + 1)
                    if i >= 3:
                        pool.wait_ge(p_pT, i - 2)
                    nc.gpsimd.tensor_scalar(diag[0:n, j, 0:n], ident[0:n, 0:n], den[0:n, j:j + 1], None, ALU.mult).then_inc(g_diag, 1)
                pool.wait_ge(ln.done, NT)


def moe(nc, S, W):
    bank, x_tok, ident, gates = S.bank, S.x_tok, S.ident("ident"), S.gates
    layer, place, turn = W.layer, W.place, W.turn
    L = f"l{layer}_"
    with Stage(nc, L) as ctx:
        sb = ctx.sb
        W.more = sb("more", [P, len(EXTRA) * (W.W13 + W.W2)])
        meta = sb("meta", [1, 64], I32)
        gidx = sb("gidx", [P, MAXB + 2], I32)
        sidx = sb("sidx", [P, MAXB + 2], I32)

        with Stage(nc, L) as rc:
            rb, rs = rc.sb, rc.sem
            C = Constants(nc, rc, S, "route", L + "const")
            xT = S.shared[:, 2 * (W.W13 + W.W2):2 * (W.W13 + W.W2) + KT * TOK].rearrange("p (k n) -> p k n", k=KT)
            wr = rb("r_w", [P, KT, NG + NE])
            bias = rb("r_b", [P, NG + NE])
            lT = rb("r_lT", [NG + NE, TOK])
            lg = rb("r_lg", [P, NT, NG + NE])
            g8 = rb("r_g8", [P, NT, 8])
            gm = rb("r_gm", [P, NT, 8])
            gi = rb("r_gi", [P, NT, 8], U32)
            gsel = rb("r_gsel", [P, NT])
            pen = rb("r_pen", [P, NT, NG])
            em = rb("r_em", [P, NT, NE])
            ev = rb("r_ev", [P, NT, 8])
            ei = rb("r_ei", [P, NT, 8], U32)
            esel = rb("r_esel", [P, NT, 2])
            ge = rb("r_ge", [P, NT, NG])
            gp = rb("r_gp", [P, NT])
            dv = rb("r_dv", [P, NT])
            ed = rb("r_ed", [P, NT])
            rden = rb("r_rden", [P, NT])
            oh = rb("r_oh", [P, NT, 2, NE])
            A = rb("r_A", [P, NT, NE])
            pre = rb("r_pre", [P, NT + 1, NE])
            rank = rb("r_rank", [P, NT * NE], I32)
            fl = rb("r_fl", [P, NT * NE], I32)
            po = rb("r_po", [P, NT * NE], I32)
            blk = rb("r_blk", [P, NT, NE])
            pos = rb("r_pos", [P, NT, NE])
            prod = rb("r_prod", [P, NT, 2, NE])
            later = prod[:, :, 0, :]
            bsel = rb("r_bsel", [P, 2 * NT])
            psel = rb("r_psel", [P, 2 * NT])
            free = xT.rearrange("p k n -> p (k n)")
            widths = [2 * NT * P, 2 * NT * MAXB, 2 * NT * MAXB]
            ohp, ohb, val = (free[:, sum(widths[:i]):sum(widths[:i + 1])].rearrange("p (i n) -> p i n", i=2 * NT) for i in range(3))
            cnt = rb("r_cnt", [NE, 1])
            cmp9 = rb("r_cmp9", [NE, 9])
            nblk = rb("r_nblk", [NE, 1])
            nblkb = rb("r_nblkb", [NE, P])
            bend = rb("r_bend", [NE, 1])
            cmpb = rb("r_cmpb", [NE, OVER])
            base = rb("r_base", [P, NE])
            row = rb("r_row", [1, 64])
            tmp1 = rb("r_tmp1", [1, 64])
            nb1 = rb("r_nb1", [1, 1])
            vf = rb("r_vf", [P, MAXB])
            pad = rb("r_pad", [P, MAXB])
            vi = rb("r_vi", [P, MAXB], I32)
            gf = rb("r_gf", [P, MAXB])
            w_in, p_tr, a_xT = rs("w_in"), rs("p_tr"), rs("a_xT")
            p_log, d_lT, p_lg, d_ready, p_ready = rs("p_log"), rs("d_lT"), rs("p_lg"), rs("d_ready"), rs("p_ready")
            a_ready, dch = rs("a_ready"), Chain(rs("d_chain"))
            block = rc.enter_context(nc.Block(no_gpsimd_drain=True))

            @block.sync
            def _(sp):
                sp.dma_start(C.tile[:], C.source).then_inc(w_in, 16)
                sp.dma_start(wr[:, :, 0:NG], S.d["router_group_w"][layer].rearrange("(k p) n -> p k n", p=P)).then_inc(w_in, 16)
                sp.dma_start(wr[:, :, NG:], S.d["router_expert_w"][layer].rearrange("(k p) n -> p k n", p=P)).then_inc(w_in, 16)
                sp.dma_start(bias[:, 0:NG], S.d["router_group_b"][layer:layer + 1, :].to_broadcast([P, NG])).then_inc(w_in, 16)
                sp.dma_start(bias[:, NG:], S.d["router_expert_b"][layer:layer + 1, :].to_broadcast([P, NE])).then_inc(w_in, 16)
                W.load_first(sp, range(2, 2 + len(EXTRA)))

            @block.tensor
            def _(pe):
                for t, n in enumerate(ROWS):
                    for h in range(2):
                        i = 2 * t + h
                        if i >= 4:
                            pe.wait_ge(a_xT, i - 3)
                        for q in range(4):
                            k = 4 * h + q
                            mm = nc.tensor.transpose(bank[i % 4][:, q * P:q * P + n], x_tok[0:n, t, k * P:(k + 1) * P], ident[0:n, 0:n])
                        mm.then_inc(p_tr, 1)
                pe.wait_ge(a_xT, 2 * NT)
                pe.wait_ge(w_in, 80)
                for h in range(2):
                    for k in range(KT):
                        mm = nc.tensor.matmul(bank[4 + h][0:NG + NE, 0:TOK // 2], wr[:, k, :], xT[:, k, h * (TOK // 2):(h + 1) * (TOK // 2)],
                                              start=(k == 0), stop=(k == KT - 1))
                    mm.then_inc(p_log, 1)
                pe.wait_ge(d_lT, 2)
                for t, n in enumerate(ROWS):
                    mm = nc.tensor.transpose(bank[6][0:n, t * 36:(t + 1) * 36], lT[:, t * P:t * P + n], ident[0:36, 0:36])
                mm.then_inc(p_lg, 1)
                pe.wait_ge(d_ready, 1)
                nc.tensor.matmul(bank[0][:, 0:NT * NE], C("tri_strict"), A[:].rearrange("p t e -> p (t e)"), start=True, stop=False)
                mm = nc.tensor.matmul(bank[0][:, 0:NT * NE], C("ones"), pre[:, 0:NT, :].rearrange("p t e -> p (t e)"), start=False, stop=True)
                mm = nc.tensor.matmul(bank[1][0:NE, 0:1], pre[:, NT, :], C("ones")[:, 0:1], start=True, stop=True)
                mm.then_inc(p_ready, 1)
                pe.wait_ge(d_ready, 2)
                nc.tensor.matmul(bank[2][:, 0:NE], nblkb[:], C("tri_strict")[0:NE, 0:NE], start=True, stop=True)
                nc.tensor.matmul(bank[3][0:NE, 0:1], C("tri_incl")[0:NE, 0:NE], nblk[:], start=True, stop=True).then_inc(p_ready, 1)
                pe.wait_ge(d_ready, 3)
                nc.tensor.matmul(bank[4][0:1, 0:OVER], C("ones")[0:NE, 0:1], cmpb[:], start=True, stop=True).then_inc(p_ready, 1)
                pe.wait_ge(d_ready, 4)
                for i in range(2 * NT):
                    mm = nc.tensor.matmul(bank[5][:, 0:MAXB], ohp[:, i, :], val[:, i, :], start=(i == 0), stop=(i == 2 * NT - 1))
                mm.then_inc(p_ready, 1)

            @block.scalar
            def _(act):
                for i in range(2 * NT):
                    t, h = i // 2, i % 2
                    n = ROWS[t]
                    act.wait_ge(p_tr, i + 1)
                    nc.scalar.activation(xT[:, 4 * h:4 * h + 4, t * P:t * P + n],
                                         bank[i % 4][:].rearrange("p (k n) -> p k n", k=4)[:, :, 0:n], ACT.Copy).then_inc(a_xT, 1)
                act.wait_ge(a_ready, 1)
                nc.scalar.activation(ge[:], ge[:], ACT.Exp).then_inc(p_lg, 1)
                nc.scalar.activation(ed[:], dv[:], ACT.Exp).then_inc(p_lg, 1)

            @block.vector
            def _(dve):
                V = nc.vector

                def link(ins):
                    dve.wait_ge(dch.sem, dch.inc(ins))

                for h in range(2):
                    dve.wait_ge(p_log, h + 1)
                    V.tensor_copy(lT[:, h * (TOK // 2):(h + 1) * (TOK // 2)], bank[4 + h][0:36, 0:TOK // 2]).then_inc(d_lT, 1)
                link(V.memset(g8[:], -BIG))
                link(V.memset(lg[:], 0.0))
                dve.wait_ge(p_lg, 1)
                dve.wait_ge(w_in, 80)
                V.tensor_tensor(lg[:, 0:4, :], bank[6][:, 0:144].rearrange("p (t n) -> p t n", t=4),
                                bias[:].unsqueeze(1).to_broadcast([P, 4, 36]), ALU.add)
                link(V.tensor_tensor(lg[0:DEC, 4, :], bank[6][0:DEC, 144:180], bias[0:DEC, :], ALU.add))
                link(V.tensor_copy(g8[:, :, 0:NG], lg[:, :, 0:NG]))
                for t in range(NT):
                    ins = V.max(gm[:, t, :], g8[:, t, :])
                link(ins)
                for t in range(NT):
                    ins = V.max_index(gi[:, t, :], gm[:, t, :], g8[:, t, :])
                link(ins)
                link(V.tensor_copy(gsel[:], gi[:, :, 0]))
                link(V.tensor_tensor(pen[:], C("iota")[:, 0:NG].unsqueeze(1).to_broadcast([P, NT, NG]),
                                     gsel[:].unsqueeze(2).to_broadcast([P, NT, NG]), ALU.is_equal))
                link(V.tensor_scalar(pen[:], pen[:], BIG, -BIG, ALU.mult, ALU.add))
                for t in range(NT):
                    ins = V.tensor_tensor(em[:, t, :].rearrange("p (g e) -> p g e", g=NG), lg[:, t, NG:].rearrange("p (g e) -> p g e", g=NG),
                                          pen[:, t, :].unsqueeze(2).to_broadcast([P, NG, EPG]), ALU.add)
                link(ins)
                for t in range(NT):
                    ins = V.max(ev[:, t, :], em[:, t, :])
                link(ins)
                for t in range(NT):
                    ins = V.max_index(ei[:, t, :], ev[:, t, :], em[:, t, :])
                link(ins)
                V.tensor_tensor(ge[:], g8[:, :, 0:NG], gm[:, :, 0:1].to_broadcast([P, NT, NG]), ALU.subtract)
                link(V.tensor_tensor(dv[:], ev[:, :, 1], ev[:, :, 0], ALU.subtract))
                link(V.tensor_copy(esel[:], ei[:, :, 0:2]))
                dve.sem_inc(a_ready, 1)
                for k in range(2):
                    ins = V.tensor_tensor(oh[:, :, k, :], C("iota")[:, 0:NE].unsqueeze(1).to_broadcast([P, NT, NE]),
                                          esel[:, :, k:k + 1].to_broadcast([P, NT, NE]), ALU.is_equal)
                link(ins)
                for k in range(2):
                    ins = V.tensor_tensor(oh[:, :, k, :], oh[:, :, k, :], C("valid").unsqueeze(2).to_broadcast([P, NT, NE]), ALU.mult)
                link(ins)
                link(V.tensor_tensor(A[:], oh[:, :, 0, :], oh[:, :, 1, :], ALU.add))
                link(V.memset(pre[:, 0, :], 0.0))
                for t in range(NT):
                    link(V.tensor_tensor(pre[:, t + 1, :], pre[:, t, :], A[:, t, :], ALU.add))
                dve.sem_inc(d_ready, 1)
                dve.wait_ge(p_lg, 3)
                V.tensor_scalar(rden[:], ed[:], 1.0, None, ALU.add)
                link(V.reduce_sum(gp[:], ge[:], AX.X))
                link(V.tensor_tensor(rden[:], rden[:], gp[:], ALU.mult))
                link(V.reciprocal(gates[:, :, 0], rden[:]))
                link(V.tensor_tensor(gates[:, :, 1], gates[:, :, 0], ed[:], ALU.mult))
                dve.wait_ge(p_ready, 1)
                link(V.tensor_copy(cnt[:], bank[1][0:NE, 0:1]))
                link(V.tensor_scalar(cmp9[:], C("fills")[0:NE, :], cnt[:], None, ALU.is_lt))
                link(V.reduce_sum(nblk[:], cmp9[:, 1:9], AX.X))
                V.tensor_copy(nblkb[:], nblk[:].to_broadcast([NE, P])).then_inc(d_ready, 1)
                link(V.tensor_copy(rank[:], bank[0][:, 0:NT * NE]))
                V.tensor_scalar(fl[:], rank[:], 6, None, ALU.arith_shift_right)
                link(V.tensor_scalar(po[:], rank[:], SLOTS - 1, None, ALU.bitwise_and))
                dve.wait_ge(p_ready, 2)
                link(V.tensor_copy(bend[:], bank[3][0:NE, 0:1]))
                V.tensor_scalar(cmpb[:], C("iota")[0:NE, 0:OVER], bend[:], None, ALU.is_ge).then_inc(d_ready, 1)
                V.tensor_copy(pos[:].rearrange("p t e -> p (t e)"), po[:])
                link(V.tensor_copy(blk[:].rearrange("p t e -> p (t e)"), fl[:]))
                link(V.scalar_tensor_tensor(base[:], C("iota")[:, 0:NE], -1.0, bank[2][:, 0:NE], ALU.mult, ALU.add))
                link(V.scalar_tensor_tensor(later, blk[:], float(NE - 1), base[:].unsqueeze(1).to_broadcast([P, NT, NE]), ALU.add, ALU.add))
                link(V.scalar_tensor_tensor(blk[:], blk[:], 1.0, later, ALU.is_ge, ALU.mult))
                link(V.tensor_tensor(blk[:], blk[:], C("iota")[:, 0:NE].unsqueeze(1).to_broadcast([P, NT, NE]), ALU.add))
                for src, dst in ((blk, bsel), (pos, psel)):
                    for k in range(2):
                        ins = V.tensor_tensor(prod[:, :, k, :], oh[:, :, k, :], src[:], ALU.mult)
                    link(ins)
                    link(V.reduce_sum(dst[:].rearrange("p (t k) -> p t k", k=2), prod[:], AX.X))
                V.tensor_tensor(ohp, C("iota_slot").unsqueeze(1).to_broadcast([P, 2 * NT, P]),
                                psel[:].unsqueeze(2).to_broadcast([P, 2 * NT, P]), ALU.is_equal)
                link(V.tensor_tensor(ohb, C("iota")[:, 0:MAXB].unsqueeze(1).to_broadcast([P, 2 * NT, MAXB]),
                                     bsel[:].unsqueeze(2).to_broadcast([P, 2 * NT, MAXB]), ALU.is_equal))
                V.tensor_tensor(val, ohb, C("assignment").unsqueeze(2).to_broadcast([P, 2 * NT, MAXB]), ALU.mult).then_inc(d_ready, 1)
                dve.wait_ge(p_ready, 3)
                link(V.tensor_copy(row[:, 0:OVER], bank[4][0:1, 0:OVER]))
                link(V.tensor_scalar(tmp1[:, 0:OVER], row[:, 0:OVER], float(NE), None, ALU.is_lt))
                link(V.reduce_sum(nb1[:], tmp1[:, 0:OVER], AX.X))
                link(V.tensor_scalar(tmp1[:, 0:OVER // 2], C("pairs")[0:1, :], nb1[:], None, ALU.is_lt))
                link(V.reduce_sum(nb1[:], tmp1[:, 0:OVER // 2], AX.X))
                V.tensor_scalar(meta[:, MAXB:MAXB + 1], nb1[:], 2.0, float(NE - 4), ALU.mult, ALU.add)
                V.tensor_copy(meta[:, 0:NE], C("iota")[0:1, 0:NE])
                link(V.tensor_scalar(meta[:, NE:MAXB], row[:, 0:OVER], float(NE - 1), None, ALU.min))
                dve.wait_ge(p_ready, 4)
                V.tensor_scalar(vf[:], bank[5][:, 0:MAXB], -1.0, None, ALU.add)
                link(V.tensor_scalar(pad[:], bank[5][:, 0:MAXB], 0.5, 131072.0, ALU.is_lt, ALU.mult))
                link(V.tensor_tensor(vf[:], vf[:], pad[:], ALU.add))
                link(V.tensor_copy(vi[:], vf[:]))
                link(V.tensor_scalar(vi[:], vi[:], -2, None, ALU.bitwise_and))
                link(V.tensor_copy(gf[:], vi[:]))
                V.tensor_scalar(gidx[:, 0:MAXB], gf[:], C("half"), None, ALU.add)
                link(V.tensor_scalar(vf[:], vf[:], 2.0, None, ALU.mult))
                link(V.tensor_scalar(sidx[:, 0:MAXB], vf[:], C("half"), None, ALU.add))

        with Stage(nc, L) as ec:
            eb, es = ec.sb, ec.sem
            xg = eb("e_xg", [P, 2, HALF])
            xTs = eb("e_xT", [P, 2, 4, P])
            up = eb("e_up", [SLOTS, 2, 512])
            hsum = eb("e_hsum", [SLOTS, 2, 512])
            sil = eb("e_sil", [SLOTS, 2, DE])
            hid = eb("e_hid", [SLOTS, 2, DE])
            hidT = eb("e_hidT", [P, 2, 2, SLOTS])
            ysb = eb("e_y", [P, 2, HALF])
            gcur = eb("e_gcur", [P, 2], I32)
            scur = eb("e_scur", [P, 2], I32)
            xg_in = [es(f"xg_in{j}") for j in range(2)]
            y_out = [es(f"y_out{j}") for j in range(2)]
            xT_ps, xT_sb, h_ps, h_up, h_sum = es("xT_ps"), es("xT_sb"), es("h_ps"), es("h_up"), es("h_sum")
            h_sil, hid_sb, hT_ps, hT_sb, y_ps, y_sb = es("h_sil"), es("hid_sb"), es("hT_ps"), es("hT_sb"), es("y_ps"), es("y_sb")
            xg_zero, going, g_cp, s_cp = es("xg_zero"), es("going"), es("g_cp"), es("s_cp")
            block = ec.enter_context(nc.Block(no_gpsimd_drain=True))

            @block.sync
            def _(sp):
                last = {j: j for j in range(2)}
                for m in range(PEELED):
                    if turn[m] > 1:
                        j = place[m]
                        sp.wait_ge(h_ps, last[j] + 1)
                        W.load13(sp, m, j)
                        sp.wait_ge(y_ps, last[j] + 1)
                        W.load2(sp, m, j)
                    if m not in EXTRA:
                        last[place[m]] = m

                def next_load(b, j, done):
                    sp.wait_ge(h_ps, done)
                    e = sp.value_load(meta[0:1, bass.ds(b + j, 1)], min_val=0, max_val=NE - 1)
                    W.load13(sp, e, j)
                    sp.wait_ge(y_ps, done)
                    W.load2(sp, e, j)

                for j in range(2):
                    next_load(PEELED, j, last[j] + 1)
                tail = sp.value_load(meta[0:1, MAXB:MAXB + 1], min_val=NE - 4, max_val=MAXB - 4)
                with sp.Fori(PEELED + 2, tail + 4, 2) as b:
                    for j in range(2):
                        next_load(b, j, b + j - 1)

            @block.gpsimd
            def _(pool):
                tail = pool.value_load(meta[0:1, MAXB:MAXB + 1], min_val=NE - 4, max_val=MAXB - 4)
                pool.wait_ge(S.x_stored, 16 * NT * (layer + 1))
                nc.gpsimd.memset(xg[:], 0.0).then_inc(xg_zero, 1)
                pool.wait_ge(xg_zero, 1)
                nc.gpsimd.memset(gcur[:], 0).then_inc(xT_ps, 2)

                gather_bound, scatter_bound = pool.to_reg(2 * TOK - 1), pool.to_reg(4 * TOK - 1)

                def gather(b, j):
                    m = b + j
                    pool.wait_ge(xT_ps, m + 1)
                    nc.gpsimd.tensor_copy(gcur[:, j:j + 1], gidx[:, bass.ds(m, 1)]).then_inc(g_cp, 1)
                    pool.wait_ge(g_cp, m + 1)
                    pool.sem_inc(going, 1)
                    nc.gpsimd.indirect_dma_start(
                        out=xg[:, j, :], out_offset=None, in_=S.x_rows,
                        in_offset=bass.IndirectOffsetOnAxis(ap=gcur[:, j:j + 1].bitcast(U32), axis=0),
                        bounds_check=gather_bound, oob_is_err=False).then_inc(xg_in[j], 16)

                def scatter(b, j, first=False):
                    m = b + j
                    if not first:
                        pool.wait_ge(y_out[j], b * 8)
                    nc.gpsimd.tensor_copy(scur[:, j:j + 1], sidx[:, bass.ds(m, 1)]).then_inc(s_cp, 1)
                    pool.wait_ge(s_cp, m + 1)
                    pool.wait_ge(y_sb, m + 3)
                    pool.sem_inc(going, 1)
                    nc.gpsimd.indirect_dma_start(
                        out=S.y_rows, out_offset=bass.IndirectOffsetOnAxis(ap=scur[:, j:j + 1].bitcast(U32), axis=0),
                        in_=ysb[:, j, :], in_offset=None,
                        bounds_check=scatter_bound, oob_is_err=False).then_inc(y_out[j], 16)

                gather(0, 0)
                gather(0, 1)
                gather(2, 0)
                gather(2, 1)
                scatter(0, 0, first=True)
                gather(4, 0)
                scatter(0, 1, first=True)
                with pool.Fori(2, tail, 2) as b:
                    gather(b + 2, 1)
                    scatter(b, 0)
                    gather(b + 4, 0)
                    scatter(b, 1)
                gather(tail + 2, 1)
                scatter(tail, 0)
                scatter(tail, 1)
                for j in range(2):
                    scatter(tail + 2, j)
                for j in range(2):
                    pool.wait_ge(y_out[j], tail * 8 + 32)

            @block.tensor
            def _(pe):
                tail = pe.value_load(meta[0:1, MAXB:MAXB + 1], min_val=NE - 4, max_val=MAXB - 4)

                def x_transposes(b, j):
                    pe.wait_ge(xg_in[j], b * 8 + 16)
                    for q in range(4):
                        mm = nc.tensor.transpose(bank[j][:, q * P:(q + 1) * P], xg[:, j, q:HALF:4], ident)
                    mm.then_inc(xT_ps, 1)

                def up_products(b, j):
                    m = b + j
                    at, loads = (place[m], 32 * turn[m]) if isinstance(b, int) and b < PEELED else (j, b * 16 + 32 - 32 * W.short)
                    pe.wait_ge(W.in13[at], loads)
                    pe.wait_ge(xT_sb, m + 1)
                    pe.wait_ge(h_sum, m + 1)
                    for q in range(4):
                        for h in range(2):
                            mm = nc.tensor.matmul(bank[2 + j][SLOTS * h:SLOTS * (h + 1), :], xTs[:, j, q, SLOTS * h:SLOTS * (h + 1)],
                                                  W.w13(at)[:, :, h, q, :], start=(q == 0), stop=(q == 3))
                    mm.then_inc(h_ps, 1)

                def hid_ready(b, j):
                    pe.wait_ge(hid_sb, b + j + 1)

                def hid_transposes(j):
                    for f in range(2):
                        mm = nc.tensor.transpose(bank[4 + j][:, f * SLOTS:(f + 1) * SLOTS], hid[:, j, f:DE:2], ident[0:SLOTS, 0:SLOTS])
                    mm.then_inc(hT_ps, 1)

                def down_products(b, j):
                    at, loads = (place[b + j], 16 * turn[b + j]) if isinstance(b, int) and b < PEELED else (j, b * 8 + 16 - 16 * W.short)
                    pe.wait_ge(W.in2[at], loads)
                    pe.wait_ge(hT_sb, b + j + 1)
                    pe.wait_ge(y_sb, b + j + 1)
                    for f in range(2):
                        for h in range(2):
                            mm = nc.tensor.matmul(bank[6 + j][SLOTS * h:SLOTS * (h + 1), :], hidT[:, j, f, :],
                                                  W.w2(at)[:, f, h * HALF:(h + 1) * HALF], start=(f == 0), stop=(f == 1))
                    mm.then_inc(y_ps, 1)

                x_transposes(0, 0)
                x_transposes(0, 1)
                up_products(0, 0)
                def pair(b):
                    up_products(b, 1)
                    hid_ready(b, 0)
                    x_transposes(b + 2, 0)
                    hid_transposes(0)
                    down_products(b, 0)
                    up_products(b + 2, 0)
                    hid_ready(b, 1)
                    x_transposes(b + 2, 1)
                    hid_transposes(1)
                    down_products(b, 1)

                for b in range(0, PEELED, 2):
                    pair(b)
                with pe.Fori(PEELED, tail + 2, 2) as b:
                    pair(b)
                hid_ready(tail + 2, 0)
                up_products(tail + 2, 1)
                hid_transposes(0)
                hid_ready(tail + 2, 1)
                down_products(tail + 2, 0)
                hid_transposes(1)
                down_products(tail + 2, 1)

            @block.scalar
            def _(act):
                tail = act.value_load(meta[0:1, MAXB:MAXB + 1], min_val=NE - 4, max_val=MAXB - 4)

                def x_copy(b, j):
                    act.wait_ge(xT_ps, b + j + 3)
                    nc.scalar.activation(xTs[:, j, :, :].rearrange("p k n -> p (k n)"), bank[j][:], ACT.Copy).then_inc(xT_sb, 1)

                def hidden(b, j):
                    m = b + j
                    act.wait_ge(h_ps, m + 1)
                    nc.scalar.activation(up[:, j, :], bank[2 + j][SLOTS:P, :], ACT.Copy).then_inc(h_up, 1)
                    act.wait_ge(h_sum, m + 3)
                    nc.scalar.activation(sil[:, j, :], hsum[:, j, 0:DE], ACT.Silu).then_inc(h_sil, 1)

                x_copy(0, 0)
                x_copy(0, 1)
                hidden(0, 0)
                with act.Fori(0, tail + 2, 2) as b:
                    hidden(b, 1)
                    x_copy(b + 2, 0)
                    hidden(b + 2, 0)
                    x_copy(b + 2, 1)
                hidden(tail + 2, 1)

            @block.vector
            def _(dve):
                tail = dve.value_load(meta[0:1, MAXB:MAXB + 1], min_val=NE - 4, max_val=MAXB - 4)
                nc.vector.memset(hsum[:, 0, 0:1], 0.0).then_inc(h_sum, 2)
                nc.vector.memset(ysb[:, 0, 0:1], 0.0).then_inc(y_sb, 2)
                dve.wait_ge(h_sum, 2)
                dve.wait_ge(y_sb, 2)

                def hidden(b, j):
                    m = b + j
                    dve.wait_ge(h_up, m + 1)
                    nc.vector.tensor_tensor(hsum[:, j, :], bank[2 + j][0:SLOTS, :], up[:, j, :], ALU.add).then_inc(h_sum, 1)
                    dve.wait_ge(h_sil, m + 1)
                    nc.vector.tensor_tensor(hid[:, j, :], sil[:, j, :], hsum[:, j, DE:2 * DE], ALU.mult).then_inc(hid_sb, 1)

                def hid_copy(b, j):
                    dve.wait_ge(hT_ps, b + j + 1)
                    nc.vector.tensor_copy(hidT[:, j, :, :].rearrange("p f n -> p (f n)"), bank[4 + j][:, 0:P]).then_inc(hT_sb, 1)

                def y_copy(b, j, first=False):
                    dve.wait_ge(y_ps, b + j + 1)
                    if not first:
                        dve.wait_ge(y_out[j], b * 8)
                    nc.vector.tensor_copy(ysb[:, j, :], bank[6 + j][:]).then_inc(y_sb, 1)

                def pair(b, first=False):
                    hid_copy(b, 0)
                    hidden(b, 1)
                    y_copy(b, 0, first)
                    hid_copy(b, 1)
                    hidden(b + 2, 0)
                    y_copy(b, 1, first)

                hidden(0, 0)
                pair(0, first=True)
                with dve.Fori(2, tail + 2, 2) as b:
                    pair(b)
                hid_copy(tail + 2, 0)
                hidden(tail + 2, 1)
                y_copy(tail + 2, 0)
                hid_copy(tail + 2, 1)
                y_copy(tail + 2, 1)


def combine(nc, S, layer, turned=None):
    bank, x_tok, ident, gates = S.bank, S.x_tok, S.ident("ident"), S.gates
    with Stage(nc, f"c{layer}_") as cc:
        cb, cs = cc.sb, cc.sem
        yin = cb("y", [P, 3, 2, DM])
        s = cb("s", [P, NT, DM])
        ln = Norm(nc, cb, cs, "ffn", ring=NT, by_act=True)
        y_in = [cs(f"y_in{j}") for j in range(3)]
        ln_w, summed, first, p_xT, a_xT = cs("ln_w"), cs("summed"), cs("first"), cs("p_xT"), cs("a_xT")
        block = cc.enter_context(nc.Block(no_gpsimd_drain=True))

        @block.sync
        def _(sp):
            for t, n in enumerate(ROWS):
                if t >= 3:
                    sp.wait_ge(summed, t - 2)
                sp.dma_start(yin[0:n, t % 3, :, :], S.y_pairs[t * P:t * P + n, :, :]).then_inc(y_in[t % 3], 16)
                if t == 0:
                    sp.dma_start(ln.g[:], S.d["ln_ffn_g"][layer:layer + 1, :].to_broadcast([P, DM])).then_inc(ln_w, 16)
                    sp.dma_start(ln.b[:], S.d["ln_ffn_b"][layer:layer + 1, :].to_broadcast([P, DM])).then_inc(ln_w, 16)
            if turned:
                turned[1](sp)
            if layer == DEPTH - 1:
                for t, n in enumerate(ROWS):
                    sp.wait_ge(ln.done, t + 1)
                    dst = S.o["y_prompt"][0, t * P:t * P + n, :] if t < 4 else S.o["y_sample"][0, :, :]
                    sp.dma_start(dst, x_tok[0:n, t, :]).then_inc(S.out_done, 16)

        @block.scalar
        def _(act):
            A = nc.scalar

            def turn(t):
                n = ROWS[t]
                for h in range(2):
                    act.wait_ge(p_xT, 2 * t + h + 1)
                    A.activation(turned[0][:, 4 * h:4 * h + 4, t * P:t * P + n],
                                 bank[(2 * t + h) % 4][:].rearrange("p (k n) -> p k n", k=4)[:, :, 0:n], ACT.Copy).then_inc(a_xT, 1)

            for t, n in enumerate(ROWS):
                A.activation(s[0:n, t, :], x_tok[0:n, t, :], ACT.Copy, scale=ALPHA).then_inc(first, 1)
            for t, n in enumerate(ROWS):
                ln.scalar(act, t, n, s[:, t, :])
                if turned and t >= 1:
                    turn(t - 1)
            if turned:
                turn(NT - 1)

        @block.vector
        def _(dve):
            V = nc.vector
            for t, n in enumerate(ROWS):
                src = s[0:n, t, :]
                dve.wait_ge(y_in[t % 3], 16 * (t // 3 + 1))
                dve.wait_ge(first, t + 1)
                for k in range(2):
                    ln.link(dve, V.scalar_tensor_tensor(src, yin[0:n, t % 3, k, :], gates[0:n, t, k:k + 1], src, ALU.mult, ALU.add))
                dve.sem_inc(summed, 1)
                if t == 0:
                    dve.wait_ge(ln_w, 32)
                ln.vector(dve, t, n, s[:, t, :], x_tok[:, t, :])

        @block.gpsimd
        def _(pool):
            pool.wait_ge(ln_w, 32)
            for t, n in enumerate(ROWS):
                ln.pool(pool, t, n, s[:, t, :], x_tok[:, t, :])
            pool.wait_ge(ln.done, NT)

        @block.tensor
        def _(pe):
            if turned:
                for t, n in enumerate(ROWS):
                    pe.wait_ge(ln.done, t + 1)
                    for h in range(2):
                        i = 2 * t + h
                        if i >= 4:
                            pe.wait_ge(a_xT, i - 3)
                        for q in range(4):
                            k = 4 * h + q
                            mm = nc.tensor.transpose(bank[i % 4][:, q * P:q * P + n], x_tok[0:n, t, k * P:(k + 1) * P], ident[0:n, 0:n])
                        mm.then_inc(p_xT, 1)


def stream_step(nc, d, o, places):
    with ExitStack() as ctx:
        S = State()
        S.d, S.o, S.places = d, o, places
        S.x_tok = ctx.enter_context(nc.sbuf_tensor("x_tok", [P, NT, DM], F32))
        S.ident = Constants(nc, ctx, S, "all", "ident")
        S.bank = [ctx.enter_context(nc.psum_tensor(f"bank{i}", [P, 512], F32)) for i in range(8)]
        S.shared = ctx.enter_context(nc.sbuf_tensor("shared", [P, max(4 * KT * 512, 2 * (Weights.W13 + Weights.W2) + KT * TOK)], F32))
        S.gates = ctx.enter_context(nc.sbuf_tensor("gates", [P, NT, 2], F32))
        S.out_done = ctx.enter_context(nc.semaphore("out_done"))
        S.x_stored = ctx.enter_context(nc.semaphore("x_stored"))
        S.out_pool = ctx.enter_context(nc.semaphore("out_pool"))
        S.x_rows = nc.dram_tensor("x_rows", [2 * TOK, HALF], F32, kind="Internal").ap()
        S.y_rows = nc.dram_tensor("y_rows", [4 * TOK, HALF], F32, kind="Internal").ap()
        S.y_pairs = S.y_rows.rearrange("(t k h) c -> t k (h c)", k=2, h=2)
        S.OUT_ODD = 16 * (4 + 2 * NT + 1)
        with Weights(nc, S, 0) as W:
            even_mixer(nc, S, W)
            moe(nc, S, W)
        with Weights(nc, S, 1) as W:
            odd_mixer(nc, S, W)
            moe(nc, S, W)
            combine(nc, S, 1)
        with nc.Block(no_gpsimd_drain=True) as block:
            @block.sync
            def _(sp):
                sp.wait_ge(S.out_done, S.OUT_ODD + 16 * NT)
                sp.wait_ge(S.out_pool, 32)


class State:
    pass


_OUTS = [("y_prompt", (1, SEQ, DM)), ("y_sample", (1, DEC, DM)),
         ("gla_state_prompt", (1, 1, GH, GK, GV)), ("gla_state_sample", (1, 1, GH, GK, GV)),
         ("pool_state_prompt", (1, 1, 15, 512)), ("pool_state_sample", (1, 1, 15, 512)),
         ("mla_ckv_prompt", (1, 1, SEQ, P)), ("mla_ckv_sample", (1, 1, DEC, P)),
         ("mla_kpe_prompt", (1, 1, SEQ, MR)), ("mla_kpe_sample", (1, 1, DEC, MR)),
         ("gmlp_v_sample", (1, 1, DEC, MW))]


def kernel(**inputs):
    import numpy as _np
    import concourse.bacc as _bacc
    from concourse import mybir as _mybir
    from concourse.bass_utils import run_bass_kernel_spmd as _run

    table, places = constant_table()
    laid = {name: _np.ascontiguousarray(a) for name, a in inputs.items()}
    laid["pool_scale"] = _np.ascontiguousarray(_np.asarray(inputs["pool_scale"]).reshape(4, P).T)
    laid["gmlp_bs"] = _np.ascontiguousarray(_np.asarray(inputs["gmlp_bs"])[0].T)
    laid["constants"] = table

    nc = _bacc.Bacc("TRN2", target_bir_lowering=False, num_devices=1)
    arrays, d, o = {}, {}, {}
    for name, a in laid.items():
        arrays[f"in_{name}"] = a
        d[name] = nc.dram_tensor(f"in_{name}", a.shape, _mybir.dt.from_np(a.dtype), kind="ExternalInput").ap()
    for name, shape in _OUTS:
        o[name] = nc.dram_tensor(f"out_{name}", shape, F32, kind="ExternalOutput").ap()
    stream_step(nc, d, o, places)
    r = _run(nc, [arrays], core_ids=[0])
    return tuple(r.results[0][f"out_{name}"] for name, _ in _OUTS)
```
